# Optimizing a Trainium2 kernel written in Bass

```python
import jax, jax.numpy as jnp
from jax import lax
import numpy as np
import math

D_MODEL = 2048
BATCH = 1
SEQ = 256
DEPTH = 1

MIX_WIDTH = D_MODEL
POOL_WIDTH = MIX_WIDTH // 2
POOL_WINDOWS = (2, 4, 8, 16)
POOL_GROUP = POOL_WIDTH // len(POOL_WINDOWS)
ATTN_WIDTH = MIX_WIDTH - POOL_WIDTH
HEAD_DIM = 128
N_HEADS = ATTN_WIDTH // HEAD_DIM
DILATED_PATTERNS = ((128, 1), (512, 4), (2048, 16))
MAX_WINDOW = max(w for w, _ in DILATED_PATTERNS)
Q_BLOCK = 128
IN_WIDTH = POOL_WIDTH + 3 * ATTN_WIDTH
D_FF = 4 * D_MODEL
NORM_EPS = 1e-6


def rmsnorm(x, g):
    xf = x.astype(jnp.float32)
    y = xf * lax.rsqrt(jnp.mean(xf * xf, axis=-1, keepdims=True) + NORM_EPS)
    return (y * g.astype(jnp.float32)).astype(x.dtype)

def alibi_slopes():
    return 2.0 ** (-8.0 * jnp.arange(1, N_HEADS + 1, dtype=jnp.float32) / N_HEADS)

def pool_mixer(u, pool_w, pool_scale):
    B, S, _ = u.shape
    uf = u.astype(jnp.float32)
    cs = jnp.cumsum(uf, axis=1)
    pos = jnp.arange(1, S + 1, dtype=jnp.float32)[None, :, None]
    diffs = []
    for g, w in enumerate(POOL_WINDOWS):
        c = cs[..., g * POOL_GROUP:(g + 1) * POOL_GROUP]
        trailing = c - jnp.pad(c, ((0, 0), (w, 0), (0, 0)))[:, :S]
        mean = trailing / jnp.minimum(pos, float(w))
        diffs.append(mean - uf[..., g * POOL_GROUP:(g + 1) * POOL_GROUP])
    d = jnp.stack(diffs, axis=2).astype(u.dtype)
    y = jnp.einsum('bsgc,gcf->bsgf', d, pool_w).reshape(B, S, POOL_WIDTH)
    return y * pool_scale

def dilated_attention(q, k, v, slopes):
    B, S, H, Dh = q.shape
    scale = Dh ** -0.5
    kp = jnp.pad(k, ((0, 0), (MAX_WINDOW, 0), (0, 0), (0, 0)))
    vp = jnp.pad(v, ((0, 0), (MAX_WINDOW, 0), (0, 0), (0, 0)))
    qi = jnp.arange(Q_BLOCK)

    def block(b0):
        qb = lax.dynamic_slice_in_dim(q, b0, Q_BLOCK, axis=1).astype(jnp.float32) * scale
        kwin = lax.dynamic_slice_in_dim(kp, b0, Q_BLOCK + MAX_WINDOW, axis=1)
        vwin = lax.dynamic_slice_in_dim(vp, b0, Q_BLOCK + MAX_WINDOW, axis=1)
        ms, dens, nums = [], [], []
        for window, dil in DILATED_PATTERNS:
            dist = jnp.arange(window // dil + 1) * dil
            idx = qi[:, None] + MAX_WINDOW - dist[None, :]
            valid = (b0 + qi)[:, None] >= dist[None, :]
            kg = jnp.take(kwin, idx, axis=1).astype(jnp.float32)
            vg = jnp.take(vwin, idx, axis=1).astype(jnp.float32)
            s = jnp.einsum('bqhd,bqjhd->bqhj', qb, kg)
            s = s - slopes[:, None] * dist.astype(jnp.float32)[None, :]
            s = jnp.where(valid[None, :, None, :], s, -jnp.inf)
            m = jnp.max(s, axis=-1)
            p = jnp.exp(s - m[..., None])
            ms.append(m)
            dens.append(jnp.sum(p, axis=-1))
            nums.append(jnp.einsum('bqhj,bqjhd->bqhd', p, vg))
        m_all = jnp.stack(ms)
        w = jnp.exp(m_all - jnp.max(m_all, axis=0))
        den = jnp.sum(w * jnp.stack(dens), axis=0)
        num = jnp.sum(w[..., None] * jnp.stack(nums), axis=0)
        return num / den[..., None]

    starts = jnp.arange(S // Q_BLOCK) * Q_BLOCK
    out = lax.map(block, starts)
    return out.transpose(1, 0, 2, 3, 4).reshape(B, S, H * Dh).astype(q.dtype)

def first_inputs(seed: int = 0) -> dict:
    key = jax.random.key(seed)
    ks = jax.random.split(key, 12)
    f32 = jnp.float32
    x = jax.random.normal(ks[0], (BATCH, SEQ, D_MODEL), f32)
    norm_mix_g = 1.0 + 0.05 * jax.random.normal(ks[1], (DEPTH, D_MODEL), f32)
    w_in = jax.random.normal(ks[2], (DEPTH, D_MODEL, IN_WIDTH), f32) * D_MODEL ** -0.5
    pool_w = jax.random.normal(ks[3], (DEPTH, len(POOL_WINDOWS), POOL_GROUP, POOL_GROUP), f32) * POOL_GROUP ** -0.5
    pool_scale = 1.0 + 0.1 * jax.random.normal(ks[4], (DEPTH, POOL_WIDTH), f32)
    pool_out_norm_g = 1.0 + 0.05 * jax.random.normal(ks[5], (DEPTH, POOL_WIDTH), f32)
    attn_out_norm_g = 1.0 + 0.05 * jax.random.normal(ks[6], (DEPTH, ATTN_WIDTH), f32)
    w_out = jax.random.normal(ks[7], (DEPTH, MIX_WIDTH, D_MODEL), f32) * MIX_WIDTH ** -0.5
    norm_mlp_g = 1.0 + 0.05 * jax.random.normal(ks[8], (DEPTH, D_MODEL), f32)
    w_up = jax.random.normal(ks[9], (DEPTH, D_MODEL, D_FF), f32) * D_MODEL ** -0.5
    w_down = jax.random.normal(ks[10], (DEPTH, D_FF, D_MODEL), f32) * D_FF ** -0.5
    norm_final_g = 1.0 + 0.05 * jax.random.normal(ks[11], (D_MODEL,), f32)
    return {"x": x, "norm_mix_g": norm_mix_g, "w_in": w_in, "pool_w": pool_w,
            "pool_scale": pool_scale, "pool_out_norm_g": pool_out_norm_g,
            "attn_out_norm_g": attn_out_norm_g, "w_out": w_out, "norm_mlp_g": norm_mlp_g,
            "w_up": w_up, "w_down": w_down, "norm_final_g": norm_final_g}

def first_block(x, norm_mix_g, w_in, pool_w, pool_scale, pool_out_norm_g, attn_out_norm_g,
              w_out, norm_mlp_g, w_up, w_down, norm_final_g):
    B, S, _ = x.shape
    slopes = alibi_slopes()
    for l in range(DEPTH):
        h = rmsnorm(x, norm_mix_g[l])
        proj = h @ w_in[l]
        u = proj[..., :POOL_WIDTH]
        qkv = proj[..., POOL_WIDTH:].reshape(B, S, 3, N_HEADS, HEAD_DIM)
        y_pool = rmsnorm(pool_mixer(u, pool_w[l], pool_scale[l]), pool_out_norm_g[l])
        y_attn = rmsnorm(dilated_attention(qkv[:, :, 0], qkv[:, :, 1], qkv[:, :, 2], slopes),
                         attn_out_norm_g[l])
        x = x + jnp.concatenate([y_pool, y_attn], axis=-1) @ w_out[l]
        h = rmsnorm(x, norm_mlp_g[l])
        x = x + jnp.square(jax.nn.relu(h @ w_up[l])) @ w_down[l]
    return rmsnorm(x, norm_final_g)


N_BRANCH = 4
BRANCH_WIDTH = 512
EPS = 1e-6
N_MOD = 6
DA_HEADS = 4
DA_QK_DIM = 64
DA_V_DIM = 128
N_BUCKETS = 32
MAX_DISTANCE = 128
ML_HEADS = 4
ML_DIM = 128
ML_CONV = 4
GLA_HEADS = 4
GLA_DK = 64
GLA_DV = 128
GLA_RANK = 16
GLA_TAU = 16.0
CHUNK = 64
S5_CH = 16
S5_GROUPS = BRANCH_WIDTH // S5_CH
S5_STATE = 64
FFN_HIDDEN = -(-(8 * D_MODEL) // (3 * 256)) * 256

DA_QK_W = DA_HEADS * 2 * DA_QK_DIM
DA_V_W = DA_HEADS * DA_V_DIM
ML_W = ML_HEADS * ML_DIM
GLA_K_W = GLA_HEADS * GLA_DK
GLA_V_W = GLA_HEADS * GLA_DV
IN_SPLITS = (DA_QK_W, DA_QK_W, DA_V_W,
             ML_W, ML_W, ML_W, ML_W, ML_HEADS, ML_HEADS,
             GLA_K_W, GLA_K_W, GLA_V_W, GLA_V_W, GLA_RANK,
             BRANCH_WIDTH)
IN_WIDTH_2 = sum(IN_SPLITS)


def _rms(x, gain=None):
    xf = x.astype(jnp.float32)
    y = xf * lax.rsqrt(jnp.mean(xf * xf, axis=-1, keepdims=True) + EPS)
    if gain is not None:
        y = y * gain.astype(jnp.float32)
    return y.astype(x.dtype)

def _t5_bucket(rel):
    n = jnp.maximum(-rel, 0)
    exact = N_BUCKETS // 2
    nf = jnp.maximum(n, 1).astype(jnp.float32)
    large = exact + (jnp.log(nf / exact) / math.log(MAX_DISTANCE / exact)
                     * (N_BUCKETS - exact)).astype(jnp.int32)
    return jnp.where(n < exact, n, jnp.minimum(large, N_BUCKETS - 1))

def _causal_conv(x, w):
    k, s = w.shape[0], x.shape[1]
    xp = jnp.pad(x, ((0, 0), (k - 1, 0), (0, 0)))
    y = xp[:, 0:s] * w[0]
    for j in range(1, k):
        y = y + xp[:, j:j + s] * w[j]
    return y

def _to_chunks(t, nc):
    t = t.reshape((t.shape[0], nc, CHUNK) + t.shape[2:])
    return jnp.moveaxis(jnp.swapaxes(t, 2, 3), 1, 0)

def _from_chunks(t):
    t = jnp.swapaxes(jnp.moveaxis(t, 0, 1), 2, 3)
    return t.reshape((t.shape[0], t.shape[1] * t.shape[2], -1))

def _diff_attention(q, k, v, lam, lam_init, rel_bias):
    B, S = q.shape[:2]
    q = q.reshape(B, S, DA_HEADS, 2, DA_QK_DIM).transpose(3, 0, 2, 1, 4)
    k = k.reshape(B, S, DA_HEADS, 2, DA_QK_DIM).transpose(3, 0, 2, 1, 4)
    v = v.reshape(B, S, DA_HEADS, DA_V_DIM).transpose(0, 2, 1, 3)
    kpos = jnp.arange(S)
    scale = DA_QK_DIM ** -0.5

    def block(i):
        start = i * Q_BLOCK
        qb = lax.dynamic_slice_in_dim(q, start, Q_BLOCK, axis=3)
        rel = kpos[None, :] - (start + jnp.arange(Q_BLOCK))[:, None]
        bias = jnp.transpose(rel_bias[_t5_bucket(rel)], (2, 0, 1))
        logits = jnp.einsum('mbhqd,mbhkd->mbhqk', qb, k) * scale + bias
        logits = jnp.where(rel <= 0, logits, -jnp.inf)
        p = jax.nn.softmax(logits, axis=-1)
        return jnp.einsum('bhqk,bhkd->bhqd', p[0] - lam * p[1], v)

    o = lax.map(block, jnp.arange(S // Q_BLOCK))
    o = o.transpose(1, 0, 3, 2, 4).reshape(B, S, DA_HEADS, DA_V_DIM)
    return (_rms(o) * (1.0 - lam_init)).reshape(B, S, DA_V_W)

def _mlstm(q, k, v, ig, lf):
    B, S = q.shape[:2]
    nc = S // CHUNK
    causal = jnp.tril(jnp.ones((CHUNK, CHUNK), bool))

    def step(carry, xs):
        C, n, m = carry
        qc, kc, vc, ic, lfc = xs
        b = jnp.cumsum(lfc, axis=-1)
        Dm = jnp.where(causal, b[..., :, None] - b[..., None, :] + ic[..., None, :], -jnp.inf)
        inter = b + m[..., None]
        m_t = jnp.maximum(inter, jnp.max(Dm, axis=-1))
        s = jnp.einsum('bhtd,bhjd->bhtj', qc, kc) * jnp.exp(Dm - m_t[..., None])
        a = jnp.exp(inter - m_t)
        num = a[..., None] * jnp.einsum('bhtd,bhde->bhte', qc, C) + jnp.einsum('bhtj,bhje->bhte', s, vc)
        den = a * jnp.einsum('bhtd,bhd->bht', qc, n) + jnp.sum(s, axis=-1)
        h = num / jnp.maximum(jnp.abs(den), jnp.exp(-m_t))[..., None]
        m_new = m_t[..., -1]
        a_state = jnp.exp(b[..., -1] + m - m_new)
        wj = jnp.exp(b[..., -1:] - b + ic - m_new[..., None])
        C = a_state[..., None, None] * C + jnp.einsum('bhj,bhjd,bhje->bhde', wj, kc, vc)
        n = a_state[..., None] * n + jnp.einsum('bhj,bhjd->bhd', wj, kc)
        return (C, n, m_new), h

    init = (jnp.zeros((B, ML_HEADS, ML_DIM, ML_DIM), jnp.float32),
            jnp.zeros((B, ML_HEADS, ML_DIM), jnp.float32),
            jnp.zeros((B, ML_HEADS), jnp.float32))
    xs = (_to_chunks(q, nc), _to_chunks(k, nc), _to_chunks(v, nc), _to_chunks(ig, nc), _to_chunks(lf, nc))
    _, h = lax.scan(step, init, xs)
    return _from_chunks(h)

def _gla(q, k, v, la):
    B, S = q.shape[:2]
    nc = S // CHUNK
    causal = jnp.tril(jnp.ones((CHUNK, CHUNK), bool))[:, :, None]

    def step(St, xs):
        qc, kc, vc, lac = xs
        bc = jnp.cumsum(lac, axis=2)
        inter = jnp.einsum('bhtd,bhde->bhte', qc * jnp.exp(bc), St)
        decay = jnp.exp(jnp.where(causal, bc[:, :, :, None, :] - bc[:, :, None, :, :], -jnp.inf))
        att = jnp.einsum('bhtd,bhjd,bhtjd->bhtj', qc, kc, decay)
        o = inter + jnp.einsum('bhtj,bhje->bhte', att, vc)
        last = bc[:, :, -1:, :]
        St = jnp.exp(last[:, :, 0])[..., None] * St + jnp.einsum('bhjd,bhje->bhde', kc * jnp.exp(last - bc), vc)
        return St, o

    init = jnp.zeros((B, GLA_HEADS, GLA_DK, GLA_DV), jnp.float32)
    xs = (_to_chunks(q, nc), _to_chunks(k, nc), _to_chunks(v, nc), _to_chunks(la, nc))
    _, o = lax.scan(step, init, xs)
    return _from_chunks(o).reshape(B, S, GLA_HEADS, GLA_DV)

def _s5(u, a_re, a_im, log_dt, b_re, b_im, c_re, c_im, d_skip):
    f32 = jnp.float32
    a_re, a_im = a_re.astype(f32), a_im.astype(f32)
    dt = jnp.exp(log_dt.astype(f32))[:, None]
    mag = jnp.exp(dt * a_re)
    ab_re, ab_im = mag * jnp.cos(dt * a_im), mag * jnp.sin(dt * a_im)
    nr, ni = ab_re - 1.0, ab_im
    den = a_re * a_re + a_im * a_im
    f_re = (nr * a_re + ni * a_im) / den
    f_im = (ni * a_re - nr * a_im) / den
    b_re, b_im = b_re.astype(f32), b_im.astype(f32)
    bb_re = f_re[..., None] * b_re - f_im[..., None] * b_im
    bb_im = f_re[..., None] * b_im + f_im[..., None] * b_re
    c_re, c_im, d_skip = c_re.astype(f32), c_im.astype(f32), d_skip.astype(f32)

    def combine(e1, e2):
        a1r, a1i, b1r, b1i = e1
        a2r, a2i, b2r, b2i = e2
        return (a2r * a1r - a2i * a1i, a2r * a1i + a2i * a1r,
                a2r * b1r - a2i * b1i + b2r, a2r * b1i + a2i * b1r + b2i)

    def one_seq(us):
        bu_re = jnp.einsum('sgc,gpc->sgp', us, bb_re)
        bu_im = jnp.einsum('sgc,gpc->sgp', us, bb_im)
        ar = jnp.broadcast_to(ab_re, bu_re.shape)
        ai = jnp.broadcast_to(ab_im, bu_re.shape)
        _, _, xr, xi = lax.associative_scan(combine, (ar, ai, bu_re, bu_im), axis=0)
        return (jnp.einsum('sgp,gcp->sgc', xr, c_re) - jnp.einsum('sgp,gcp->sgc', xi, c_im)
                + d_skip * us)

    return lax.map(one_seq, u)

def second_inputs(seed: int = 0) -> dict:
    key = jax.random.key(seed)
    ks = jax.random.split(key, 32)
    f32 = jnp.float32

    def nrm(k, shape, scale):
        return jax.random.normal(k, shape, f32) * scale

    L, D, W, G, P, C = DEPTH, D_MODEL, BRANCH_WIDTH, S5_GROUPS, S5_STATE, S5_CH
    return {
        'x': nrm(ks[0], (BATCH, SEQ, D), 1.0),
        'c': nrm(ks[1], (BATCH, D), 1.0),
        'ada_w': nrm(ks[2], (L, D, N_MOD * D), 0.5 * D ** -0.5),
        'ada_b': nrm(ks[3], (L, N_MOD * D), 0.01),
        'norm_g': 1.0 + nrm(ks[4], (L, 4, D), 0.01),
        'w_in': nrm(ks[5], (L, D, IN_WIDTH_2), D ** -0.5),
        'rel_bias': nrm(ks[6], (N_BUCKETS, DA_HEADS), 0.5),
        'diff_lambda': nrm(ks[7], (L, 4, DA_QK_DIM), 0.1),
        'ml_conv': nrm(ks[8], (L, ML_CONV, 2 * ML_W), ML_CONV ** -0.5),
        'ml_gate_b': jnp.stack([nrm(ks[9], (L, ML_HEADS), 0.1),
                                jnp.linspace(3.0, 6.0, ML_HEADS, dtype=f32)[None, :]
                                + nrm(ks[10], (L, ML_HEADS), 0.1)], axis=1),
        'gla_wa2': nrm(ks[11], (L, GLA_RANK, GLA_K_W), GLA_RANK ** -0.5),
        'gla_ba': nrm(ks[12], (L, GLA_K_W), 0.1),
        's5_a_re': -0.5 + nrm(ks[13], (L, G, P), 0.01),
        's5_a_im': math.pi * jnp.arange(P, dtype=f32) + nrm(ks[14], (L, G, P), 0.01),
        's5_log_dt': jax.random.uniform(ks[15], (L, G), f32, math.log(1e-3), math.log(1e-1)),
        's5_b_re': nrm(ks[16], (L, G, P, C), (2 * C) ** -0.5),
        's5_b_im': nrm(ks[17], (L, G, P, C), (2 * C) ** -0.5),
        's5_c_re': nrm(ks[18], (L, G, C, P), (2 * P) ** -0.5),
        's5_c_im': nrm(ks[19], (L, G, C, P), (2 * P) ** -0.5),
        's5_d': nrm(ks[20], (L, G, C), 1.0),
        's5_glu_w': nrm(ks[21], (L, W, W), W ** -0.5),
        's5_glu_b': nrm(ks[22], (L, W), 0.01),
        'w_branch': nrm(ks[23], (L, N_BRANCH, W, D), W ** -0.5),
        'w_gate': nrm(ks[24], (L, N_BRANCH, D, D), D ** -0.5),
        'b_gate': nrm(ks[25], (L, N_BRANCH, D), 0.01),
        'w_out': nrm(ks[26], (L, D, D), D ** -0.5),
        'ffn_w_in': nrm(ks[27], (L, D, 2 * FFN_HIDDEN), D ** -0.5),
        'ffn_w_out': nrm(ks[28], (L, FFN_HIDDEN, D), FFN_HIDDEN ** -0.5),
    }

def second_block(x, c, ada_w, ada_b, norm_g, w_in, rel_bias, diff_lambda, ml_conv, ml_gate_b,
              gla_wa2, gla_ba, s5_a_re, s5_a_im, s5_log_dt, s5_b_re, s5_b_im, s5_c_re, s5_c_im,
              s5_d, s5_glu_w, s5_glu_b, w_branch, w_gate, b_gate, w_out, ffn_w_in, ffn_w_out):
    B, S, _ = x.shape
    f32 = jnp.float32
    split_points = [int(p) for p in np.cumsum(IN_SPLITS)[:-1]]
    cs = jax.nn.silu(c)
    rel_bias32 = rel_bias.astype(f32)
    for l in range(DEPTH):
        mod = (cs @ ada_w[l] + ada_b[l]).reshape(B, N_MOD, D_MODEL)[:, :, None, :]
        shift_m, scale_m, gate_m, shift_f, scale_f, gate_f = (mod[:, i] for i in range(N_MOD))

        h = _rms(x, norm_g[l, 0]) * (1.0 + scale_m) + shift_m
        proj = (h @ w_in[l]).astype(f32)
        (da_q, da_k, da_v, ml_q, ml_k, ml_v, ml_o, ml_i, ml_f,
         gl_q, gl_k, gl_v, gl_r, gl_a, s5_u) = jnp.split(proj, split_points, axis=-1)

        lam_init = 0.8 - 0.6 * math.exp(-0.3 * l)
        lp = diff_lambda[l].astype(f32)
        lam = jnp.exp(jnp.sum(lp[0] * lp[1])) - jnp.exp(jnp.sum(lp[2] * lp[3])) + lam_init
        o_a = _diff_attention(da_q, da_k, da_v, lam, lam_init, rel_bias32)

        qk = jax.nn.silu(_causal_conv(jnp.concatenate([ml_q, ml_k], axis=-1), ml_conv[l].astype(f32)))
        mq, mk = jnp.split(qk, 2, axis=-1)
        gb = ml_gate_b[l].astype(f32)
        hm = _mlstm(mq.reshape(B, S, ML_HEADS, ML_DIM),
                    mk.reshape(B, S, ML_HEADS, ML_DIM) * ML_DIM ** -0.5,
                    ml_v.reshape(B, S, ML_HEADS, ML_DIM),
                    ml_i + gb[0], jax.nn.log_sigmoid(ml_f + gb[1]))
        o_b = jax.nn.sigmoid(ml_o) * hm

        la = jax.nn.log_sigmoid(gl_a @ gla_wa2[l].astype(f32) + gla_ba[l].astype(f32)) / GLA_TAU
        og = _gla(gl_q.reshape(B, S, GLA_HEADS, GLA_DK) * GLA_DK ** -0.5,
                  gl_k.reshape(B, S, GLA_HEADS, GLA_DK),
                  gl_v.reshape(B, S, GLA_HEADS, GLA_DV),
                  la.reshape(B, S, GLA_HEADS, GLA_DK))
        o_c = _rms(og).reshape(B, S, GLA_V_W) * jax.nn.silu(gl_r)

        y = _s5(s5_u.reshape(B, S, S5_GROUPS, S5_CH), s5_a_re[l], s5_a_im[l], s5_log_dt[l],
                s5_b_re[l], s5_b_im[l], s5_c_re[l], s5_c_im[l], s5_d[l]).reshape(B, S, BRANCH_WIDTH)
        z = jax.nn.gelu(y)
        o_d = z * jax.nn.sigmoid(z @ s5_glu_w[l].astype(f32) + s5_glu_b[l].astype(f32))

        branches = (o_a, o_b, o_c, o_d)
        merged = [jax.nn.sigmoid(h @ w_gate[l, i] + b_gate[l, i]) * (branches[i].astype(h.dtype) @ w_branch[l, i])
                  for i in range(N_BRANCH)]
        mix = (merged[0] + merged[1] + merged[2] + merged[3]) @ w_out[l]
        x = x + (gate_m * _rms(mix, norm_g[l, 1])).astype(x.dtype)

        h = _rms(x, norm_g[l, 2]) * (1.0 + scale_f) + shift_f
        a, g = jnp.split(h @ ffn_w_in[l], 2, axis=-1)
        x = x + (gate_f * _rms((jax.nn.silu(a) * g) @ ffn_w_out[l], norm_g[l, 3])).astype(x.dtype)
    return x


def setup_inputs(seed=0):
    out = dict(first_inputs(seed))
    for name, value in second_inputs(seed + 1).items():
        if name != "x":
            out[name + "_2"] = value
    return out


def reference(
    x, norm_mix_g, w_in, pool_w, pool_scale, pool_out_norm_g, attn_out_norm_g, w_out,
    norm_mlp_g, w_up, w_down, norm_final_g, c_2, ada_w_2, ada_b_2, norm_g_2, w_in_2, rel_bias_2,
    diff_lambda_2, ml_conv_2, ml_gate_b_2, gla_wa2_2, gla_ba_2, s5_a_re_2, s5_a_im_2,
    s5_log_dt_2, s5_b_re_2, s5_b_im_2, s5_c_re_2, s5_c_im_2, s5_d_2, s5_glu_w_2, s5_glu_b_2,
    w_branch_2, w_gate_2, b_gate_2, w_out_2, ffn_w_in_2, ffn_w_out_2,
):
    x = first_block(
        x, norm_mix_g, w_in, pool_w, pool_scale, pool_out_norm_g, attn_out_norm_g, w_out,
        norm_mlp_g, w_up, w_down, norm_final_g,
    )
    return second_block(
        x, c_2, ada_w_2, ada_b_2, norm_g_2, w_in_2, rel_bias_2, diff_lambda_2, ml_conv_2,
        ml_gate_b_2, gla_wa2_2, gla_ba_2, s5_a_re_2, s5_a_im_2, s5_log_dt_2, s5_b_re_2,
        s5_b_im_2, s5_c_re_2, s5_c_im_2, s5_d_2, s5_glu_w_2, s5_glu_b_2, w_branch_2, w_gate_2,
        b_gate_2, w_out_2, ffn_w_in_2, ffn_w_out_2,
    )


_drawn_inputs = setup_inputs


def setup_inputs(seed=0):
    import zlib

    import numpy as np

    out = dict(_drawn_inputs(seed))
    spreads = {}
    factors = {'ada_b_2': 3.315,
     'norm_g_2': 7.569,
     'gla_ba_2': 6.012,
     's5_a_re_2': 64.0,
     's5_a_im_2': 64.0,
     's5_log_dt_2': 64.0,
     's5_b_re_2': 64.0,
     's5_b_im_2': 64.0,
     's5_c_re_2': 64.0,
     's5_c_im_2': 64.0,
     's5_glu_b_2': 64.0,
     'b_gate_2': 36.443,
     'rel_bias_2': 7.784}
    for name, (base, spread) in spreads.items():
        noise = np.random.default_rng([zlib.crc32(name.encode()), seed]).standard_normal(out[name].shape)
        drawn = base * np.exp(spread * noise) if base else spread * noise
        out[name] = __import__('jax').numpy.asarray(drawn.astype(out[name].dtype))
    for name, factor in factors.items():
        out[name] = (out[name] * factor).astype(out[name].dtype)
    return out
```

```python
from contextlib import ExitStack

import numpy as np
import concourse.bass as bass
from concourse import mybir

F32 = mybir.dt.float32
F32R = mybir.dt.float32r
ALU = mybir.AluOpType
ACT = mybir.ActivationFunctionType
AX_X = mybir.AxisListType.X

P = 128
S = 256
D = 2048
KT = D // P
TT = S // P
EPS = 1e-6
NEG = -1e30

UK = 2
COLS = 512
FT = COLS // P
RAW = 8
LEAD = 4
UA = KT // UK
UB = FT // UK
D_FF = 4 * D
FFN = 5632
MLP_SUPER = D_FF // COLS
FFN_SUPER = FFN // COLS
R_IN, R_OUT, R_MLP, R_IN2, R_GATE, R_OUT2, R_FFN = 0, 8, 12, 44, 56, 76, 80
H_IN, H_OUT, H_MLP, H_IN2, H_GATE, H_OUT2, H_FFN = 0, 4, 6, 46, 52, 68, 70
R_END_H = H_FFN + 3 * FFN_SUPER

POOL_WINDOWS = (2, 4, 8, 16)
POOL_PAD = max(POOL_WINDOWS)
HEADS = 8
DILATED_PATTERNS = ((128, 1), (512, 4), (2048, 16))
A_SCALE = float(P) ** -0.5

BR_HEADS = 4
DA_DIM = 64
DA_SCALE = float(DA_DIM) ** -0.5
N_BUCKETS, MAX_DISTANCE = 32, 128
LAM_INIT = 0.8 - 0.6 * float(np.exp(-0.3 * 0))
ML_SCALE = float(P) ** -0.5
GLA_DK = 64
GLA_SCALE = float(GLA_DK) ** -0.5
GLA_TAU = 16.0
GLA_RANK = 16
GLA_LEVELS = (64, 32, 16, 8, 4, 2, 1)
S5_STATE, S5_CH = 64, 16
ROUND = 1.5 * 2.0 ** 23
_two_pi = 2 * np.pi
_c1 = float(np.floor(_two_pi * 2 ** 8) / 2 ** 8)
_c2 = float(np.floor((_two_pi - _c1) * 2 ** 20) / 2 ** 20)
TWO_PI = (_c1, _c2, float(_two_pi - _c1 - _c2))
PI_BELOW = 3.1415925
N_SMALL = 10
COL_GATES, COL_GLA, COL_GLA_A, COL_S5 = 3584, 3592, 5128, 5144
ADA_COLS = 768
ADA_F = ADA_COLS // P
ADA_GROUPS = 6 * D // ADA_COLS
ADA_RING = 4
ADA_ACC, ADA_SLOTS = (44, 16), (32, 44)

CW = P + S

CONST = {}
_at = 0
for _n, _w in (("ident", P), ("dist", CW), ("count", CW), ("causal", P), ("levels", len(GLA_LEVELS) * P),
               ("poolfix", len(POOL_WINDOWS) * POOL_PAD), ("s5b", 32), ("s5c", 8), ("rowsel", BR_HEADS * P)):
    CONST[_n] = (_at, _w)
    _at += _w
CONST_COLS = _at

VEC_GROUPS = [
    [("norm_mix_g", 16), ("pool_scale", 8), ("pool_out_norm_g", 8), ("attn_out_norm_g", 8), ("norm_mlp_g", 16),
     ("norm_final_g", 16), ("c_2", 16), ("gla_ba_2", 2), ("s5_d_2", 4), ("s5_glu_b_2", 4), ("s5_a_re_2", 16)],
    [("norm_g_2", 64), ("b_gate_2", 64)],
    [("ada_b_2", 96), ("ml_conv_2", 32)],
    [("s5_a_im_2", 16)],
]
VEC = {}
for _g, _rows in enumerate(VEC_GROUPS):
    _r = 0
    for _n, _k in _rows:
        VEC[_n] = (_g, _r, _k)
        _r += _k
VEC_ROWS = [sum(k for _, k in rows) for rows in VEC_GROUPS]
N_VEC_DMAS = sum(len(rows) for rows in VEC_GROUPS)


def shape_constants():
    c = {n: np.zeros((P, w), np.float32) for n, (_, w) in CONST.items()}
    c["ident"][:] = np.eye(P)
    p = np.arange(P)[:, None]
    for qt, (at, keys) in enumerate(((0, P), (P, S))):
        d = qt * P + p - np.arange(keys)[None, :]
        n = np.zeros(d.shape)
        for window, dil in DILATED_PATTERNS:
            n += (d >= 0) & (d <= window) & (d % dil == 0)
        c["count"][:, at:at + keys] = n
        c["dist"][:, at:at + keys] = np.where(n > 0, -d, NEG)
    j, t = np.arange(P)[:, None], np.arange(P)[None, :]
    for i, level in enumerate(GLA_LEVELS):
        c["levels"][:, i * P:(i + 1) * P] = ((t // level) % 2 == 1) & (j // level == t // level - 1)
    c["causal"][:] = np.where(j >= t, 0.0, NEG)
    for g, w in enumerate(POOL_WINDOWS):
        c["poolfix"][:, g * POOL_PAD:(g + 1) * POOL_PAD] = 1.0 / np.minimum(np.arange(POOL_PAD) + 1, w)
    for ii in range(4):
        for g in range(8):
            c["s5b"][:, ii * 8 + g] = (g == 2 * ii + np.arange(P) // S5_STATE)
    for g in range(8):
        c["s5c"][:, g] = np.arange(P) // S5_CH == g
    for h in range(BR_HEADS):
        c["rowsel"][h, h * P:(h + 1) * P] = 1.0
    n = S - 1 - np.arange(384)
    exact = N_BUCKETS // 2
    large = exact + (np.log(np.maximum(n, 1) / exact) / np.log(MAX_DISTANCE / exact) * (N_BUCKETS - exact)).astype(int)
    bucket = np.where(n < exact, n, np.minimum(large, N_BUCKETS - 1))
    for i in range(384):
        if n[i] >= 0:
            c["rowsel"][64 + bucket[i], i] = 1.0
        else:
            c["rowsel"][64 + N_BUCKETS, i] = NEG
    return np.concatenate([c[n] for n in CONST], axis=1)


SEMS = """const_in x_in vec_in small_in x_turned x_copied vec_turned vecs_ready cs_ready
lam_sums lam_exps bias_rows_ready bias_psum bias_copied bias_out bias_in
hi_ready lo_ready unit_done drained0 drained1
sq_ready sum_ready var_ready std_ready normed hop_hi hop_ready
pool_w_in pooled pool_psum pool_ready
a_scores a_masked a_negmax a_exp a_probs a_probsT_psum a_probsT a_vT_psum a_vT a_out_psum a_out
relu_sq hid_hi hid_ready
ada_used mod_psum mod_ready
small_w_in gates_ready
d_scores d_masked d_negmax d_exp d_probs d_probsT_psum d_probsT d_vT_psum d_vT d_out_psum d_out
hn_sq hn_sum hn_var hn_std
m_conv m_silu m_absz m_log m_rows m_bc m_BT m_qk m_vT_psum m_vT m_A m_E m_S m_ST_psum m_ST m_out_psum m_out m_sig
g_z_psum g_z g_absz g_log g_arg g_exp g_qk g_att_psum g_att_read g_vT_psum g_vT g_att g_x g_x_copied g_out_psum g_out g_sig
s_in s_dt s_exp s_trig s_sin s_bb s_pad s_turned s_BT s_bu_psum s_bu s_x s_cpad s_cturned s_CT s_y_psum s_y s_z s_glu_psum s_glu s_out
glu_w_in table_clear
op_hi gated sig_free merged_hi merged_ready
res_ready out_psum out_copied stored
act_chain dve_chain pool_chain""".split()


def two_blocks(nc, a, consts, out):
    ctx = ExitStack()

    def sb(name, shape, dt=F32):
        return ctx.enter_context(nc.sbuf_tensor(name, shape, dt))

    sem = {n: ctx.enter_context(nc.semaphore(n)) for n in SEMS}
    raw_landed = [ctx.enter_context(nc.semaphore(f"raw_landed{i}")) for i in range(RAW)]
    ada_landed = [ctx.enter_context(nc.semaphore(f"ada_landed{i}")) for i in range(ADA_RING)]
    drained = [sem["drained0"], sem["drained1"]]

    const = sb("const", [P, CONST_COLS])
    vecs = sb("vecs", [P, (len(VEC_GROUPS) - 1) * P + VEC_ROWS[-1]])
    x = sb("x", [P, KT, S])
    hop_hi = sb("hop_hi_part", [P, KT, S], F32R)
    hop_lo = sb("hop_lo_part", [P, KT, S], F32R)
    hid_hi = sb("hid_hi_part", [P, 2, FT, S], F32R)
    hid_lo = sb("hid_lo_part", [P, 2, FT, S], F32R)
    w_raw = sb("w_raw", [P, RAW, UK, COLS])
    w_hi = sb("w_hi", [P, LEAD, UK, COLS], F32R)
    w_lo = sb("w_lo", [P, LEAD, UK, COLS], F32R)
    NT = 56
    arena = sb("arena", [P, NT, S])
    ones = sb("ones", [P, P])
    var, std, rstd = (sb(n, [P, S]) for n in ("var", "std", "rstd"))
    fix = std
    cs = sb("cs", [P, KT])
    mod = sb("mod", [P, 6 * KT])
    gain5, gain6, gain7, gain8 = (sb(n, [P, KT]) for n in ("gain5", "gain6", "gain7", "gain8"))
    st = sb("st", [P, 2, 16])
    lam = arena[:, 52, :].rearrange("p (a b) -> p a b", a=4)
    lam_prod = arena[:, 53, 0:2 * DA_DIM].rearrange("p (a b) -> p a b", a=2)
    lam_s = sb("lam_s", [P, 8])
    bias_all = sb("bias_table", [P, BR_HEADS])
    BROWS = slice(64, 64 + N_BUCKETS + 1)
    bias_table = bias_all[BROWS, :]
    gate_b = sb("gate_b", [BR_HEADS, 2])
    row_store = sb("row_store", [P, 2, S])
    gate_rows = row_store[0:BR_HEADS]
    gla_a, wa2 = (row_store[64:64 + GLA_RANK, i, :] for i in range(2))
    BT = sb("BT", [P, TT, BR_HEADS])
    gate_bias = sb("gate_bias", [P, KT])
    s5b = [sb(n, [P, 16, S5_CH]) for n in ("s5b_re", "s5b_im")]
    s5c = [sb(n, [P, 4, S5_STATE]) for n in ("s5c_re", "s5c_im")]
    s5v = sb("s5v", [P, 16, 16])
    s5pow = [std[:, i * P:(i + 1) * P].rearrange("p (l i) -> p l i", l=8) for i in range(2)]
    bias_scratch = nc.dram_tensor("bias_scratch", [BR_HEADS, P, 384], F32, kind="Internal")

    PS = [ctx.enter_context(nc.psum_tensor(f"ps{i}", [P, 512], F32)) for i in range(8)]
    SETS = [(PS[0], PS[1]), (PS[2], PS[3])]

    def C(name, rows=P, lo=0, n=None):
        at, w = CONST[name]
        return const[0:rows, at + lo:at + (w if n is None else lo + n)]

    def vec(name, i=0, n=1):
        g, r, k = VEC[name]
        return vecs[:, g * P + r + i:g * P + r + i + n]

    def T(t, n=None):
        return arena[:, t, :] if n is None else arena[:, t:t + n, :]

    def flat(ap):
        return ap.rearrange("p a b -> p (a b)")

    ident = C("ident")

    def span(t, off, n):
        return arena[:, :, :].rearrange("p a b -> p (a b)")[:, t * S + off:t * S + off + n]

    def units(w):
        return w.rearrange("(q k p) n -> q p k n", p=P, k=UK)

    w_in, w_out, w_up, w_down = (units(a[n][0]) for n in ("w_in", "w_out", "w_up", "w_down"))
    w_in2, w_out2, w_ffn_in, w_ffn_out = (units(a[n][0]) for n in ("w_in_2", "w_out_2", "ffn_w_in_2", "ffn_w_out_2"))
    w_gate = a["w_gate_2"][0].rearrange("i (q k p) n -> i q p k n", p=P, k=UK)
    w_branch = a["w_branch_2"][0].rearrange("i (q k p) n -> i q p k n", p=P, k=UK)
    ada_w = a["ada_w_2"][0].rearrange("(k p) n -> k p n", p=P)

    NORMS = [(16, 1), (8, 1), (8, 1), (16, 1), (16, 0), (16, 1), (16, 0), (16, 1), (16, 0)]

    def before(n, what):
        return sum({"sq": k // 4, "normed": k, "hop": k * split}[what] for k, split in NORMS[:n])

    NORM_SQ = [0, 16, 16, 0, 0, 0, 16, 0, 16]
    NORM_T = [16, 24, 24, 16, None, 16, 32, 16, 32]

    block = ctx.enter_context(nc.Block())

    @block.sync
    def _(sp):
        sp.dma_start(flat(T(32, 16)).rearrange("p (t d) -> p t d", t=TT),
                     a["x"][0].rearrange("(t p) d -> p t d", p=P)).then_inc(sem["x_in"], 16)
        sp.dma_start(const[:], consts).then_inc(sem["const_in"], 16)

        def load(R, j, src, cond=True):
            if cond:
                sp.wait_ge(sem["lo_ready"], R * 8 + (j - RAW + 1))
            sp.dma_start(w_raw[:, j % RAW], src).then_inc(raw_landed[j % RAW], 16)

        for q in range(UA):
            load(0, q, w_in[q, :, :, 0:COLS], cond=False)
        with sp.Fori(1, 8) as c:
            col = sp.snap(c * COLS)
            for q in range(UA):
                load(R_IN + c, q, w_in[q, :, :, bass.ds(col, COLS)])
        with sp.Fori(0, 4) as c:
            col = sp.snap(c * COLS)
            for q in range(UA):
                load(R_OUT + c, q, w_out[q, :, :, bass.ds(col, COLS)])

        for q in range(UA):
            load(R_MLP, q, w_up[q, :, :, 0:COLS])
        with sp.Fori(0, MLP_SUPER - 1) as c:
            col = sp.snap(c * COLS + COLS)
            rows = [sp.snap(c * UB + k) for k in range(UB)]
            for q in range(UA):
                load(R_MLP + 1 + 2 * c, q, w_up[q, :, :, bass.ds(col, COLS)])
            for n in range(4):
                for k in range(UB):
                    load(R_MLP + 1 + 2 * c, UA + UB * n + k,
                         w_down[bass.ds(rows[k], 1), :, :, n * COLS:(n + 1) * COLS].rearrange("a p k n -> (a p) k n"))
        for n in range(4):
            for k in range(UB):
                load(R_IN2 - 1, UB * n + k, w_down[UB * (MLP_SUPER - 1) + k, :, :, n * COLS:(n + 1) * COLS])

        with sp.Fori(0, 7) as c:
            col = sp.snap(c * COLS)
            for q in range(UA):
                load(R_IN2 + c, q, w_in2[q, :, :, bass.ds(col, COLS)])
        with sp.Fori(0, 3) as c:
            col = sp.snap(c * COLS + COL_GLA)
            for q in range(UA):
                load(R_IN2 + 7 + c, q, w_in2[q, :, :, bass.ds(col, COLS)])
        for q in range(UA):
            load(R_IN2 + 10, q, w_in2[q, :, :, COL_S5:COL_S5 + COLS])
        for q in range(UA):
            sp.wait_ge(sem["lo_ready"], (R_IN2 + 11) * 8 + q - RAW + 1)
            for at, col in ((0, COL_GATES), (32, COL_GATES + BR_HEADS)):
                sp.dma_start(w_raw[:, q, :, at:at + BR_HEADS],
                             w_in2[q, :, :, col:col + BR_HEADS]).then_inc(sem["small_w_in"], 16)
            sp.dma_start(w_raw[:, q, :, 64:64 + GLA_RANK],
                         w_in2[q, :, :, COL_GLA_A:COL_GLA_A + GLA_RANK]).then_inc(raw_landed[q], 16)

        with sp.Fori(0, 4) as i:
            br = sp.snap(i * 1)
            for n in range(4):
                for q in range(UA):
                    load(R_GATE + 5 * i, 10 * n + q,
                         w_gate[bass.ds(br, 1), q, :, :, n * COLS:(n + 1) * COLS].rearrange("a p k n -> (a p) k n"))
                for k in range(UB):
                    load(R_GATE + 5 * i, 10 * n + UA + k,
                         w_branch[bass.ds(br, 1), k, :, :, n * COLS:(n + 1) * COLS].rearrange("a p k n -> (a p) k n"))
        with sp.Fori(0, 4) as c:
            col = sp.snap(c * COLS)
            for q in range(UA):
                load(R_OUT2 + c, q, w_out2[q, :, :, bass.ds(col, COLS)])

        for q in range(2 * UA):
            col = 0 if q < UA else FFN
            load(R_FFN, q, w_ffn_in[q % UA, :, :, col:col + COLS])
        with sp.Fori(0, FFN_SUPER - 1) as c:
            ca = sp.snap(c * COLS + COLS)
            cg = sp.snap(c * COLS + (FFN + COLS))
            rows = [sp.snap(c * UB + k) for k in range(UB)]
            for q in range(2 * UA):
                load(R_FFN + 2 + 3 * c, q, w_ffn_in[q % UA, :, :, bass.ds(ca if q < UA else cg, COLS)])
            for n in range(4):
                for k in range(UB):
                    load(R_FFN + 2 + 3 * c, 2 * UA + UB * n + k,
                         w_ffn_out[bass.ds(rows[k], 1), :, :, n * COLS:(n + 1) * COLS].rearrange("a p k n -> (a p) k n"))
        for n in range(4):
            for k in range(UB):
                load(R_FFN + 3 * FFN_SUPER - 1, UB * n + k, w_ffn_out[UB * (FFN_SUPER - 1) + k, :, :, n * COLS:(n + 1) * COLS])

        sp.wait_ge(sem["out_copied"], 8)
        sp.dma_start(out[0].rearrange("(t p) d -> p t d", p=P),
                     flat(T(0, 16)).rearrange("p (t d) -> p t d", t=TT)).then_inc(sem["stored"], 16)
        sp.wait_ge(sem["stored"], 16)

    @block.tensor
    def _(pe):
        def mm(o, w, r, start=True, stop=True):
            return nc.tensor.matmul(o, w, r, start=start, stop=stop, skip_group_check=True)

        def unit(R, j, s, hi, lo, k0, first, last, ftiles=FT):
            pe.wait_ge(sem["lo_ready"], R * 8 + (j + 1))
            slot = j % LEAD
            for f in range(ftiles):
                o = SETS[s][f // 2][:, (f % 2) * S:(f % 2 + 1) * S]
                cols = slice(f * P, (f + 1) * P)
                for k in range(UK):
                    mm(o, w_hi[:, slot, k, cols], hi[:, k0 + k], start=first and k == 0 and f % 2 == 0, stop=False)
                    mm(o, w_hi[:, slot, k, cols], lo[:, k0 + k], start=False, stop=False)
                    m = mm(o, w_lo[:, slot, k, cols], hi[:, k0 + k], start=False, stop=last and k == UK - 1)
            m.then_inc(sem["unit_done"], 1)

        def chunk(R, j0, H, s, hi=hop_hi, lo=hop_lo, nu=UA, ftiles=FT):
            pe.wait_ge(drained[s], H + 1)
            for q in range(nu):
                unit(R, j0 + q, s, hi, lo, UK * q, q == 0, q == nu - 1, ftiles)

        def norm(n):
            tiles = NORMS[n][0]
            sq = T(NORM_SQ[n], tiles)
            for k in range(tiles):
                if k % 4 == 0:
                    pe.wait_ge(sem["sq_ready"], before(n, "sq") + k // 4 + 1)
                m = mm(PS[4][:, 0:S], ones[:], sq[:, k], start=k == 0, stop=k == tiles - 1)
            m.then_inc(sem["sum_ready"], 1)

        def operand(n):
            pe.wait_ge(sem["hop_ready"], before(n + 1, "hop"))

        def scores(o, q, k):
            mm(o[:, 0:P], q[:, 0:P], k[:, 0:P])
            return mm(o[:, P:CW], q[:, P:S], k[:, 0:S])

        def turn_probs(o, p):
            for b in range(3):
                m = nc.tensor.transpose(o[:, b * P:(b + 1) * P], p[:, b * P:(b + 1) * P], ident)
            return m

        def weighted_values(o, v, pt):
            mm(o[:, 0:S], v[:, 0:P], pt[:, 0:S], stop=False)
            return mm(o[:, P:S], v[:, P:S], pt[:, S:CW], start=False)

        def turn_pair(o, src):
            nc.tensor.transpose(o[:, 0:P], src[:, 0:P], ident)
            return nc.tensor.transpose(o[:, P:S], src[:, P:S], ident)

        pe.wait_ge(sem["const_in"], 16)
        pe.wait_ge(sem["vec_in"], 16 * N_VEC_DMAS)
        for g, rows in enumerate(VEC_ROWS):
            m = nc.tensor.transpose(PS[0][:, g * P:g * P + rows], span(48, g * P, P)[0:rows, :], ident[0:rows, 0:rows])
        m.then_inc(sem["vec_turned"], 1)
        pe.wait_ge(sem["x_in"], 16)
        for b in range(KT // 2):
            if b >= 4:
                pe.wait_ge(sem["x_copied"], b - 3)
            for k in range(2):
                for t in range(TT):
                    m = nc.tensor.transpose(PS[4 + b % 4][:, (k * TT + t) * P:(k * TT + t + 1) * P],
                                            span(32, t * D + (2 * b + k) * P, P), ident)
            m.then_inc(sem["x_turned"], 1)
        pe.wait_ge(sem["bias_rows_ready"], 1)
        pe.wait_ge(sem["vecs_ready"], 1)
        for h in range(BR_HEADS):
            m = mm(PS[h][:, 0:384], span(50, h * P, P)[BROWS, :], C("rowsel", n=384)[BROWS, :])
        m.then_inc(sem["bias_psum"], 1)
        pe.wait_ge(sem["x_copied"], 8)
        norm(0)
        pe.wait_ge(sem["bias_copied"], 1)

        operand(0)
        with pe.Fori(0, 4) as i:
            for s in range(2):
                chunk(R_IN + 2 * i, UA * s, H_IN + i, s)

        for s in range(2):
            pe.wait_ge(drained[s], H_OUT + 1)
        for h in range(HEADS + 1):
            if h < HEADS:
                if h >= 2:
                    pe.wait_ge(sem["a_masked"], h - 1)
                scores(PS[h % 2], T(8 + h), T(16 + h)).then_inc(sem["a_scores"], 1)
                if h >= 2:
                    pe.wait_ge(sem["a_vT"], h - 1)
                turn_pair(PS[2 + h % 2], T(24 + h)).then_inc(sem["a_vT_psum"], 1)
            if h >= 1:
                g = h - 1
                pe.wait_ge(sem["a_probs"], g + 1)
                if g >= 2:
                    pe.wait_ge(sem["a_probsT"], g - 1)
                turn_probs(PS[4 + g % 2], span(46, CW * (g % 2), CW)).then_inc(sem["a_probsT_psum"], 1)
                pe.wait_ge(sem["a_probsT"], g + 1)
                pe.wait_ge(sem["a_vT"], g + 1)
                if g >= 2:
                    pe.wait_ge(sem["a_out"], g - 1)
                weighted_values(PS[6 + g % 2], T(24 + g), span(49, CW * (g % 2), CW)).then_inc(sem["a_out_psum"], 1)
        pe.wait_ge(sem["pool_w_in"], 16)
        pe.wait_ge(sem["a_masked"], HEADS)
        pe.wait_ge(sem["a_vT"], HEADS)
        pool_w = T(32, 8)
        for g in range(4):
            pe.wait_ge(sem["pooled"], g + 1)
            for f in range(2):
                for c in range(2):
                    m = mm(PS[g][:, f * S:(f + 1) * S], pool_w[:, 2 * g + c, f * P:(f + 1) * P], T(2 * g + c),
                           start=c == 0 and f == 0, stop=c == 1)
            m.then_inc(sem["pool_psum"], 1)
        pe.wait_ge(sem["a_out"], HEADS)
        pe.wait_ge(sem["a_probsT"], HEADS)
        norm(1)
        norm(2)
        operand(2)
        with pe.Fori(0, 2) as i:
            for s in range(2):
                chunk(R_OUT + 2 * i, UA * s, H_OUT + i, s)

        for s in range(2):
            pe.wait_ge(drained[s], H_MLP + 1)
        norm(3)
        operand(3)

        def down(R, j0, H, s0, par, ready):
            pe.wait_ge(sem["hid_ready"], ready)
            for n in range(4):
                s = (s0 + n) % 2
                chunk(R, j0 + UB * n, H + (s0 + n) // 2, s, hid_hi[:, par], hid_lo[:, par], UB)

        def modulation(used, acc):
            pe.wait_ge(sem["ada_used"], used)
            for f in range(ADA_F):
                m = mm(PS[5][:, f:f + 1], span(acc, f * P, P), ones[:, 0:1])
            m.then_inc(sem["mod_psum"], 1)

        chunk(R_MLP, 0, H_MLP, 0)
        with pe.Fori(0, MLP_SUPER // 2 - 1) as i:
            R, H = R_MLP + 1 + 4 * i, H_MLP + 5 * i
            chunk(R, 0, H, 1)
            down(R, 8, H + 1, 0, 0, 2 * i + 1)
            chunk(R, 16, H + 3, 0)
            modulation(16 * i + 16, ADA_ACC[0])
            down(R, 24, H + 3, 1, 1, 2 * i + 2)
        R, H = R_MLP + 29, H_MLP + 35
        chunk(R, 0, H, 1)
        down(R, 8, H + 1, 0, 0, MLP_SUPER - 1)
        modulation(16 * 8, ADA_ACC[0])
        down(R, 16, H + 3, 0, 1, MLP_SUPER)

        for s in range(2):
            pe.wait_ge(drained[s], H_IN2 + 1)
        norm(4)
        norm(5)
        operand(5)
        with pe.Fori(0, 5) as i:
            for s in range(2):
                chunk(R_IN2 + 2 * i, UA * s, H_IN2 + i, s)
        chunk(R_IN2 + 10, 0, H_IN2 + 5, 0)
        chunk(R_IN2 + 11, 0, H_IN2 + 5, 1, ftiles=1)

        for s in range(2):
            pe.wait_ge(drained[s], H_GATE + 1)
        pe.wait_ge(sem["gates_ready"], 1)
        for h in range(BR_HEADS):
            if h >= 1:
                pe.wait_ge(sem["d_masked"], 2 * h)
            for m in range(2):
                scores(PS[m], T(h)[64 * m:64 * m + 64], T(4 + h)[64 * m:64 * m + 64]).then_inc(sem["d_scores"], 1)
            if h >= 1:
                pe.wait_ge(sem["d_vT"], h)
            turn_pair(PS[2], T(8 + h)).then_inc(sem["d_vT_psum"], 1)
            pe.wait_ge(sem["d_probs"], h + 1)
            turn_probs(PS[3], span(53, 0, CW)).then_inc(sem["d_probsT_psum"], 1)
            pe.wait_ge(sem["d_probsT"], h + 1)
            pe.wait_ge(sem["d_vT"], h + 1)
            if h >= 2:
                pe.wait_ge(sem["d_out"], h - 1)
            weighted_values(PS[4 + h % 2], T(8 + h), span(53, CW, CW)).then_inc(sem["d_out_psum"], 1)

        def head_norm(n):
            pe.wait_ge(sem["hn_sq"], n + 1)
            for b in range(2):
                m = mm(PS[6 + b][:, :], ones[:], flat(T((50, 21)[n] + 2 * b, 2)))
            m.then_inc(sem["hn_sum"], 1)

        head_norm(0)

        pe.wait_ge(sem["m_rows"], 1)
        for t in range(TT):
            m = mm(PS[3][:, t * BR_HEADS:(t + 1) * BR_HEADS], span(11, t * P, P)[0:BR_HEADS, :],
                   ident[0:BR_HEADS, 0:BR_HEADS])
        m.then_inc(sem["m_BT"], 1)
        pe.wait_ge(sem["m_silu"], 1)
        for h in range(BR_HEADS):
            if h >= 1:
                pe.wait_ge(sem["m_A"], h)
            mm(PS[0][:, 0:S], C("rowsel", BR_HEADS, h * P, P), T(8)[0:BR_HEADS, :]).then_inc(sem["m_bc"], 1)
            if h >= 1:
                pe.wait_ge(sem["m_S"], h)
            scores(PS[1], T(44 + h), T(48 + h)).then_inc(sem["m_qk"], 1)
            if h >= 1:
                pe.wait_ge(sem["m_vT"], h)
            turn_pair(PS[2], T(20 + h)).then_inc(sem["m_vT_psum"], 1)
            pe.wait_ge(sem["m_S"], h + 1)
            if h >= 1:
                pe.wait_ge(sem["m_ST"], h)
            turn_probs(PS[4], span(52, 0, CW)).then_inc(sem["m_ST_psum"], 1)
            pe.wait_ge(sem["m_ST"], h + 1)
            pe.wait_ge(sem["m_vT"], h + 1)
            if h >= 1:
                pe.wait_ge(sem["m_out"], h)
            weighted_values(PS[5], T(20 + h), span(52, CW, CW)).then_inc(sem["m_out_psum"], 1)

        for t in range(2):
            m = mm(PS[0][:, t * S:(t + 1) * S], wa2[:, t * P:(t + 1) * P], gla_a, start=t == 0)
        m.then_inc(sem["g_z_psum"], 1)
        for h in range(BR_HEADS):
            if h >= 1:
                pe.wait_ge(sem["g_vT"], h)
            turn_pair(PS[1], T(32 + h)).then_inc(sem["g_vT_psum"], 1)
        for n, level in enumerate(GLA_LEVELS + (0, 128)):
            if level:
                pe.wait_ge(sem["g_qk"], n + 1 if level < 128 else len(GLA_LEVELS) + 1)
            if n >= 1:
                pe.wait_ge(sem["g_att_read"], n)
            q0, k0 = (28, 30) if level == 0 else (44, 46)
            for h in range(BR_HEADS):
                rows = slice(64 * (h % 2), 64 * (h % 2) + 64)
                q, k = T(q0 + h // 2)[rows], T(k0 + h // 2)[rows]
                o = PS[2 + h % 2]
                if level == 128:
                    m = mm(o[:, (h // 2) * P:(h // 2 + 1) * P], k[:, 0:P], q[:, P:S])
                else:
                    for t in range(TT):
                        m = mm(o[:, (h // 2) * S + t * P:(h // 2) * S + (t + 1) * P],
                               k[:, t * P:(t + 1) * P], q[:, t * P:(t + 1) * P])
            m.then_inc(sem["g_att_psum"], 1)
        pe.wait_ge(sem["g_att"], 1)
        pe.wait_ge(sem["g_x_copied"], 1)
        pe.wait_ge(sem["g_vT"], BR_HEADS)
        for h in range(BR_HEADS):
            o = PS[4 + h // 2][:, (h % 2) * S:(h % 2 + 1) * S]
            att = span(48 + 2 * (h % 2), (h // 2) * S, S)
            v = T(32 + h)
            mm(o[:, 0:P], v[:, 0:P], att[:, 0:P], start=h % 2 == 0)
            mm(o[:, P:S], v[:, 0:P], span(54, h * P, P), start=False, stop=False)
            m = mm(o[:, P:S], v[:, P:S], att[:, P:S], start=False)
        m.then_inc(sem["g_out_psum"], 1)
        head_norm(1)

        for t in range(4):
            pe.wait_ge(sem["s_pad"], t + 1)
            if t == 0:
                pe.wait_ge(sem["g_x_copied"], 1)
            else:
                pe.wait_ge(sem["s_BT"], t)
            for part in range(2):
                for ii in range(4):
                    m = nc.tensor.transpose(PS[part][:, ii * P:(ii + 1) * P], span(52 + 2 * part, ii * P, P), ident)
            m.then_inc(sem["s_turned"], 1)
            pe.wait_ge(sem["s_BT"], t + 1)
            if t >= 1:
                pe.wait_ge(sem["s_bu"], t)
            for part in range(2):
                for ii in range(4):
                    m = mm(PS[2 + 2 * part + ii // 2][:, (ii % 2) * S:(ii % 2 + 1) * S], span(44 + 2 * part, ii * P, P),
                           T(40 + t), start=ii % 2 == 0)
            m.then_inc(sem["s_bu_psum"], 1)
            pe.wait_ge(sem["s_cpad"], t + 1)
            for part in range(2):
                for ii in range(4):
                    m = nc.tensor.transpose(PS[part][:, ii * P:(ii + 1) * P], span(52 + 2 * part, ii * P, P), ident)
            m.then_inc(sem["s_cturned"], 1)
            pe.wait_ge(sem["s_CT"], t + 1)
            pe.wait_ge(sem["s_x"], t + 1)
            if t >= 1:
                pe.wait_ge(sem["s_y"], t)
            for part in range(2):
                for ii in range(4):
                    m = mm(PS[6][:, 0:S], span(48 + 2 * part, ii * P, P), T(32 + 4 * part + ii),
                           start=part == 0 and ii == 0, stop=part == 1 and ii == 3)
            m.then_inc(sem["s_y_psum"], 1)
        pe.wait_ge(sem["s_z"], 1)
        pe.wait_ge(sem["glu_w_in"], 16)
        glu = flat(T(16, 8)).rearrange("p (k n) -> p k n", k=4)
        for f in range(4):
            for k in range(4):
                m = mm(PS[f // 2][:, (f % 2) * S:(f % 2 + 1) * S], glu[:, k, f * P:(f + 1) * P], T(24 + k),
                       start=f % 2 == 0 and k == 0, stop=k == 3)
        m.then_inc(sem["s_glu_psum"], 1)

        pe.wait_ge(sem["s_out"], 1)
        with pe.Fori(0, 4) as i:
            R, H = R_GATE + 5 * i, H_GATE + 4 * i
            for n in range(4):
                chunk(R, 10 * n, H + n, 0)
                if n == 3:
                    modulation(32 * i + 16 * 10, ADA_ACC[1])
                if n == 0:
                    pe.wait_ge(sem["hid_ready"], i + (MLP_SUPER + 1))
                chunk(R, 10 * n + UA, H + n, 1, hid_hi[:, 0], hid_lo[:, 0], UB)
                if n == 1:
                    modulation(32 * i + 16 * 9, ADA_ACC[1])
        pe.wait_ge(sem["merged_ready"], 4)
        with pe.Fori(0, 2) as i:
            for s in range(2):
                chunk(R_OUT2 + 2 * i, UA * s, H_OUT2 + i, s)
        norm(6)
        norm(7)
        operand(7)

        base = MLP_SUPER + 4
        for s in range(2):
            chunk(R_FFN, UA * s, H_FFN, s)
        with pe.Fori(0, FFN_SUPER // 2) as i:
            R, H = R_FFN + 2 + 6 * i, H_FFN + 1 + 6 * i
            for par in range(2):
                for s in range(2):
                    chunk(R, 24 * par + UA * s, H + 3 * par, s)
                down(R, 24 * par + 16, H + 3 * par + 1, 0, par, 2 * i + (base + par + 1))
        R, H = R_FFN + 2 + 3 * (FFN_SUPER - 1), H_FFN + 1 + 3 * (FFN_SUPER - 1)
        down(R, 0, H, 0, (FFN_SUPER - 1) % 2, base + FFN_SUPER)
        norm(8)

        pe.wait_ge(sem["res_ready"], 2)
        for b in range(8):
            if b >= 4:
                pe.wait_ge(sem["out_copied"], b - 3)
            t, k0 = b // 4, 4 * (b % 4)
            for k in range(4):
                m = nc.tensor.transpose(PS[b % 4][:, k * P:(k + 1) * P], x[:, k0 + k, t * P:(t + 1) * P], ident)
            m.then_inc(sem["out_psum"], 1)

    @block.scalar
    def _(act):
        def copy(o, i, scale=1.0):
            return nc.scalar.activation(o, i, ACT.Copy, scale=scale)

        def split(R, j, first=False, cols=COLS):
            act.wait_ge(raw_landed[j % RAW], (R + j // RAW) * 16 + 16)
            if not first:
                act.wait_ge(sem["unit_done"], R * 8 + (j - LEAD + 1))
            copy(w_hi[:, j % LEAD, :, 0:cols], w_raw[:, j % RAW, :, 0:cols]).then_inc(sem["hi_ready"], 1)

        def halves(ap):
            return ap.rearrange("p (a b) -> p a b", a=2)

        def store_chunk(s, tile):
            for b in range(2):
                m = copy(arena[:, tile(2 * b), :], halves(SETS[s][b][:]))
            m.then_inc(drained[s], 1)

        def norm(n, src, bias=None):
            tiles, is_split = NORMS[n]
            for k in range(0, tiles, 4):
                nc.scalar.activation(T(NORM_SQ[n] + k, 4), src(k, 4), ACT.Square).then_inc(sem["sq_ready"], 1)
            act.wait_ge(sem["var_ready"], n + 1)
            nc.scalar.activation(std[:], var[:], ACT.Sqrt).then_inc(sem["std_ready"], 1)
            if is_split:
                dst = 8 if n == 2 else 0
                for k in range(tiles):
                    act.wait_ge(sem["normed"], before(n, "normed") + k + 1)
                    t = T(NORM_T[n] + k)
                    if bias is None:
                        m = copy(hop_hi[:, dst + k], t)
                    else:
                        m = nc.scalar.activation(hop_hi[:, dst + k], t, ACT.Identity, bias=bias(k))
                    m.then_inc(sem["hop_hi"], 1)

        def of_x(k, n):
            return x[:, k:k + n]

        def of_arena(t):
            return lambda k, n: T(t + k, n)

        for g, rows in enumerate(VEC_GROUPS):
            for name, k in rows:
                v = a[name]
                v = v if len(v.shape) == 1 else v[0]
                names = "abc"[:len(v.shape)]
                if len(names) > 1:
                    v = v.rearrange(f"{' '.join(names)} -> ({' '.join(names)})")
                act.dma_start(span(48, g * P, P)[VEC[name][1]:VEC[name][1] + k, :],
                              v.rearrange("(r c) -> r c", c=P)).then_inc(sem["vec_in"], 16)
        act.wait_ge(sem["vec_turned"], 1)
        for g, rows in enumerate(VEC_ROWS):
            m = copy(vecs[:, g * P:g * P + rows], PS[0][:, g * P:g * P + rows])
        m.then_inc(sem["vecs_ready"], 1)
        for b in range(KT // 2):
            act.wait_ge(sem["x_turned"], b + 1)
            copy(x[:, 2 * b:2 * b + 2], halves(PS[4 + b % 4][:])).then_inc(sem["x_copied"], 1)
        act.wait_ge(sem["x_copied"], 8)
        act.wait_ge(sem["vecs_ready"], 1)
        act.wait_ge(sem["bias_psum"], 1)
        for h in range(BR_HEADS):
            m = copy(span(32, h * 384, 384), PS[h][:, 0:384])
        m.then_inc(sem["bias_copied"], 1)
        for j in range(LEAD):
            split(0, j, first=True)
        norm(0, of_x)
        nc.scalar.activation(cs[:], vec("c_2", 0, KT), ACT.Silu).then_inc(sem["cs_ready"], 1)
        act.wait_ge(sem["lam_sums"], 1)
        nc.scalar.activation(lam_s[:, 2:4], lam_s[:, 0:2], ACT.Exp).then_inc(sem["lam_exps"], 1)

        with act.Fori(0, 4) as i:
            for j in range(2 * UA):
                split(R_IN + 2 * i, j + LEAD)
                if j % UA == UA - 1:
                    store_chunk(j // UA, lambda o: bass.ds(i * 8 + (4 * (j // UA) + o), 2))

        for h in range(HEADS + 1):
            if h < HEADS:
                act.wait_ge(sem["a_vT_psum"], h + 1)
                copy(T(24 + h), PS[2 + h % 2][:, 0:S]).then_inc(sem["a_vT"], 1)
                act.wait_ge(sem["a_negmax"], h + 1)
                e = span(46, CW * (h % 2), CW)
                for qt, cols in enumerate((slice(0, P), slice(P, CW))):
                    m = nc.scalar.activation(e[:, cols], e[:, cols], ACT.Exp, scale=A_SCALE,
                                             bias=st[:, h % 2, 2 + qt:3 + qt])
                m.then_inc(sem["a_exp"], 1)
            if h >= 1:
                g = h - 1
                act.wait_ge(sem["a_probsT_psum"], g + 1)
                if g >= 2:
                    act.wait_ge(sem["a_out_psum"], g - 1)
                copy(span(49, CW * (g % 2), CW), PS[4 + g % 2][:, 0:CW]).then_inc(sem["a_probsT"], 1)
                act.wait_ge(sem["a_out_psum"], g + 1)
                copy(T(8 + g), PS[6 + g % 2][:, 0:S]).then_inc(sem["a_out"], 1)
        for g in range(4):
            act.wait_ge(sem["pool_psum"], g + 1)
            for f in range(2):
                m = nc.scalar.activation(T(2 * g + f), PS[g][:, f * S:(f + 1) * S], ACT.Copy,
                                         scale=vec("pool_scale", 2 * g + f))
            m.then_inc(sem["pool_ready"], 1)
        act.wait_ge(sem["pool_ready"], 4)
        act.wait_ge(sem["a_out"], HEADS)
        norm(1, of_arena(0))
        norm(2, of_arena(8))
        with act.Fori(0, 2) as i:
            for j in range(2 * UA):
                split(R_OUT + 2 * i, j + LEAD)

        act.wait_ge(drained[0], H_MLP + 1)
        act.wait_ge(drained[1], H_MLP + 1)
        norm(3, of_x)

        def relu(s):
            for b in range(2):
                m = nc.scalar.activation(T(2 * b, 2), halves(SETS[s][b][:]), ACT.Relu)
            m.then_inc(drained[s], 1)

        def hidden_hi(par, sig, count, tile):
            act.wait_ge(sig, count)
            copy(hid_hi[:, par], T(tile, FT)).then_inc(sem["hid_hi"], 1)

        for j in range(UA):
            split(R_MLP, j + LEAD)
        relu(0)
        hidden_hi(0, sem["relu_sq"], 1, 4)
        with act.Fori(0, MLP_SUPER // 2 - 1) as i:
            for j in range(4 * UA):
                split(R_MLP + 1 + 4 * i, j + LEAD)
                if j in (7, 23):
                    relu(1 if j == 7 else 0)
                if j in (8, 24):
                    hidden_hi(1 if j == 8 else 0, sem["relu_sq"], 2 * i + (2 if j == 8 else 3), 4)
        for j in range(3 * UA):
            split(R_MLP + 29, j + LEAD)
            if j == 7:
                relu(1)
            if j == 8:
                hidden_hi(1, sem["relu_sq"], MLP_SUPER, 4)

        act.wait_ge(drained[0], H_IN2 + 1)
        act.wait_ge(drained[1], H_IN2 + 1)
        norm(4, of_x)
        act.wait_ge(sem["normed"], before(5, "normed"))
        norm(5, of_x, lambda k: mod[:, k:k + 1])

        with act.Fori(0, 5) as i:
            for j in range(2 * UA):
                split(R_IN2 + 2 * i, j + LEAD)
                if j % UA == UA - 1:
                    store_chunk(j // UA, lambda o: bass.ds(i * 8 + (4 * (j // UA) + o), 2))
        for j in range(2 * UA):
            narrow = UA <= j + LEAD < 2 * UA
            if j + LEAD == UA:
                act.wait_ge(sem["small_w_in"], 16 * 2 * UA)
            split(R_IN2 + 10, j + LEAD, cols=P if narrow else COLS)
            if j == UA - 1:
                store_chunk(0, lambda o: slice(40 + o, 42 + o))
        narrow = SETS[1][0]
        copy(gate_rows[:, 0, :], narrow[0:BR_HEADS, 0:S])
        copy(gate_rows[:, 1, :], narrow[32:32 + BR_HEADS, 0:S])
        copy(gla_a, narrow[64:64 + GLA_RANK, 0:S]).then_inc(drained[1], 1)
        act.wait_ge(drained[1], H_GATE + 1)
        act.sem_inc(sem["gates_ready"], 1)

        for h in range(BR_HEADS):
            act.wait_ge(sem["d_vT_psum"], h + 1)
            copy(T(8 + h), PS[2][:, 0:S]).then_inc(sem["d_vT"], 1)
            for m in range(2):
                act.wait_ge(sem["d_negmax"], 2 * h + m + 1)
                e = span(50, CW * m, CW)
                for qt, cols in enumerate((slice(0, P), slice(P, CW))):
                    i = nc.scalar.activation(e[:, cols], e[:, cols], ACT.Exp, bias=st[:, 0, 2 * m + qt:2 * m + qt + 1],
                                             accum_out=st[:, 1, 2 * m + qt:2 * m + qt + 1])
                i.then_inc(sem["d_exp"], 1)
            act.wait_ge(sem["d_probsT_psum"], h + 1)
            copy(span(53, CW, CW), PS[3][:, 0:CW]).then_inc(sem["d_probsT"], 1)
            act.wait_ge(sem["d_out_psum"], h + 1)
            copy(T(h), PS[4 + h % 2][:, 0:S]).then_inc(sem["d_out"], 1)
        act.wait_ge(sem["d_out"], BR_HEADS)

        def head_norm(n, src, sq):
            nc.scalar.activation(T(sq, 4), T(src, 4), ACT.Square).then_inc(sem["hn_sq"], 1)
            act.wait_ge(sem["hn_var"], n + 1)
            nc.scalar.activation(T(sq, 4), T(sq, 4), ACT.Sqrt).then_inc(sem["hn_std"], 1)

        head_norm(0, 0, 50)

        rows = BR_HEADS
        act.wait_ge(sem["m_absz"], 1)
        nc.scalar.activation(T(10)[0:rows, :], T(10)[0:rows, :], ACT.Exp, scale=-1.0).then_inc(sem["act_chain"], 1)
        act.wait_ge(sem["act_chain"], 1)
        nc.scalar.activation(T(10)[0:rows, :], T(10)[0:rows, :], ACT.Ln, bias=1.0).then_inc(sem["m_log"], 1)
        act.wait_ge(sem["m_conv"], 1)
        nc.scalar.activation(T(44, 8), T(44, 8), ACT.Silu).then_inc(sem["m_silu"], 1)
        nc.scalar.activation(T(24, 4), T(24, 4), ACT.Sigmoid).then_inc(sem["m_sig"], 1)
        act.wait_ge(sem["m_BT"], 1)
        copy(BT[:].rearrange("p a b -> p (a b)"), PS[3][:, 0:TT * BR_HEADS]).then_inc(sem["m_rows"], 1)
        for h in range(BR_HEADS):
            act.wait_ge(sem["m_vT_psum"], h + 1)
            copy(T(20 + h), PS[2][:, 0:S]).then_inc(sem["m_vT"], 1)
            act.wait_ge(sem["m_A"], h + 1)
            e = span(52, 0, CW)
            nc.scalar.activation(st[:, 1, 0:2], st[:, 0, 4:6], ACT.Exp)
            for qt, cols in enumerate((slice(0, P), slice(P, CW))):
                m = nc.scalar.activation(e[:, cols], e[:, cols], ACT.Exp, bias=st[:, 0, 2 + qt:3 + qt])
            m.then_inc(sem["m_E"], 1)
            act.wait_ge(sem["m_ST_psum"], h + 1)
            copy(span(52, CW, CW), PS[4][:, 0:CW]).then_inc(sem["m_ST"], 1)

        act.wait_ge(sem["g_z_psum"], 1)
        act.wait_ge(sem["m_out"], BR_HEADS)
        for t in range(2):
            m = nc.scalar.activation(T(19 + t), PS[0][:, t * S:(t + 1) * S], ACT.Identity, bias=vec("gla_ba_2", t))
        m.then_inc(sem["g_z"], 1)
        act.wait_ge(sem["g_absz"], 1)
        nc.scalar.activation(T(21, 2), T(21, 2), ACT.Exp, scale=-1.0).then_inc(sem["act_chain"], 1)
        act.wait_ge(sem["act_chain"], 2)
        nc.scalar.activation(T(21, 2), T(21, 2), ACT.Ln, bias=1.0).then_inc(sem["g_log"], 1)
        for h in range(BR_HEADS):
            act.wait_ge(sem["g_vT_psum"], h + 1)
            copy(T(32 + h), PS[1][:, 0:S]).then_inc(sem["g_vT"], 1)
        for n in range(len(GLA_LEVELS) + 1):
            act.wait_ge(sem["g_arg"], n + 1)
            nc.scalar.activation(T(21, 4), T(21, 4), ACT.Exp).then_inc(sem["g_exp"], 1)
        nc.scalar.activation(T(36, 4), T(36, 4), ACT.Silu).then_inc(sem["g_sig"], 1)
        act.wait_ge(sem["g_att_psum"], len(GLA_LEVELS) + 2)
        x_att = span(54, 0, BR_HEADS * P).rearrange("p (a b c) -> p b a c", a=2, b=2)
        for par in range(2):
            m = copy(x_att[:, par], halves(PS[2 + par][:, 0:2 * P]))
        m.then_inc(sem["g_x_copied"], 1)
        act.wait_ge(sem["g_out_psum"], 1)
        for b in range(2):
            m = copy(T(8 + 2 * b, 2), halves(PS[4 + b][:]), scale=GLA_SCALE)
        m.then_inc(sem["g_out"], 1)
        act.wait_ge(sem["g_out"], 1)
        head_norm(1, 8, 21)

        act.wait_ge(sem["small_in"], 16 * N_SMALL)
        DT, MAG, THR, SIN, HALF = 0, 1, 2, 3, 4
        nc.scalar.activation(s5v[:, DT], s5v[:, 15], ACT.Exp).then_inc(sem["s_dt"], 1)
        act.wait_ge(sem["s_trig"], 1)
        nc.scalar.activation(s5v[:, MAG], s5v[:, MAG], ACT.Exp).then_inc(sem["s_exp"], 1)
        nc.scalar.activation(s5v[:, SIN], s5v[:, THR], ACT.Sin)
        nc.scalar.activation(s5v[:, HALF], s5v[:, THR], ACT.Sin, scale=0.5).then_inc(sem["s_sin"], 1)
        for t in range(4):
            act.wait_ge(sem["s_turned"], t + 1)
            for part in range(2):
                m = copy(T(44 + 2 * part, 2), halves(PS[part][:]))
            m.then_inc(sem["s_BT"], 1)
            act.wait_ge(sem["s_bu_psum"], t + 1)
            for b in range(4):
                m = copy(T(24 + 2 * b, 2), halves(PS[2 + b][:]))
            m.then_inc(sem["s_bu"], 1)
            act.wait_ge(sem["s_cturned"], t + 1)
            for part in range(2):
                m = copy(T(48 + 2 * part, 2), halves(PS[part][:]), scale=1.0 if part == 0 else -1.0)
            m.then_inc(sem["s_CT"], 1)
        act.wait_ge(sem["s_y"], 4)
        nc.scalar.activation(T(24, 4), T(12, 4), ACT.Gelu_apprx_tanh).then_inc(sem["s_z"], 1)
        act.wait_ge(sem["s_glu_psum"], 1)
        for f in range(4):
            m = nc.scalar.activation(T(28 + f), PS[f // 2][:, (f % 2) * S:(f % 2 + 1) * S], ACT.Sigmoid,
                                     bias=vec("s5_glu_b_2", f))
        m.then_inc(sem["s_glu"], 1)

        act.wait_ge(sem["s_out"], 1)
        with act.Fori(0, 4) as i:
            for j in range(40):
                split(R_GATE + 5 * i, j + LEAD)
                if j == 0:
                    g, r, _ = VEC["b_gate_2"]
                    copy(gate_bias[:], vecs[:, bass.ds(i * KT + (g * P + r), KT)])
                    copy(hid_hi[:, 0], arena[:, bass.ds(i * FT, FT), :]).then_inc(sem["op_hi"], 1)
                    act.wait_ge(sem["op_hi"], i + 1)
                if j % 10 == 7:
                    n = j // 10
                    act.wait_ge(sem["sig_free"], 4 * i + (n + 1))
                    for f in range(FT):
                        m = nc.scalar.activation(T(36 + f), SETS[0][f // 2][:, (f % 2) * S:(f % 2 + 1) * S],
                                                 ACT.Sigmoid, bias=gate_bias[:, FT * n + f:FT * n + f + 1])
                    m.then_inc(drained[0], 1)
        act.wait_ge(sem["sig_free"], 17)
        for k in range(0, KT, 4):
            copy(hop_hi[:, k:k + 4], T(20 + k, 4)).then_inc(sem["merged_hi"], 1)
        with act.Fori(0, 2) as i:
            for j in range(2 * UA):
                split(R_OUT2 + 2 * i, j + LEAD)
                if j % UA == UA - 1:
                    store_chunk(j // UA, lambda o: bass.ds(i * 8 + (4 * (j // UA) + o), 2))
        act.wait_ge(drained[0], H_FFN + 1)
        act.wait_ge(drained[1], H_FFN + 1)
        norm(6, of_arena(0))
        act.wait_ge(sem["res_ready"], 1)
        norm(7, of_x, lambda k: mod[:, 3 * KT + k:3 * KT + k + 1])

        def silu():
            for b in range(2):
                m = nc.scalar.activation(T(16 + 2 * b, 2), halves(SETS[0][b][:]), ACT.Silu)
            m.then_inc(drained[0], 1)

        for j in range(2 * UA):
            split(R_FFN, j + LEAD)
            if j == 7:
                silu()
        hidden_hi(0, drained[1], H_FFN + 2, 20)
        with act.Fori(0, FFN_SUPER // 2) as i:
            for j in range(6 * UA):
                split(R_FFN + 2 + 6 * i, j + LEAD)
                par = j // 24
                if j % 24 == 7:
                    silu()
                if j % 24 == 16:
                    hidden_hi(1 - par, drained[1], 6 * i + (H_FFN + 1 + 3 * par + 2), 20)
        for j in range(UA - LEAD):
            split(R_FFN + 2 + 3 * (FFN_SUPER - 1), j + LEAD)
        act.wait_ge(drained[0], R_END_H + 1)
        act.wait_ge(drained[1], R_END_H + 1)
        norm(8, of_arena(0))
        for b in range(8):
            act.wait_ge(sem["out_psum"], b + 1)
            copy(span(0, b * 512, 512), PS[b % 4][:]).then_inc(sem["out_copied"], 1)

    @block.vector
    def _(dve):
        V = nc.vector
        steps = [0]

        def then(ins):
            steps[0] += 1
            ins.then_inc(sem["dve_chain"], 1)
            dve.wait_ge(sem["dve_chain"], steps[0])

        def stt(o, i0, scalar, i1, op0, op1, **k):
            return V.scalar_tensor_tensor(o, i0, scalar, i1, op0, op1, **k)

        def split(R, j, cols=COLS):
            dve.wait_ge(sem["hi_ready"], R * 8 + (j + 1))
            V.tensor_tensor(w_lo[:, j % LEAD, :, 0:cols], w_raw[:, j % RAW, :, 0:cols],
                            w_hi[:, j % LEAD, :, 0:cols].bitcast(F32), ALU.subtract).then_inc(sem["lo_ready"], 1)

        def halves(ap):
            return ap.rearrange("p (a b) -> p a b", a=2)

        def add_chunk(R, j, s, at, tile):
            dve.wait_ge(sem["unit_done"], R * 8 + (j + 1))
            for b in range(2):
                dst = at[:, tile(2 * b), :]
                m = V.tensor_tensor(dst, halves(SETS[s][b][:]), dst, ALU.add)
            m.then_inc(drained[s], 1)

        def norm(n, src, gain, bias=None, to=None):
            tiles, is_split = NORMS[n]
            dve.wait_ge(sem["sum_ready"], n + 1)
            V.tensor_scalar(var[:], PS[4][:, 0:S], 1.0 / (tiles * P), EPS, ALU.mult, ALU.add).then_inc(sem["var_ready"], 1)
            dve.wait_ge(sem["std_ready"], n + 1)
            then(V.reciprocal(rstd[:], std[:]))
            then(V.tensor_tensor(fix[:], rstd[:], rstd[:], ALU.mult))
            then(V.tensor_tensor(fix[:], fix[:], var[:], ALU.mult))
            then(V.tensor_scalar(fix[:], fix[:], -0.5, 1.5, ALU.mult, ALU.add))
            then(V.tensor_tensor(rstd[:], rstd[:], fix[:], ALU.mult))
            for k in range(tiles):
                o = to[:, k] if to is not None else T(NORM_T[n] + k)
                stt(o, src(k), gain(k), rstd[:], ALU.mult, ALU.mult).then_inc(sem["normed"], 1)
            if is_split:
                dst = 8 if n == 2 else 0
                for k in range(tiles):
                    dve.wait_ge(sem["hop_hi"], before(n, "hop") + k + 1)
                    hi, t = hop_hi[:, dst + k].bitcast(F32), T(NORM_T[n] + k)
                    if bias is None:
                        m = V.tensor_tensor(hop_lo[:, dst + k], t, hi, ALU.subtract)
                    else:
                        m = stt(hop_lo[:, dst + k], t, bias(k), hi, ALU.add, ALU.subtract)
                    m.then_inc(sem["hop_ready"], 1)

        def residual(n):
            dve.wait_ge(sem["normed"], before(n + 1, "normed"))
            for k in range(0, KT, 4):
                m = V.tensor_tensor(x[:, k:k + 4], x[:, k:k + 4], T(NORM_T[n] + k, 4), ALU.add)
            m.then_inc(sem["res_ready"], 1)

        def of_x(k):
            return x[:, k]

        def of_arena(t):
            return lambda k: T(t + k)

        QT = (slice(0, P), slice(P, CW))

        V.memset(ones[:], 1.0)
        V.memset(bias_all[:], 1.0).then_inc(sem["dve_chain"], 1)
        steps[0] += 1
        dve.wait_ge(sem["dve_chain"], 1)
        dve.sem_inc(drained[0], 1)
        dve.sem_inc(drained[1], 1)
        dve.sem_inc(sem["sig_free"], 1)
        dve.sem_inc(sem["table_clear"], 1)
        dve.wait_ge(sem["small_in"], 16 * N_SMALL)
        for h in range(BR_HEADS):
            m = V.tensor_scalar(span(50, h * P, P)[BROWS, :], ones[BROWS, :],
                                bias_table[:, h:h + 1], None, ALU.mult)
        m.then_inc(sem["bias_rows_ready"], 1)
        then(V.tensor_tensor(lam_prod, lam[:, 0::2, :], lam[:, 1::2, :], ALU.mult))
        V.reduce_sum(lam_s[:, 0:2], lam_prod, axis=AX_X).then_inc(sem["lam_sums"], 1)
        for j in range(LEAD):
            split(0, j)
        dve.wait_ge(sem["vecs_ready"], 1)
        norm(0, of_x, lambda k: vec("norm_mix_g", k))
        dve.wait_ge(sem["lam_exps"], 1)
        then(V.tensor_tensor(lam_s[:, 4:5], lam_s[:, 3:4], lam_s[:, 2:3], ALU.subtract))
        then(V.tensor_scalar(lam_s[:, 5:6], lam_s[:, 4:5], -LAM_INIT, None, ALU.add))
        neg_lam = lam_s[:, 5:6]

        with dve.Fori(0, 4) as i:
            for j in range(2 * UA):
                split(R_IN + 2 * i, j + LEAD)

        for h in range(HEADS + 1):
            if h < HEADS:
                s, stat = span(46, CW * (h % 2), CW), st[:, h % 2]
                dve.wait_ge(sem["a_scores"], h + 1)
                if h >= 2:
                    dve.wait_ge(sem["a_probsT_psum"], h - 1)
                slope = 2.0 ** (-8.0 * (h + 1) / HEADS)
                stt(s, C("dist"), slope / A_SCALE, PS[h % 2][:, 0:CW], ALU.mult, ALU.add).then_inc(sem["a_masked"], 1)
                dve.wait_ge(sem["a_masked"], h + 1)
                for qt, cols in enumerate(QT):
                    m = V.reduce_max(stat[:, qt:qt + 1], s[:, cols], axis=AX_X)
                then(m)
                V.tensor_scalar(stat[:, 2:4], stat[:, 0:2], -A_SCALE, None, ALU.mult).then_inc(sem["a_negmax"], 1)
            if h >= 1:
                g = h - 1
                p, stat = span(46, CW * (g % 2), CW), st[:, g % 2]
                dve.wait_ge(sem["a_exp"], g + 1)
                for qt, cols in enumerate(QT):
                    m = stt(p[:, cols], p[:, cols], 1.0, C("count")[:, cols], ALU.mult, ALU.mult,
                            accum_out=stat[:, 4 + qt:5 + qt])
                then(m)
                then(V.reciprocal(stat[:, 6:8], stat[:, 4:6]))
                for qt, cols in enumerate(QT):
                    m = V.tensor_scalar(p[:, cols], p[:, cols], stat[:, 6 + qt:7 + qt], None, ALU.mult)
                m.then_inc(sem["a_probs"], 1)
        norm(1, of_arena(0), lambda k: vec("pool_out_norm_g", k))
        norm(2, of_arena(8), lambda k: vec("attn_out_norm_g", k))
        with dve.Fori(0, 2) as i:
            for j in range(2 * UA):
                split(R_OUT + 2 * i, j + LEAD)
                if j % UA == UA - 1:
                    add_chunk(R_OUT + 2 * i, j, j // UA, x, lambda o: bass.ds(i * 8 + (4 * (j // UA) + o), 2))
        dve.wait_ge(drained[0], H_MLP + 1)
        dve.wait_ge(drained[1], H_MLP + 1)
        norm(3, of_x, lambda k: vec("norm_mlp_g", k))
        dve.wait_ge(sem["cs_ready"], 1)

        def square(s, H):
            dve.wait_ge(drained[s], H + 2)
            V.tensor_tensor(T(4, FT), T(0, FT), T(0, FT), ALU.mult).then_inc(sem["relu_sq"], 1)

        def hidden_lo(par, count, tile):
            dve.wait_ge(sem["hid_hi"], count)
            V.tensor_tensor(hid_lo[:, par], T(tile, FT), hid_hi[:, par].bitcast(F32),
                            ALU.subtract).then_inc(sem["hid_ready"], 1)

        def ada(g, k, where):
            slot = k % ADA_RING
            acc = span(ADA_ACC[where], 0, ADA_COLS)
            w = span(ADA_SLOTS[where], slot * ADA_COLS, ADA_COLS)
            dve.wait_ge(ada_landed[slot], (g * (KT // ADA_RING) + (k // ADA_RING + 1)) * 16)
            if k == 0:
                m = V.tensor_scalar(acc, w, cs[:, 0:1], None, ALU.mult)
            else:
                dve.wait_ge(sem["ada_used"], g * KT + k)
                m = stt(acc, w, cs[:, k:k + 1], acc, ALU.mult, ALU.add)
            m.then_inc(sem["ada_used"], 1)

        def modulation(g):
            dve.wait_ge(sem["mod_psum"], g + 1)
            vg, r, _ = VEC["ada_b_2"]
            cols = bass.ds(g * ADA_F, ADA_F)
            V.tensor_tensor(mod[:, cols], PS[5][:, 0:ADA_F], vecs[:, bass.ds(g * ADA_F + (vg * P + r), ADA_F)],
                            ALU.add).then_inc(sem["mod_ready"], 1)

        def down_ends(R, j, j0, s0, at):
            q = j - j0
            if 0 <= q < 4 * UB and q % UB == UB - 1:
                n = q // UB
                add_chunk(R, j, (s0 + n) % 2, at, lambda o: slice(FT * n + o, FT * n + o + 2))

        for j in range(UA):
            split(R_MLP, j + LEAD)
        square(0, H_MLP)
        hidden_lo(0, 1, 4)
        with dve.Fori(0, MLP_SUPER // 2 - 1) as i:
            R, H = R_MLP + 1 + 4 * i, H_MLP + 5 * i
            for j in range(4 * UA):
                split(R, j + LEAD)
                if j == 7:
                    square(1, H)
                if j == 23:
                    square(0, H + 3)
                if j in (9, 25):
                    hidden_lo(1 if j == 9 else 0, 2 * i + (2 if j == 9 else 3), 4)
                down_ends(R, j, 8, 0, x)
                down_ends(R, j, 24, 1, x)
                if j < 24 and j % 3 != 2:
                    ada(i, j - j // 3, 0)
                if j == 26:
                    modulation(i)
        for j in range(3 * UA):
            split(R_MLP + 29, j + LEAD)
            if j == 7:
                square(1, H_MLP + 35)
            if j == 9:
                hidden_lo(1, MLP_SUPER, 4)
            down_ends(R_MLP + 29, j, 8, 0, x)
            down_ends(R_MLP + 29, j, 16, 0, x)
            if j < KT:
                ada(7, j, 0)
            if j == 18:
                modulation(7)
        dve.wait_ge(drained[0], H_IN2 + 1)
        dve.wait_ge(drained[1], H_IN2 + 1)

        norm(4, of_x, lambda k: vec("norm_final_g", k), to=x)
        dve.wait_ge(sem["mod_ready"], 8)
        then(stt(gain5[:], mod[:, KT:2 * KT], 1.0, vec("norm_g_2", 0, KT), ALU.add, ALU.mult))
        then(V.tensor_tensor(gain6[:], mod[:, 2 * KT:3 * KT], vec("norm_g_2", KT, KT), ALU.mult))
        norm(5, of_x, lambda k: gain5[:, k:k + 1], bias=lambda k: mod[:, k:k + 1])

        with dve.Fori(0, 5) as i:
            for j in range(2 * UA):
                split(R_IN2 + 2 * i, j + LEAD)
        for j in range(2 * UA):
            split(R_IN2 + 10, j + LEAD, cols=P if UA <= j + LEAD < 2 * UA else COLS)

        dve.wait_ge(sem["bias_in"], 32)
        stat = st[:, 0]
        for h in range(BR_HEADS):
            for m in range(2):
                s = span(50, CW * m, CW)
                dve.wait_ge(sem["d_scores"], 2 * h + m + 1)
                stt(s, PS[m][:, 0:CW], DA_SCALE, span(44, h * CW, CW), ALU.mult, ALU.add).then_inc(sem["d_masked"], 1)
                dve.wait_ge(sem["d_masked"], 2 * h + m + 1)
                for qt, cols in enumerate(QT):
                    i = V.reduce_max(st[:, 0, 4 + 2 * m + qt:5 + 2 * m + qt], s[:, cols], axis=AX_X)
                then(i)
                V.tensor_scalar(st[:, 0, 2 * m:2 * m + 2], st[:, 0, 4 + 2 * m:6 + 2 * m], -1.0, None,
                                ALU.mult).then_inc(sem["d_negmax"], 1)
            dve.wait_ge(sem["d_exp"], 2 * h + 2)
            then(V.reciprocal(st[:, 1, 4:8], st[:, 1, 0:4]))
            then(V.tensor_scalar(st[:, 1, 6:8], st[:, 1, 6:8], neg_lam, None, ALU.mult))
            e0, e1, p = span(50, 0, CW), span(50, CW, CW), span(53, 0, CW)
            for qt, cols in enumerate(QT):
                i = V.tensor_scalar(e0[:, cols], e0[:, cols], st[:, 1, 4 + qt:5 + qt], None, ALU.mult)
            then(i)
            if h >= 1:
                dve.wait_ge(sem["d_probsT_psum"], h)
            for qt, cols in enumerate(QT):
                i = stt(p[:, cols], e1[:, cols], st[:, 1, 6 + qt:7 + qt], e0[:, cols], ALU.mult, ALU.add)
            i.then_inc(sem["d_probs"], 1)

        def head_norm(n, sq):
            dve.wait_ge(sem["hn_sum"], n + 1)
            for b in range(2):
                m = V.tensor_scalar(T(sq + 2 * b, 2), halves(PS[6 + b][:]), 1.0 / P, EPS, ALU.mult, ALU.add)
            m.then_inc(sem["hn_var"], 1)
            dve.wait_ge(sem["hn_std"], n + 1)
            then(V.reciprocal(T(sq, 4), T(sq, 4)))

        head_norm(0, 50)
        then(stt(T(0, 4), T(0, 4), 1.0 - LAM_INIT, T(50, 4), ALU.mult, ALU.mult))

        rows = BR_HEADS
        ig, z, b = gate_rows[:, 0, :], gate_rows[:, 1, :], T(11)[0:rows, :]
        soft, a_row = T(10)[0:rows, :], T(8)[0:rows, :]
        then(V.tensor_scalar(z, z, gate_b[:, 1:2], None, ALU.add))
        stt(soft, z, -1.0, z, ALU.mult, ALU.max).then_inc(sem["m_absz"], 1)
        for t in range(8):
            o, i = T(44 + t), T(12 + t)
            then(V.tensor_scalar(o, i, vec("ml_conv_2", 3 * 8 + t), None, ALU.mult))
            for tap in (2, 1, 0):
                lag = 3 - tap
                m = stt(o[:, lag:S], i[:, 0:S - lag], vec("ml_conv_2", tap * 8 + t), o[:, lag:S], ALU.mult, ALU.add)
                if tap:
                    then(m)
        then(m)
        dve.sem_inc(sem["m_conv"], 1)
        dve.wait_ge(sem["m_log"], 1)
        then(stt(soft, z, 0.0, soft, ALU.min, ALU.subtract))
        then(V.memset(T(9)[0:rows, :], 1.0))
        then(V.tensor_tensor_scan(b, T(9)[0:rows, :], soft, 0.0, ALU.mult, ALU.add))
        stt(a_row, ig, gate_b[:, 0:1], b, ALU.add, ALU.subtract).then_inc(sem["m_rows"], 1)
        for h in range(BR_HEADS):
            dve.wait_ge(sem["m_bc"], h + 1)
            if h >= 1:
                dve.wait_ge(sem["m_ST_psum"], h)
            e = span(52, 0, CW)
            V.tensor_tensor(e[:, 0:P], PS[0][:, 0:P], C("causal"), ALU.add)
            V.tensor_copy(e[:, P:S], PS[0][:, 0:P])
            then(V.tensor_tensor(e[:, S:CW], PS[0][:, P:S], C("causal"), ALU.add))
            for qt, cols in enumerate(QT):
                m = V.reduce_max(st[:, 0, qt:qt + 1], e[:, cols], axis=AX_X)
            then(m)
            then(V.tensor_scalar(st[:, 0, 0:2], st[:, 0, 0:2], 0.0, None, ALU.max))
            if h == 0:
                dve.wait_ge(sem["m_rows"], 2)
            V.tensor_scalar(st[:, 0, 2:4], st[:, 0, 0:2], -1.0, None, ALU.mult)
            stt(st[:, 0, 4:6], st[:, 0, 0:2], -1.0, BT[:, :, h], ALU.mult, ALU.subtract).then_inc(sem["m_A"], 1)
            dve.wait_ge(sem["m_qk"], h + 1)
            dve.wait_ge(sem["m_E"], h + 1)
            for qt, cols in enumerate(QT):
                m = stt(e[:, cols], PS[1][:, cols], ML_SCALE, e[:, cols], ALU.mult, ALU.mult,
                        accum_out=st[:, 1, 4 + qt:5 + qt])
            then(m)
            then(stt(st[:, 1, 4:6], st[:, 1, 4:6], -1.0, st[:, 1, 4:6], ALU.mult, ALU.max))
            then(V.tensor_tensor(st[:, 1, 4:6], st[:, 1, 4:6], st[:, 1, 0:2], ALU.max))
            then(V.reciprocal(st[:, 1, 6:8], st[:, 1, 4:6]))
            for qt, cols in enumerate(QT):
                m = V.tensor_scalar(e[:, cols], e[:, cols], st[:, 1, 6 + qt:7 + qt], None, ALU.mult)
            m.then_inc(sem["m_S"], 1)
            dve.wait_ge(sem["m_sig"], 1)
            dve.wait_ge(sem["m_out_psum"], h + 1)
            V.tensor_tensor(T(4 + h), PS[5][:, 0:S], T(24 + h), ALU.mult).then_inc(sem["m_out"], 1)

        dve.wait_ge(sem["g_z"], 1)
        stt(T(21, 2), T(19, 2), -1.0, T(19, 2), ALU.mult, ALU.max).then_inc(sem["g_absz"], 1)
        dve.wait_ge(sem["g_log"], 1)
        then(stt(T(19, 2), T(19, 2), 0.0, T(21, 2), ALU.min, ALU.subtract))
        then(V.tensor_scalar(T(19, 2), T(19, 2), 1.0 / GLA_TAU, None, ALU.mult))
        then(V.memset(T(23), 1.0))
        run = span(16, 0, 2 * (S + 1)).rearrange("p (a b) -> p a b", a=2)
        then(V.memset(run[:, :, 0:1], 0.0))
        for t in range(2):
            m = V.tensor_tensor_scan(run[:, t, 1:S + 1], T(23), T(19 + t), 0.0, ALU.mult, ALU.add)
        then(m)

        def level_args(level):
            nb = S // level
            now = run[:, :, 1:S + 1].rearrange("p a (n l) -> p a n l", l=level)
            arg = T(21, 4).rearrange("p (w a) (n l) -> p w a n l", w=2, l=level)
            start = run[:, :, 0:S].rearrange("p a (n l) -> p a n l", l=level)[:, :, :, 0:1]
            end = now[:, :, :, level - 1:level]
            for t in range(2):
                V.tensor_tensor(arg[:, 0, t], now[:, t], start[:, t].to_broadcast([P, nb, level]), ALU.subtract)
                m = V.tensor_tensor(arg[:, 1, t], end[:, t].to_broadcast([P, nb, level]), now[:, t], ALU.subtract)
            m.then_inc(sem["g_arg"], 1)

        for n, level in enumerate(GLA_LEVELS + (0, 128)):
            if level:
                q = n if level < 128 else len(GLA_LEVELS)
                level_args(level)
                dve.wait_ge(sem["g_exp"], q + 1)
                if n >= 1:
                    dve.wait_ge(sem["g_att_psum"], n)
                V.tensor_tensor(T(44, 2), T(21, 2), T(28, 2), ALU.mult)
                V.tensor_tensor(T(46, 2), T(23, 2), T(30, 2), ALU.mult).then_inc(sem["g_qk"], 1)
            if level < 128:
                dve.wait_ge(sem["g_att_psum"], n + 1)
                mask = (C("levels", lo=n * P, n=P) if level else ident).unsqueeze(1).to_broadcast([P, 4, P])
                for par in range(2):
                    acc = span(48 + 2 * par, 0, 512).rearrange("p (a b) -> p a b", a=4)
                    tmp = span(52, 0, 512).rearrange("p (a b) -> p a b", a=4)
                    ps = PS[2 + par][:].rearrange("p (a b) -> p a b", a=4)
                    m = V.tensor_tensor(acc if n == 0 else tmp, ps, mask, ALU.mult)
                    if par == 1:
                        m.then_inc(sem["g_att_read"], 1)
                        dve.wait_ge(sem["g_att_read"], n + 1)
                    else:
                        then(m)
                    if n:
                        then(V.tensor_tensor(acc, acc, tmp, ALU.add))
        dve.sem_inc(sem["g_att"], 1)
        head_norm(1, 21)
        dve.wait_ge(sem["g_sig"], 1)
        then(V.tensor_tensor(T(8, 4), T(8, 4), T(21, 4), ALU.mult))
        then(V.tensor_tensor(T(8, 4), T(8, 4), T(36, 4), ALU.mult))

        DT, MAG, THR, SIN, HALF, COS, RE, IM, DEN, FRE, FIM, T0, T1, K = range(14)
        are, aim = vec("s5_a_re_2", 0, 16), vec("s5_a_im_2", 0, 16)

        def v(i):
            return s5v[:, i]

        dve.wait_ge(sem["s_dt"], 1)
        then(V.tensor_tensor(v(MAG), v(DT), are, ALU.mult))
        then(V.tensor_tensor(v(THR), v(DT), aim, ALU.mult))
        then(V.tensor_scalar(v(K), v(THR), float(1 / (2 * np.pi)), ROUND, ALU.mult, ALU.add))
        then(V.tensor_scalar(v(K), v(K), -ROUND, None, ALU.add))
        for part in TWO_PI:
            then(stt(v(THR), v(K), -part, v(THR), ALU.mult, ALU.add))
        then(V.tensor_scalar(v(THR), v(THR), -PI_BELOW, PI_BELOW, ALU.max, ALU.min))
        dve.sem_inc(sem["s_trig"], 1)
        dve.wait_ge(sem["s_sin"], 1)
        then(V.tensor_tensor(v(COS), v(HALF), v(HALF), ALU.mult))
        then(V.tensor_scalar(v(COS), v(COS), -2.0, 1.0, ALU.mult, ALU.add))
        then(V.tensor_tensor(v(RE), v(MAG), v(COS), ALU.mult))
        then(V.tensor_tensor(v(IM), v(MAG), v(SIN), ALU.mult))
        then(V.tensor_scalar(v(RE), v(RE), -1.0, None, ALU.add))
        then(V.tensor_tensor(v(DEN), are, are, ALU.mult))
        then(V.tensor_tensor(v(T0), aim, aim, ALU.mult))
        then(V.tensor_tensor(v(DEN), v(DEN), v(T0), ALU.add))
        then(V.reciprocal(v(DEN), v(DEN)))
        for o, p0, p1, op in ((FRE, (RE, are), (IM, aim), ALU.add), (FIM, (IM, are), (RE, aim), ALU.subtract)):
            then(V.tensor_tensor(v(T0), v(p0[0]), p0[1], ALU.mult))
            then(V.tensor_tensor(v(T1), v(p1[0]), p1[1], ALU.mult))
            then(V.tensor_tensor(v(o), v(T0), v(T1), op))
            then(V.tensor_tensor(v(o), v(o), v(DEN), ALU.mult))
        wide = [P, 16, S5_CH]
        fre, fim = (v(i).unsqueeze(2).to_broadcast(wide) for i in (FRE, FIM))
        t54, t55 = (T(i).rearrange("p (i c) -> p i c", c=S5_CH) for i in (54, 55))
        then(V.tensor_tensor(t54, s5b[1][:], fim, ALU.mult))
        then(V.tensor_tensor(t55, s5b[0][:], fim, ALU.mult))
        for o, t, op in ((s5b[0], t54, ALU.subtract), (s5b[1], t55, ALU.add)):
            then(V.tensor_tensor(o[:], o[:], fre, ALU.mult))
            then(V.tensor_tensor(o[:], o[:], t, op))
        then(V.tensor_copy(s5pow[0][:, 0], v(COS)))
        then(V.tensor_copy(s5pow[1][:, 0], v(SIN)))
        for l in range(7):
            c0, s0, c1, s1 = s5pow[0][:, l], s5pow[1][:, l], s5pow[0][:, l + 1], s5pow[1][:, l + 1]
            then(V.tensor_tensor(v(T0), s0, s0, ALU.mult))
            then(V.tensor_tensor(c1, c0, c0, ALU.mult))
            then(V.tensor_tensor(c1, c1, v(T0), ALU.subtract))
            then(stt(s1, c0, 2.0, s0, ALU.mult, ALU.mult))
        cosT, sinT = T(16, 4), T(20, 4)
        bu, rot = (T(24, 4), T(28, 4)), (T(32, 4), T(36, 4))
        for t in range(4):
            mask = C("s5b").rearrange("p (i g) -> p i g", i=4).unsqueeze(3).to_broadcast([P, 4, 8, S5_CH])
            if t >= 1:
                dve.wait_ge(sem["s_cturned"], t)
            for part in range(2):
                m = V.tensor_tensor(span(52 + 2 * part, 0, 512).rearrange("p (i g c) -> p i g c", i=4, g=8),
                                    s5b[part][:, 4 * t:4 * t + 4].unsqueeze(2).to_broadcast([P, 4, 8, S5_CH]), mask, ALU.mult)
            m.then_inc(sem["s_pad"], 1)
            V.memset(cosT[:, :, 0:1], 1.0)
            then(V.memset(sinT[:, :, 0:1], 0.0))
            for l in range(8):
                n = 1 << l
                c1, s1 = (s5pow[i][:, l, 4 * t:4 * t + 4].unsqueeze(2).to_broadcast([P, 4, n]) for i in range(2))
                c0, s0 = cosT[:, :, 0:n], sinT[:, :, 0:n]
                cn, sn = cosT[:, :, n:2 * n], sinT[:, :, n:2 * n]
                tmp = rot[0][:, :, 0:n]
                if l == 0 and t >= 1:
                    dve.wait_ge(sem["s_y_psum"], t)
                then(V.tensor_tensor(tmp, s0, s1, ALU.mult))
                then(V.tensor_tensor(cn, c0, c1, ALU.mult))
                then(V.tensor_tensor(cn, cn, tmp, ALU.subtract))
                then(V.tensor_tensor(tmp, c0, s1, ALU.mult))
                then(V.tensor_tensor(sn, s0, c1, ALU.mult))
                then(V.tensor_tensor(sn, sn, tmp, ALU.add))
            dve.wait_ge(sem["s_bu"], t + 1)
            V.tensor_tensor(rot[0], bu[0], cosT, ALU.mult)
            then(V.tensor_tensor(rot[1], bu[1], sinT, ALU.mult))
            then(V.tensor_tensor(rot[0], rot[0], rot[1], ALU.add))
            V.tensor_tensor(rot[1], bu[1], cosT, ALU.mult)
            then(V.tensor_tensor(bu[0], bu[0], sinT, ALU.mult))
            then(V.tensor_tensor(rot[1], rot[1], bu[0], ALU.subtract))
            for part in range(2):
                for ii in range(4):
                    m = V.tensor_tensor_scan(bu[part][:, ii], v(MAG)[:, 4 * t + ii:4 * t + ii + 1].to_broadcast([P, S]),
                                             rot[part][:, ii], 0.0, ALU.mult, ALU.add)
            then(m)
            V.tensor_tensor(rot[0], bu[0], cosT, ALU.mult)
            then(V.tensor_tensor(rot[1], bu[1], sinT, ALU.mult))
            then(V.tensor_tensor(rot[0], rot[0], rot[1], ALU.subtract))
            V.tensor_tensor(rot[1], bu[0], sinT, ALU.mult)
            then(V.tensor_tensor(bu[1], bu[1], cosT, ALU.mult))
            V.tensor_tensor(rot[1], rot[1], bu[1], ALU.add).then_inc(sem["s_x"], 1)
            dve.wait_ge(sem["s_turned"], t + 1)
            for part in range(2):
                m = V.tensor_tensor(span(52 + 2 * part, 0, 512).rearrange("p (h s) -> p h s", h=8),
                                    s5c[part][:, t:t + 1].to_broadcast([P, 8, S5_STATE]),
                                    C("s5c").unsqueeze(2).to_broadcast([P, 8, S5_STATE]), ALU.mult)
            m.then_inc(sem["s_cpad"], 1)
            dve.wait_ge(sem["s_y_psum"], t + 1)
            stt(T(12 + t), T(40 + t), vec("s5_d_2", t), PS[6][:, 0:S], ALU.mult, ALU.add).then_inc(sem["s_y"], 1)
        dve.wait_ge(sem["s_glu"], 1)
        then(V.tensor_tensor(T(12, 4), T(24, 4), T(28, 4), ALU.mult))
        then(V.memset(T(20, KT), 0.0))
        dve.sem_inc(sem["s_out"], 1)

        with dve.Fori(0, 4) as i:
            R, H = R_GATE + 5 * i, H_GATE + 4 * i
            for j in range(40):
                split(R, j + LEAD)
                if j == 1:
                    dve.wait_ge(sem["op_hi"], i + 1)
                    V.tensor_tensor(hid_lo[:, 0], arena[:, bass.ds(i * FT, FT), :], hid_hi[:, 0].bitcast(F32),
                                    ALU.subtract).then_inc(sem["hid_ready"], 1)
                if j % 10 == 9:
                    n = j // 10
                    dve.wait_ge(drained[0], H + (n + 2))
                    dve.wait_ge(sem["unit_done"], R * 8 + (j + 1))
                    for b in range(2):
                        m = V.tensor_tensor(T(36 + 2 * b, 2), halves(SETS[1][b][:]), T(36 + 2 * b, 2), ALU.mult)
                    m.then_inc(drained[1], 1)
                    dve.wait_ge(drained[1], H + (n + 2))
                    V.tensor_tensor(T(20 + FT * n, FT), T(20 + FT * n, FT), T(36, FT), ALU.add).then_inc(sem["sig_free"], 1)
                if j == 20:
                    modulation(2 * i + 8)
                if j < KT:
                    ada(2 * i + 8, j, 1)
                if 20 <= j < 20 + KT:
                    ada(2 * i + 9, j - 20, 1)
                if j == 38:
                    modulation(2 * i + 9)
        for k in range(0, KT, 4):
            dve.wait_ge(sem["merged_hi"], k // 4 + 1)
            V.tensor_tensor(hop_lo[:, k:k + 4], T(20 + k, 4), hop_hi[:, k:k + 4].bitcast(F32),
                            ALU.subtract).then_inc(sem["merged_ready"], 1)
        dve.wait_ge(sem["mod_ready"], 16)
        then(stt(gain7[:], mod[:, 4 * KT:5 * KT], 1.0, vec("norm_g_2", 2 * KT, KT), ALU.add, ALU.mult))
        then(V.tensor_tensor(gain8[:], mod[:, 5 * KT:6 * KT], vec("norm_g_2", 3 * KT, KT), ALU.mult))
        with dve.Fori(0, 2) as i:
            for j in range(2 * UA):
                split(R_OUT2 + 2 * i, j + LEAD)
        norm(6, of_arena(0), lambda k: gain6[:, k:k + 1])
        residual(6)
        dve.wait_ge(sem["res_ready"], 1)
        norm(7, of_x, lambda k: gain7[:, k:k + 1], bias=lambda k: mod[:, 3 * KT + k:3 * KT + k + 1])

        then(V.memset(T(0, KT), 0.0))

        def product(H):
            dve.wait_ge(drained[0], H + 2)
            for b in range(2):
                m = V.tensor_tensor(T(20 + 2 * b, 2), halves(SETS[1][b][:]), T(16 + 2 * b, 2), ALU.mult)
            m.then_inc(drained[1], 1)

        base = MLP_SUPER
        for j in range(2 * UA):
            split(R_FFN, j + LEAD)
        dve.wait_ge(sem["unit_done"], R_FFN * 8 + 2 * UA)
        product(H_FFN)
        hidden_lo(0, base + 1, 20)
        with dve.Fori(0, FFN_SUPER // 2) as i:
            R, H = R_FFN + 2 + 6 * i, H_FFN + 1 + 6 * i
            for j in range(6 * UA):
                split(R, j + LEAD)
                par = j // 24
                if j % 24 == 15:
                    dve.wait_ge(sem["unit_done"], R * 8 + (j + 1))
                    product(H + 3 * par)
                if j % 24 == 17:
                    hidden_lo(1 - par, 2 * i + (base + par + 2), 20)
                down_ends(R, j, 24 * par + 16, 0, arena)
        R = R_FFN + 2 + 3 * (FFN_SUPER - 1)
        for j in range(UA):
            if j < UA - LEAD:
                split(R, j + LEAD)
            down_ends(R, j, 0, 0, arena)
        dve.wait_ge(drained[0], R_END_H + 1)
        dve.wait_ge(drained[1], R_END_H + 1)
        norm(8, of_arena(0), lambda k: gain8[:, k:k + 1])
        residual(8)

    @block.gpsimd
    def _(pool):
        G = nc.gpsimd
        steps = [0]

        def then(ins):
            steps[0] += 1
            ins.then_inc(sem["pool_chain"], 1)
            pool.wait_ge(sem["pool_chain"], steps[0])

        def small(o, i):
            pool.dma_start(o, i).then_inc(sem["small_in"], 16)

        pool.wait_ge(sem["table_clear"], 1)
        small(bias_all[64:64 + N_BUCKETS, :], a["rel_bias_2"])
        small(lam, a["diff_lambda_2"][0].partition_broadcast(P))
        with nc.allow_non_contiguous_dma(reason="a few words"):
            small(gate_b[:], a["ml_gate_b_2"][0].rearrange("w h -> h w"))
            log_dt = a["s5_log_dt_2"]
            for half in range(2):
                small(s5v[64 * half:64 * half + 64, 15, :],
                      bass.AP(log_dt.tensor, log_dt.offset + half, [[0, S5_STATE], [2, 16], [1, 1]]).rearrange("p a b -> p (a b)"))
        small(wa2, a["gla_wa2_2"][0])
        for o, name in ((s5b[0], "s5_b_re_2"), (s5b[1], "s5_b_im_2")):
            small(o[:], a[name][0].rearrange("(i h) s c -> (h s) i c", h=2))
        for o, name in ((s5c[0], "s5_c_re_2"), (s5c[1], "s5_c_im_2")):
            small(o[:], a[name][0].rearrange("(t g) c s -> (g c) t s", t=4))
        pool.wait_ge(sem["bias_copied"], 1)
        pool.dma_start(bias_scratch[:].rearrange("h p j -> p h j"),
                       span(32, 0, BR_HEADS * 384).rearrange("p (h j) -> p h j", h=BR_HEADS)).then_inc(sem["bias_out"], 16)
        pool.wait_ge(sem["bias_out"], 16)
        pool.dma_start(T(32, 8), a["pool_w"][0].rearrange("g (c p) f -> p (g c) f", p=P)).then_inc(sem["pool_w_in"], 16)

        pad = POOL_PAD
        bufs = [span(40 + 3 * i, 0, 2 * (pad + S)).rearrange("p (a b) -> p a b", a=2) for i in range(2)]
        head = span(54, 0, 2 * pad).rearrange("p (a b) -> p a b", a=2)
        for b in bufs:
            then(G.memset(b, 0.0))
        for s in range(2):
            pool.wait_ge(drained[s], H_OUT + 1)
        for g, w in enumerate(POOL_WINDOWS):
            u = T(2 * g, 2)
            cur = 0
            then(G.tensor_copy(bufs[0][:, :, pad:], u))
            lag = 1
            while lag < w:
                src, dst = bufs[cur], bufs[1 - cur]
                then(G.tensor_tensor(dst[:, :, pad:], src[:, :, pad:], src[:, :, pad - lag:pad + S - lag], ALU.add))
                cur, lag = 1 - cur, 2 * lag
            tail = bufs[cur]
            scale = C("poolfix", lo=g * pad, n=pad).unsqueeze(1).to_broadcast([P, 2, pad])
            then(G.tensor_tensor(head, tail[:, :, pad:2 * pad], scale, ALU.mult))
            then(G.tensor_tensor(head, head, u[:, :, 0:pad], ALU.subtract))
            then(G.tensor_scalar(tail[:, :, pad:], tail[:, :, pad:], 1.0 / w, None, ALU.mult))
            then(G.tensor_tensor(u, tail[:, :, pad:], u, ALU.subtract))
            then(G.tensor_copy(u[:, :, 0:pad], head))
            pool.sem_inc(sem["pooled"], 1)

        def ada_load(g, k, where, col, wait=True):
            if wait:
                pool.wait_ge(sem["ada_used"], g * KT + (k - ADA_RING + 1))
            slot = k % ADA_RING
            pool.dma_start(span(ADA_SLOTS[where], slot * ADA_COLS, ADA_COLS),
                           ada_w[k, :, bass.ds(col, ADA_COLS)]).then_inc(ada_landed[slot], 16)

        pool.wait_ge(sem["hop_ready"], before(3, "hop"))
        for k in range(KT):
            ada_load(0, k, 0, 0, wait=k >= ADA_RING)
        with pool.Fori(1, 8) as g:
            col = pool.snap(g * ADA_COLS)
            for k in range(KT):
                ada_load(g, k, 0, col)
        pool.wait_ge(sem["mod_ready"], 8)
        tensor = bias_scratch
        at = [[383, P], [P * 384, BR_HEADS]]
        bias = span(44, 0, BR_HEADS * CW).rearrange("p (h j) -> p h j", h=BR_HEADS)
        pool.dma_start(bias[:, :, 0:P], bass.AP(tensor, P - 1 + P, at + [[1, P]])).then_inc(sem["bias_in"], 16)
        pool.dma_start(bias[:, :, P:CW], bass.AP(tensor, P - 1, at + [[1, S]])).then_inc(sem["bias_in"], 16)
        pool.wait_ge(sem["s_x"], 4)
        pool.dma_start(flat(T(16, 8)).rearrange("p (k n) -> p k n", k=4),
                       a["s5_glu_w_2"][0].rearrange("(k p) n -> p k n", p=P)).then_inc(sem["glu_w_in"], 16)
        pool.wait_ge(sem["s_out"], 1)
        with pool.Fori(8, 16) as g:
            col = pool.snap(g * ADA_COLS)
            for k in range(KT):
                ada_load(g, k, 1, col)
    ctx.close()


INPUTS = """x norm_mix_g w_in pool_w pool_scale pool_out_norm_g attn_out_norm_g w_out norm_mlp_g w_up w_down norm_final_g
c_2 ada_w_2 ada_b_2 norm_g_2 w_in_2 rel_bias_2 diff_lambda_2 ml_conv_2 ml_gate_b_2 gla_wa2_2 gla_ba_2 s5_a_re_2 s5_a_im_2
s5_log_dt_2 s5_b_re_2 s5_b_im_2 s5_c_re_2 s5_c_im_2 s5_d_2 s5_glu_w_2 s5_glu_b_2 w_branch_2 w_gate_2 b_gate_2 w_out_2
ffn_w_in_2 ffn_w_out_2""".split()


def kernel(**inputs):
    import concourse.bacc as bacc
    from concourse.bass_utils import run_bass_kernel_spmd

    nc = bacc.Bacc("TRN2", target_bir_lowering=False, num_devices=1)
    arrays, aps = {}, {}
    for name in INPUTS:
        v = np.ascontiguousarray(inputs[name])
        arrays[f"in_{name}"] = v
        aps[name] = nc.dram_tensor(f"in_{name}", v.shape, mybir.dt.from_np(v.dtype), kind="ExternalInput").ap()
    arrays["in_constants"] = shape_constants()
    consts = nc.dram_tensor("in_constants", arrays["in_constants"].shape, F32, kind="ExternalInput").ap()
    out = nc.dram_tensor("out_0", (1, S, D), F32, kind="ExternalOutput").ap()
    two_blocks(nc, aps, consts, out)
    r = run_bass_kernel_spmd(nc, [arrays], core_ids=[0])
    return r.results[0]["out_0"]
```

```python
from contextlib import ExitStack

import numpy as np
import concourse.bass as bass
from concourse import mybir

F32 = mybir.dt.float32
F32R = mybir.dt.float32r
ALU = mybir.AluOpType
ACT = mybir.ActivationFunctionType
AX_X = mybir.AxisListType.X

P = 128
S = 256
D = 2048
KT = D // P
TT = S // P
EPS = 1e-6
NEG = -1e30

UK = 2
COLS = 512
FT = COLS // P
RAW = 4
LEAD = 4
UA = KT // UK
UB = FT // UK
D_FF = 4 * D
FFN = 5632
MLP_SUPER = D_FF // COLS
FFN_SUPER = FFN // COLS
R_IN, R_OUT, R_MLP, R_IN2, R_GATE, R_OUT2, R_FFN = 0, 8, 12, 44, 56, 76, 80
H_IN, H_OUT, H_MLP, H_IN2, H_GATE, H_OUT2, H_FFN = 0, 4, 6, 46, 52, 68, 70
R_END_H = H_FFN + 3 * FFN_SUPER

POOL_WINDOWS = (2, 4, 8, 16)
POOL_PAD = max(POOL_WINDOWS)
HEADS = 8
DILATED_PATTERNS = ((128, 1), (512, 4), (2048, 16))
A_SCALE = float(P) ** -0.5

BR_HEADS = 4
DA_DIM = 64
DA_SCALE = float(DA_DIM) ** -0.5
N_BUCKETS, MAX_DISTANCE = 32, 128
LAM_INIT = 0.8 - 0.6 * float(np.exp(-0.3 * 0))
ML_SCALE = float(P) ** -0.5
GLA_DK = 64
GLA_SCALE = float(GLA_DK) ** -0.5
GLA_TAU = 16.0
GLA_RANK = 16
GLA_LEVELS = (64, 32, 16, 8, 4, 2, 1)
S5_STATE, S5_CH = 64, 16
ROUND = 1.5 * 2.0 ** 23
_two_pi = 2 * np.pi
_c1 = float(np.floor(_two_pi * 2 ** 8) / 2 ** 8)
_c2 = float(np.floor((_two_pi - _c1) * 2 ** 20) / 2 ** 20)
TWO_PI = (_c1, _c2, float(_two_pi - _c1 - _c2))
PI_BELOW = 3.1415925
N_SMALL = 10
COL_GATES, COL_GLA, COL_GLA_A, COL_S5 = 3584, 3592, 5128, 5144
ADA_COLS = 768
ADA_F = ADA_COLS // P
ADA_GROUPS = 6 * D // ADA_COLS
ADA_RING = 4
ADA_ACC, ADA_SLOTS = 56, 59
G_IN, G_OUT, G_MLP, G_IN2, G_GATE, G_OUT2 = 0, 2, 4, 12, 13, 15
ADA_AHEAD = 4
ADA_ONE = [j for j in range(24) if j % 3 != 2]
ADA_TAIL = [k + k // 4 for k in range(KT)]
ADA_TWO = [g * 16 + k * (12 - g) // 15 for g in range(2) for k in range(KT)]
ADA_GATE = [4 + k for k in range(2 * KT)]

CW = P + S

CONST = {}
_at = 0
for _n, _w in (("ident", P), ("dist", CW), ("count", CW), ("causal", P), ("levels", len(GLA_LEVELS) * P),
               ("poolfix", len(POOL_WINDOWS) * POOL_PAD), ("s5b", 32), ("s5c", 8), ("rowsel", BR_HEADS * P)):
    CONST[_n] = (_at, _w)
    _at += _w
CONST_COLS = _at

VEC_GROUPS = [
    [("norm_mix_g", 16), ("pool_scale", 8), ("pool_out_norm_g", 8), ("attn_out_norm_g", 8), ("norm_mlp_g", 16),
     ("norm_final_g", 16), ("c_2", 16), ("gla_ba_2", 2), ("s5_d_2", 4), ("s5_glu_b_2", 4), ("s5_a_re_2", 16)],
    [("norm_g_2", 64), ("b_gate_2", 64)],
    [("ada_b_2", 96), ("ml_conv_2", 32)],
    [("s5_a_im_2", 16)],
]
VEC = {}
for _g, _rows in enumerate(VEC_GROUPS):
    _r = 0
    for _n, _k in _rows:
        VEC[_n] = (_g, _r, _k)
        _r += _k
VEC_ROWS = [sum(k for _, k in rows) for rows in VEC_GROUPS]
N_VEC_DMAS = sum(len(rows) for rows in VEC_GROUPS)


def shape_constants():
    c = {n: np.zeros((P, w), np.float32) for n, (_, w) in CONST.items()}
    c["ident"][:] = np.eye(P)
    p = np.arange(P)[:, None]
    for qt, (at, keys) in enumerate(((0, P), (P, S))):
        d = qt * P + p - np.arange(keys)[None, :]
        n = np.zeros(d.shape)
        for window, dil in DILATED_PATTERNS:
            n += (d >= 0) & (d <= window) & (d % dil == 0)
        c["count"][:, at:at + keys] = n
        c["dist"][:, at:at + keys] = np.where(n > 0, -d, NEG)
    j, t = np.arange(P)[:, None], np.arange(P)[None, :]
    for i, level in enumerate(GLA_LEVELS):
        c["levels"][:, i * P:(i + 1) * P] = ((t // level) % 2 == 1) & (j // level == t // level - 1)
    c["causal"][:] = np.where(j >= t, 0.0, NEG)
    for g, w in enumerate(POOL_WINDOWS):
        c["poolfix"][:, g * POOL_PAD:(g + 1) * POOL_PAD] = 1.0 / np.minimum(np.arange(POOL_PAD) + 1, w)
    for ii in range(4):
        for g in range(8):
            c["s5b"][:, ii * 8 + g] = (g == 2 * ii + np.arange(P) // S5_STATE)
    for g in range(8):
        c["s5c"][:, g] = np.arange(P) // S5_CH == g
    for h in range(BR_HEADS):
        c["rowsel"][h, h * P:(h + 1) * P] = 1.0
    n = S - 1 - np.arange(384)
    exact = N_BUCKETS // 2
    large = exact + (np.log(np.maximum(n, 1) / exact) / np.log(MAX_DISTANCE / exact) * (N_BUCKETS - exact)).astype(int)
    bucket = np.where(n < exact, n, np.minimum(large, N_BUCKETS - 1))
    for i in range(384):
        if n[i] >= 0:
            c["rowsel"][64 + bucket[i], i] = 1.0
        else:
            c["rowsel"][64 + N_BUCKETS, i] = NEG
    return np.concatenate([c[n] for n in CONST], axis=1)


SEMS = """const_in x_in vec_in small_in x_turned x_copied vec_turned vecs_ready cs_ready
lam_sums lam_exps bias_rows_ready bias_psum bias_copied bias_out bias_in
hi_ready lo_ready unit_done drained0 drained1
sq_ready sum_ready var_ready std_ready normed hop_hi hop_ready
pool_w_in pooled pool_psum pool_ready
a_scores a_masked a_negmax a_exp a_probs a_probsT_psum a_probsT a_vT_psum a_vT a_out_psum a_out
relu_sq hid_hi hid_ready
ada_used mod_psum mod_ready
small_w_in gates_ready
d_scores d_masked d_negmax d_exp d_probs d_probsT_psum d_probsT d_vT_psum d_vT d_out_psum d_out branch_ready
hn_sq hn_sum hn_var hn_std
m_conv m_silu m_absz m_log m_rows m_bc m_BT m_qk m_vT_psum m_vT m_A m_E m_S m_ST_psum m_ST m_out_psum m_out m_sig
g_z_psum g_z g_absz g_log g_arg g_exp g_qk g_att_psum g_att_read g_vT_psum g_vT g_att g_x g_x_copied g_out_psum g_out g_sig
s_dt s_exp s_trig s_sin s_pow s_table s_pad s_turned s_BT s_bu_psum s_bu s_x s_cpad s_cturned s_CT s_y_psum s_y s_z s_glu_psum s_glu
glu_w_in table_clear x_parked x_back
op_hi gated sig_free merged_hi merged_ready
res_ready out_psum out_copied stored
act_chain dve_chain pool_chain""".split()


def two_blocks(nc, a, consts, out):
    ctx = ExitStack()

    def sb(name, shape, dt=F32):
        return ctx.enter_context(nc.sbuf_tensor(name, shape, dt))

    sem = {n: ctx.enter_context(nc.semaphore(n)) for n in SEMS}
    raw_landed = [ctx.enter_context(nc.semaphore(f"raw_landed{i}")) for i in range(RAW)]
    ada_landed = [ctx.enter_context(nc.semaphore(f"ada_landed{i}")) for i in range(ADA_RING)]
    drained = [sem["drained0"], sem["drained1"]]

    const = sb("const", [P, CONST_COLS])
    vecs = sb("vecs", [P, (len(VEC_GROUPS) - 1) * P + VEC_ROWS[-1]])
    x = sb("x", [P, KT, S])
    hop_hi = sb("hop_hi_part", [P, KT, S], F32R)
    hop_lo = sb("hop_lo_part", [P, KT, S], F32R)
    hid_hi = sb("hid_hi_part", [P, 2, FT, S], F32R)
    hid_lo = sb("hid_lo_part", [P, 2, FT, S], F32R)
    w_raw = sb("w_raw", [P, RAW, UK, COLS])
    w_hi = sb("w_hi", [P, LEAD, UK, COLS], F32R)
    w_lo = sb("w_lo", [P, LEAD, UK, COLS], F32R)
    NT = 72
    arena = sb("arena", [P, NT, S])
    ones = sb("ones", [P, P])
    var, std, rstd = (sb(n, [P, S]) for n in ("var", "std", "rstd"))
    fix = std
    cs = sb("cs", [P, KT])
    mod = sb("mod", [P, 6 * KT])
    gain5, gain6, gain7, gain8 = (sb(n, [P, KT]) for n in ("gain5", "gain6", "gain7", "gain8"))
    st = sb("st", [P, 2, 16])
    lam = arena[:, 52, :].rearrange("p (a b) -> p a b", a=4)
    lam_prod = arena[:, 53, 0:2 * DA_DIM].rearrange("p (a b) -> p a b", a=2)
    lam_s = sb("lam_s", [P, 8])
    bias_all = sb("bias_table", [P, BR_HEADS])
    BROWS = slice(64, 64 + N_BUCKETS + 1)
    bias_table = bias_all[BROWS, :]
    gate_b = sb("gate_b", [BR_HEADS, 2])
    row_store = sb("row_store", [P, 2, S])
    gate_rows = row_store[0:BR_HEADS]
    gla_a, wa2 = (row_store[64:64 + GLA_RANK, i, :] for i in range(2))
    BT = sb("BT", [P, TT, BR_HEADS])
    gate_bias = sb("gate_bias", [P, KT])
    s5b = [sb(n, [P, 16, S5_CH]) for n in ("s5b_re", "s5b_im")]
    s5c = [sb(n, [P, 4, S5_STATE]) for n in ("s5c_re", "s5c_im")]
    s5v = sb("s5v", [P, 16, 16])
    s5pow = [std[:, i * P:(i + 1) * P].rearrange("p (l i) -> p l i", l=8) for i in range(2)]
    x_scratch = nc.dram_tensor("x_scratch", [P, KT, S], F32, kind="Internal")
    bias_scratch = nc.dram_tensor("bias_scratch", [BR_HEADS, P, 384], F32, kind="Internal")

    PS = [ctx.enter_context(nc.psum_tensor(f"ps{i}", [P, 512], F32)) for i in range(8)]
    SETS = [(PS[0], PS[1]), (PS[2], PS[3])]

    def C(name, rows=P, lo=0, n=None):
        at, w = CONST[name]
        return const[0:rows, at + lo:at + (w if n is None else lo + n)]

    def vec(name, i=0, n=1):
        g, r, k = VEC[name]
        return vecs[:, g * P + r + i:g * P + r + i + n]

    def T(t, n=None):
        return arena[:, t, :] if n is None else arena[:, t:t + n, :]

    def flat(ap):
        return ap.rearrange("p a b -> p (a b)")

    ident = C("ident")

    def merged(n):
        return x[:, FT * n:FT * n + FT]

    def rotation(t):
        return T((16, 58)[t % 2], 4), T((20, 62)[t % 2], 4)

    def turned_level(n):
        return (GLA_LEVELS + (0, P))[n]

    GLA_STEPS = len(GLA_LEVELS) + 2

    def span(t, off, n):
        return arena[:, :, :].rearrange("p a b -> p (a b)")[:, t * S + off:t * S + off + n]

    def units(w):
        return w.rearrange("(q k p) n -> q p k n", p=P, k=UK)

    w_in, w_out, w_up, w_down = (units(a[n][0]) for n in ("w_in", "w_out", "w_up", "w_down"))
    w_in2, w_out2, w_ffn_in, w_ffn_out = (units(a[n][0]) for n in ("w_in_2", "w_out_2", "ffn_w_in_2", "ffn_w_out_2"))
    w_gate = a["w_gate_2"][0].rearrange("i (q k p) n -> i q p k n", p=P, k=UK)
    w_branch = a["w_branch_2"][0].rearrange("i (q k p) n -> i q p k n", p=P, k=UK)
    ada_w = a["ada_w_2"][0].rearrange("(k p) n -> k p n", p=P)

    NORMS = [(16, 1), (8, 1), (8, 1), (16, 1), (16, 0), (16, 1), (16, 0), (16, 1), (16, 0)]

    def before(n, what):
        return sum({"sq": k // 4, "normed": k, "hop": k * split}[what] for k, split in NORMS[:n])

    NORM_SQ = [0, 16, 16, 0, 0, 0, 16, 0, 16]
    NORM_T = [16, 24, 24, 16, None, 16, 32, 16, 32]

    block = ctx.enter_context(nc.Block())

    @block.sync
    def _(sp):
        sp.dma_start(flat(T(32, 16)).rearrange("p (t d) -> p t d", t=TT),
                     a["x"][0].rearrange("(t p) d -> p t d", p=P)).then_inc(sem["x_in"], 16)
        sp.dma_start(const[:], consts).then_inc(sem["const_in"], 16)

        def load(R, j, src, cond=True):
            if cond:
                sp.wait_ge(sem["lo_ready"], R * 8 + (j - RAW + 1))
            sp.dma_start(w_raw[:, j % RAW], src).then_inc(raw_landed[j % RAW], 16)

        def ada(slots, j, g, col):
            for i, u in enumerate(slots):
                if u + ADA_AHEAD == j:
                    k = i % KT
                    more = (g if isinstance(g, int) else 1) + i // KT > 0 or k >= ADA_RING
                    if more:
                        sp.wait_ge(sem["ada_used"], (g + i // KT) * KT + (k - ADA_RING + 1))
                    sp.dma_start(span(ADA_SLOTS, (k % ADA_RING) * ADA_COLS, ADA_COLS),
                                 ada_w[k, :, col(i // KT)]).then_inc(ada_landed[k % ADA_RING], 16)

        def ada_cols(g):
            return lambda i: slice((g + i) * ADA_COLS, (g + i + 1) * ADA_COLS)

        for q in range(RAW):
            load(0, q, w_in[q, :, :, 0:COLS], cond=False)
        for g in range(2):
            for j in range(4 * UA):
                if g == 0 and j < RAW:
                    continue
                ada(ADA_ONE, j, G_IN + g, ada_cols(G_IN + g))
                c = 4 * g + j // UA
                load(R_IN + 4 * g, j, w_in[j % UA, :, :, c * COLS:(c + 1) * COLS])
        for j in range(4 * UA):
            ada(ADA_TWO, j, G_OUT, ada_cols(G_OUT))
            load(R_OUT, j, w_out[j % UA, :, :, (j // UA) * COLS:(j // UA + 1) * COLS])

        for q in range(UA):
            load(R_MLP, q, w_up[q, :, :, 0:COLS])
        with sp.Fori(0, MLP_SUPER // 2 - 1) as i:
            ada_col = sp.snap(i * ADA_COLS + G_MLP * ADA_COLS)
            cols = [sp.snap(i * (2 * COLS) + (1 + par) * COLS) for par in range(2)]
            rows = [sp.snap(i * (2 * UB) + k) for k in range(2 * UB)]
            for j in range(4 * UA):
                par, u = j // (2 * UA), j % (2 * UA)
                ada(ADA_ONE, j, i + G_MLP, lambda _: bass.ds(ada_col, ADA_COLS))
                if u < UA:
                    load(R_MLP + 1 + 4 * i, j, w_up[u, :, :, bass.ds(cols[par], COLS)])
                else:
                    n, k = (u - UA) // UB, (u - UA) % UB
                    load(R_MLP + 1 + 4 * i, j, w_down[bass.ds(rows[UB * par + k], 1), :, :, n * COLS:(n + 1) * COLS]
                         .rearrange("a p k n -> (a p) k n"))
        for j in range(3 * UA):
            g = G_MLP + MLP_SUPER // 2 - 1
            ada(ADA_TAIL, j, g, ada_cols(g))
            if j < UA:
                load(R_IN2 - 3, j, w_up[j, :, :, (MLP_SUPER - 1) * COLS:])
            else:
                c, n, k = MLP_SUPER - 3 + j // UA, j % UA // UB, j % UB
                load(R_IN2 - 3, j, w_down[UB * c + k, :, :, n * COLS:(n + 1) * COLS])

        for c in range(12):
            for q in range(UA):
                ada(ADA_ONE, UA * c + q, G_IN2, ada_cols(G_IN2))
                if c == 3:
                    sp.wait_ge(sem["lo_ready"], (R_IN2 + 3) * 8 + q - RAW + 1)
                    for at, col in ((0, COL_GATES), (32, COL_GATES + BR_HEADS)):
                        sp.dma_start(w_raw[:, q % RAW, :, at:at + BR_HEADS],
                                     w_in2[q, :, :, col:col + BR_HEADS]).then_inc(sem["small_w_in"], 16)
                    sp.dma_start(w_raw[:, q % RAW, :, 64:64 + GLA_RANK],
                                 w_in2[q, :, :, COL_GLA_A:COL_GLA_A + GLA_RANK]).then_inc(raw_landed[q % RAW], 16)
                else:
                    col = c * COLS if c < 3 else (c - 1) * COLS if c < 8 else COL_GLA + (c - 8) * COLS
                    col = COL_S5 if c == 11 else col
                    load(R_IN2 + c, q, w_in2[q, :, :, col:col + COLS])

        for i in range(4):
            for j in range(40):
                if i == 3:
                    ada(ADA_GATE, j, G_GATE, ada_cols(G_GATE))
                n, q = j // 10, j % 10
                w = w_gate[i, q] if q < UA else w_branch[i, q - UA]
                load(R_GATE + 5 * i, j, w[:, :, n * COLS:(n + 1) * COLS])
        for j in range(4 * UA):
            ada(ADA_ONE, j, G_OUT2, ada_cols(G_OUT2))
            load(R_OUT2, j, w_out2[j % UA, :, :, (j // UA) * COLS:(j // UA + 1) * COLS])

        for q in range(2 * UA):
            col = 0 if q < UA else FFN
            load(R_FFN, q, w_ffn_in[q % UA, :, :, col:col + COLS])
        with sp.Fori(0, FFN_SUPER - 1) as c:
            ca = sp.snap(c * COLS + COLS)
            cg = sp.snap(c * COLS + (FFN + COLS))
            rows = [sp.snap(c * UB + k) for k in range(UB)]
            for q in range(2 * UA):
                load(R_FFN + 2 + 3 * c, q, w_ffn_in[q % UA, :, :, bass.ds(ca if q < UA else cg, COLS)])
            for n in range(4):
                for k in range(UB):
                    load(R_FFN + 2 + 3 * c, 2 * UA + UB * n + k,
                         w_ffn_out[bass.ds(rows[k], 1), :, :, n * COLS:(n + 1) * COLS].rearrange("a p k n -> (a p) k n"))
        for n in range(4):
            for k in range(UB):
                load(R_FFN + 3 * FFN_SUPER - 1, UB * n + k, w_ffn_out[UB * (FFN_SUPER - 1) + k, :, :, n * COLS:(n + 1) * COLS])

        sp.wait_ge(sem["out_copied"], 8)
        sp.dma_start(out[0].rearrange("(t p) d -> p t d", p=P),
                     flat(T(0, 16)).rearrange("p (t d) -> p t d", t=TT)).then_inc(sem["stored"], 16)
        sp.wait_ge(sem["stored"], 16)

    @block.tensor
    def _(pe):
        def mm(o, w, r, start=True, stop=True):
            return nc.tensor.matmul(o, w, r, start=start, stop=stop, skip_group_check=True)

        def unit(R, j, s, hi, lo, k0, first, last, ftiles=FT):
            pe.wait_ge(sem["lo_ready"], R * 8 + (j + 1))
            slot = j % LEAD
            for f in range(ftiles):
                o = SETS[s][f // 2][:, (f % 2) * S:(f % 2 + 1) * S]
                cols = slice(f * P, (f + 1) * P)
                for k in range(UK):
                    mm(o, w_hi[:, slot, k, cols], hi[:, k0 + k], start=first and k == 0 and f % 2 == 0, stop=False)
                    mm(o, w_hi[:, slot, k, cols], lo[:, k0 + k], start=False, stop=False)
                    m = mm(o, w_lo[:, slot, k, cols], hi[:, k0 + k], start=False, stop=last and k == UK - 1)
            m.then_inc(sem["unit_done"], 1)

        def chunk(R, j0, H, s, hi=hop_hi, lo=hop_lo, nu=UA, ftiles=FT, ready=None, between=None):
            pe.wait_ge(drained[s], H + 1)
            for q in range(nu):
                if ready:
                    ready(q)
                unit(R, j0 + q, s, hi, lo, UK * q, q == 0, q == nu - 1, ftiles)
                if between:
                    between(j0 + q)

        def norm(n):
            tiles = NORMS[n][0]
            sq = T(NORM_SQ[n], tiles)
            for k in range(tiles):
                if k % 4 == 0:
                    pe.wait_ge(sem["sq_ready"], before(n, "sq") + k // 4 + 1)
                m = mm(PS[4][:, 0:S], ones[:], sq[:, k], start=k == 0, stop=k == tiles - 1)
            m.then_inc(sem["sum_ready"], 1)

        def normed(n):
            return lambda q: pe.wait_ge(sem["hop_ready"], before(n + 1, "hop") - KT + UK * (q + 1))

        def scores(o, q, k):
            mm(o[:, 0:P], q[:, 0:P], k[:, 0:P])
            return mm(o[:, P:CW], q[:, P:S], k[:, 0:S])

        def turn_probs(o, p):
            for b in range(3):
                m = nc.tensor.transpose(o[:, b * P:(b + 1) * P], p[:, b * P:(b + 1) * P], ident)
            return m

        def weighted_values(o, v, pt):
            mm(o[:, 0:S], v[:, 0:P], pt[:, 0:S], stop=False)
            return mm(o[:, P:S], v[:, P:S], pt[:, S:CW], start=False)

        def turn_pair(o, src):
            nc.tensor.transpose(o[:, 0:P], src[:, 0:P], ident)
            return nc.tensor.transpose(o[:, P:S], src[:, P:S], ident)

        pe.wait_ge(sem["const_in"], 16)
        pe.wait_ge(sem["vec_in"], 16 * N_VEC_DMAS)
        for g, rows in enumerate(VEC_ROWS):
            m = nc.tensor.transpose(PS[0][:, g * P:g * P + rows], span(48, g * P, P)[0:rows, :], ident[0:rows, 0:rows])
        m.then_inc(sem["vec_turned"], 1)
        pe.wait_ge(sem["x_in"], 16)
        for b in range(KT // 2):
            if b >= 4:
                pe.wait_ge(sem["x_copied"], b - 3)
            for k in range(2):
                for t in range(TT):
                    m = nc.tensor.transpose(PS[4 + b % 4][:, (k * TT + t) * P:(k * TT + t + 1) * P],
                                            span(32, t * D + (2 * b + k) * P, P), ident)
            m.then_inc(sem["x_turned"], 1)
        pe.wait_ge(sem["bias_rows_ready"], 1)
        pe.wait_ge(sem["vecs_ready"], 1)
        for h in range(BR_HEADS):
            m = mm(PS[h][:, 0:384], span(50, h * P, P)[BROWS, :], C("rowsel", n=384)[BROWS, :])
        m.then_inc(sem["bias_psum"], 1)
        pe.wait_ge(sem["x_copied"], 8)
        norm(0)
        pe.wait_ge(sem["bias_copied"], 1)

        def modulation(used):
            pe.wait_ge(sem["ada_used"], used)
            for f in range(ADA_F):
                m = mm(PS[7][:, f:f + 1], span(ADA_ACC, f * P, P), ones[:, 0:1])
            m.then_inc(sem["mod_psum"], 1)

        with pe.Fori(0, 2) as g:
            for c in range(4):
                chunk(R_IN + 4 * g, UA * c, H_IN + 2 * g + c // 2, c % 2, ready=normed(0) if c == 0 else None)
                if c == 2:
                    modulation((g + (G_IN + 1)) * KT)

        for s in range(2):
            pe.wait_ge(drained[s], H_OUT + 1)
        for h in range(HEADS + 1):
            if h < HEADS:
                if h >= 2:
                    pe.wait_ge(sem["a_masked"], h - 1)
                scores(PS[h % 2], T(8 + h), T(16 + h)).then_inc(sem["a_scores"], 1)
                if h >= 2:
                    pe.wait_ge(sem["a_vT"], h - 1)
                turn_pair(PS[2 + h % 2], T(24 + h)).then_inc(sem["a_vT_psum"], 1)
            if h >= 1:
                g = h - 1
                pe.wait_ge(sem["a_probs"], g + 1)
                if g >= 2:
                    pe.wait_ge(sem["a_probsT"], g - 1)
                turn_probs(PS[4 + g % 2], span(46, CW * (g % 2), CW)).then_inc(sem["a_probsT_psum"], 1)
                pe.wait_ge(sem["a_probsT"], g + 1)
                pe.wait_ge(sem["a_vT"], g + 1)
                pe.wait_ge(sem["mod_ready"], G_OUT)
                if g >= 2:
                    pe.wait_ge(sem["a_out"], g - 1)
                weighted_values(PS[6 + g % 2], T(24 + g), span(49, CW * (g % 2), CW)).then_inc(sem["a_out_psum"], 1)
        pe.wait_ge(sem["pool_w_in"], 16)
        pe.wait_ge(sem["a_masked"], HEADS)
        pe.wait_ge(sem["a_vT"], HEADS)
        pool_w = T(32, 8)
        for g in range(4):
            pe.wait_ge(sem["pooled"], g + 1)
            for f in range(2):
                for c in range(2):
                    m = mm(PS[g][:, f * S:(f + 1) * S], pool_w[:, 2 * g + c, f * P:(f + 1) * P], T(2 * g + c),
                           start=c == 0 and f == 0, stop=c == 1)
            m.then_inc(sem["pool_psum"], 1)
        pe.wait_ge(sem["a_out"], HEADS)
        pe.wait_ge(sem["a_probsT"], HEADS)
        norm(1)
        norm(2)
        for c in range(4):
            chunk(R_OUT, UA * c, H_OUT + c // 2, c % 2, ready=normed(2) if c == 0 else None)
            if c % 2 == 1:
                modulation((G_OUT + c // 2 + 1) * KT)

        for s in range(2):
            pe.wait_ge(drained[s], H_MLP + 1)
        norm(3)

        def down(R, j0, H, s0, par, ready):
            pe.wait_ge(sem["hid_ready"], ready)
            for n in range(4):
                s = (s0 + n) % 2
                chunk(R, j0 + UB * n, H + (s0 + n) // 2, s, hid_hi[:, par], hid_lo[:, par], UB)

        chunk(R_MLP, 0, H_MLP, 0, ready=normed(3))
        with pe.Fori(0, MLP_SUPER // 2 - 1) as i:
            R, H = R_MLP + 1 + 4 * i, H_MLP + 5 * i
            chunk(R, 0, H, 1)
            down(R, 8, H + 1, 0, 0, 2 * i + 1)
            chunk(R, 16, H + 3, 0)
            modulation((i + (G_MLP + 1)) * KT)
            down(R, 24, H + 3, 1, 1, 2 * i + 2)
        R, H = R_MLP + 29, H_MLP + 35
        chunk(R, 0, H, 1)
        down(R, 8, H + 1, 0, 0, MLP_SUPER - 1)
        down(R, 16, H + 3, 0, 1, MLP_SUPER)
        modulation((G_MLP + MLP_SUPER // 2) * KT)

        for s in range(2):
            pe.wait_ge(drained[s], H_IN2 + 1)
        norm(4)
        norm(5)
        for c in range(4):
            chunk(R_IN2, UA * c, H_IN2 + c // 2, c % 2, ftiles=1 if c == 3 else FT, ready=normed(5) if c == 0 else None)
        modulation((G_IN2 + 1) * KT)

        def attention_steps(h):
            def steps(u):
                q = u % UA
                if q == 0:
                    for c in range(2):
                        pe.wait_ge(drained[c], H_IN2 + 3 - c)
                    if h >= 1:
                        pe.wait_ge(sem["d_masked"], 2 * h)
                    for m in range(2):
                        scores(PS[4 + m], T(h)[64 * m:64 * m + 64], T(4 + h)[64 * m:64 * m + 64]).then_inc(sem["d_scores"], 1)
                    if h >= 1:
                        pe.wait_ge(sem["d_out"], h)
                    turn_pair(PS[6][:, 0:S], T(8 + h)).then_inc(sem["d_vT_psum"], 1)
                if q == 3 and h == 3:
                    pe.wait_ge(sem["m_rows"], 1)
                    pe.wait_ge(sem["d_probsT"], h)
                    for t in range(TT):
                        m = mm(PS[7][:, CW + t * BR_HEADS:CW + (t + 1) * BR_HEADS], span(43, t * P, P)[0:BR_HEADS, :],
                               ident[0:BR_HEADS, 0:BR_HEADS])
                    m.then_inc(sem["m_BT"], 1)
                if q == 5:
                    if h == 0:
                        pe.wait_ge(sem["mod_ready"], G_IN2 + 1)
                    elif h < 3:
                        pe.wait_ge(sem["d_probsT"], h)
                    else:
                        pe.wait_ge(sem["m_rows"], 2)
                    pe.wait_ge(sem["d_probs"], h + 1)
                    turn_probs(PS[7], span(37, 0, CW)).then_inc(sem["d_probsT_psum"], 1)
                if q == 6:
                    pe.wait_ge(sem["d_probsT"], h + 1)
                    pe.wait_ge(sem["d_vT"], h + 1)
                    if h >= 1:
                        pe.wait_ge(sem["d_out"], h)
                    weighted_values(PS[6][:, S:2 * S], T(8 + h), span(37, CW, CW)).then_inc(sem["d_out_psum"], 1)
            return steps

        for h in range(BR_HEADS):
            c = 4 + h
            chunk(R_IN2, UA * c, H_IN2 + c // 2, c % 2, between=attention_steps(h))

        def head_norm(n):
            pe.wait_ge(sem["hn_sq"], n + 1)
            for b in range(2):
                m = mm(PS[6 + b][:, :], ones[:], flat(T((34, 44)[n] + 2 * b, 2)))
            m.then_inc(sem["hn_sum"], 1)

        def mlstm_steps(h):
            def steps(u):
                q = u % UA
                if h == 0 and q == 0:
                    head_norm(0)
                if h == 0 and q == 1:
                    pe.wait_ge(sem["d_masked"], 2 * BR_HEADS)
                    for t in range(2):
                        m = mm(PS[4][:, t * S:(t + 1) * S], wa2[:, t * P:(t + 1) * P], gla_a, start=t == 0)
                    m.then_inc(sem["g_z_psum"], 1)
                if q == 2:
                    if h == 0:
                        pe.wait_ge(sem["g_z"], 1)
                        pe.wait_ge(sem["hn_var"], 1)
                        pe.wait_ge(sem["m_silu"], 1)
                    else:
                        pe.wait_ge(sem["m_A"], h)
                        pe.wait_ge(sem["m_S"], h)
                        pe.wait_ge(sem["m_out"], h)
                    mm(PS[4][:, 0:S], C("rowsel", BR_HEADS, h * P, P), T(40)[0:BR_HEADS, :]).then_inc(sem["m_bc"], 1)
                    scores(PS[5], T(44 + h), T(48 + h)).then_inc(sem["m_qk"], 1)
                    turn_pair(PS[6][:, 0:S], T(20 + h)).then_inc(sem["m_vT_psum"], 1)
                if q == 6:
                    pe.wait_ge(sem["m_S"], h + 1)
                    if h >= 1:
                        pe.wait_ge(sem["m_ST"], h)
                    turn_probs(PS[7], span(52, 0, CW)).then_inc(sem["m_ST_psum"], 1)
                if q == 7:
                    pe.wait_ge(sem["m_ST"], h + 1)
                    pe.wait_ge(sem["m_vT"], h + 1)
                    if h >= 1:
                        pe.wait_ge(sem["m_out"], h)
                    weighted_values(PS[6][:, S:2 * S], T(20 + h), span(52, CW, CW)).then_inc(sem["m_out_psum"], 1)
            return steps

        for h in range(BR_HEADS):
            c = 8 + h
            chunk(R_IN2, UA * c, H_IN2 + c // 2, c % 2, between=mlstm_steps(h))

        def gla_steps(u):
            if u == 0:
                pe.wait_ge(sem["m_out"], BR_HEADS)
                pe.wait_ge(sem["m_ST"], BR_HEADS)
                for h in range(BR_HEADS):
                    m = turn_pair(PS[6 + h // 2][:, (h % 2) * S:(h % 2 + 1) * S], T(32 + h))
                m.then_inc(sem["g_vT_psum"], 1)
            if u % 4 == 1 and u // 4 < GLA_STEPS:
                n = u // 4
                level = turned_level(n)
                if level:
                    pe.wait_ge(sem["g_qk"], n + 1 if level < P else GLA_STEPS - 1)
                if n >= 1:
                    pe.wait_ge(sem["g_att_read"], n)
                q0, k0 = (28, 30) if level == 0 else (44, 46)
                for h in range(BR_HEADS):
                    rows = slice(64 * (h % 2), 64 * (h % 2) + 64)
                    q, k = T(q0 + h // 2)[rows], T(k0 + h // 2)[rows]
                    o = PS[4 + h % 2]
                    if level == P:
                        m = mm(o[:, (h // 2) * P:(h // 2 + 1) * P], k[:, 0:P], q[:, P:S])
                    else:
                        for t in range(TT):
                            m = mm(o[:, (h // 2) * S + t * P:(h // 2) * S + (t + 1) * P],
                                   k[:, t * P:(t + 1) * P], q[:, t * P:(t + 1) * P])
                m.then_inc(sem["g_att_psum"], 1)
            if u == 36:
                pe.wait_ge(sem["g_att"], 1)
                pe.wait_ge(sem["g_x_copied"], 1)
                pe.wait_ge(sem["g_vT"], 1)
                for h in range(BR_HEADS):
                    o = PS[6 + h // 2][:, (h % 2) * S:(h % 2 + 1) * S]
                    att = span(48 + 2 * (h % 2), (h // 2) * S, S)
                    v = T(32 + h)
                    mm(o[:, 0:P], v[:, 0:P], att[:, 0:P], start=h % 2 == 0)
                    mm(o[:, P:S], v[:, 0:P], span(54, h * P, P), start=False, stop=False)
                    m = mm(o[:, P:S], v[:, P:S], att[:, P:S], start=False)
                m.then_inc(sem["g_out_psum"], 1)
            if u == 38:
                head_norm(1)

        def s5_steps(t, u):
            if u == 1:
                pe.wait_ge(sem["s_pad"], t + 1)
                if t == 0:
                    pe.wait_ge(sem["g_x_copied"], 1)
                else:
                    pe.wait_ge(sem["s_CT"], t)
                for part in range(2):
                    for ii in range(4):
                        m = nc.tensor.transpose(PS[4 + part][:, ii * P:(ii + 1) * P], span(52 + 2 * part, ii * P, P), ident)
                m.then_inc(sem["s_turned"], 1)
            if u == 3:
                pe.wait_ge(sem["s_BT"], t + 1)
                if t == 0:
                    pe.wait_ge(sem["hn_var"], 2)
                else:
                    pe.wait_ge(sem["s_y"], t)
                for part in range(2):
                    for ii in range(4):
                        m = mm(PS[6 - 2 * part + ii // 2][:, (ii % 2) * S:(ii % 2 + 1) * S], span(44 + 2 * part, ii * P, P),
                               T(40 + t), start=ii % 2 == 0)
                m.then_inc(sem["s_bu_psum"], 1)
            if u == 6:
                pe.wait_ge(sem["s_cpad"], t + 1)
                pe.wait_ge(sem["s_bu"], t + 1)
                for part in range(2):
                    for ii in range(4):
                        m = nc.tensor.transpose(PS[4 + part][:, ii * P:(ii + 1) * P], span(66 + 2 * part, ii * P, P), ident)
                m.then_inc(sem["s_cturned"], 1)
            if u == 18:
                pe.wait_ge(sem["s_CT"], t + 1)
                pe.wait_ge(sem["s_x"], t + 1)
                for part in range(2):
                    for ii in range(4):
                        m = mm(PS[6][:, 0:S], span(48 + 2 * part, ii * P, P), T(32 + 4 * part + ii),
                               start=part == 0 and ii == 0, stop=part == 1 and ii == 3)
                m.then_inc(sem["s_y_psum"], 1)

        def last_steps(u):
            if u == 1:
                pe.wait_ge(sem["s_z"], 1)
                pe.wait_ge(sem["glu_w_in"], 16)
                glu = flat(T(16, 8)).rearrange("p (k n) -> p k n", k=4)
                for f in range(4):
                    for k in range(4):
                        m = mm(PS[4 + f // 2][:, (f % 2) * S:(f % 2 + 1) * S], glu[:, k, f * P:(f + 1) * P], T(24 + k),
                               start=f % 2 == 0 and k == 0, stop=k == 3)
                m.then_inc(sem["s_glu_psum"], 1)
            for g in range(2):
                if u == ADA_GATE[KT * g + KT - 1] + 1:
                    modulation((G_GATE + g + 1) * KT)

        for i in range(4):
            R, H = R_GATE + 5 * i, H_GATE + 4 * i
            steps = (gla_steps, lambda u: s5_steps(u // 20, u % 20), lambda u: s5_steps(2 + u // 20, u % 20), last_steps)[i]
            for n in range(4):
                chunk(R, 10 * n, H + n, 0, between=steps)
                if n == 0:
                    pe.wait_ge(sem["hid_ready"], i + (MLP_SUPER + 1))
                chunk(R, 10 * n + UA, H + n, 1, hid_hi[:, 0], hid_lo[:, 0], UB, between=steps)

        def merged_split(q):
            pe.wait_ge(sem["merged_ready"], q // 2 + 1)

        for c in range(4):
            chunk(R_OUT2, UA * c, H_OUT2 + c // 2, c % 2, ready=merged_split if c == 0 else None)
            if c == 2:
                modulation((G_OUT2 + 1) * KT)
        norm(6)
        norm(7)

        base = MLP_SUPER + 4
        for s in range(2):
            chunk(R_FFN, UA * s, H_FFN, s, ready=normed(7) if s == 0 else None)
        with pe.Fori(0, FFN_SUPER // 2) as i:
            R, H = R_FFN + 2 + 6 * i, H_FFN + 1 + 6 * i
            for par in range(2):
                for s in range(2):
                    chunk(R, 24 * par + UA * s, H + 3 * par, s)
                down(R, 24 * par + 16, H + 3 * par + 1, 0, par, 2 * i + (base + par + 1))
        R, H = R_FFN + 2 + 3 * (FFN_SUPER - 1), H_FFN + 1 + 3 * (FFN_SUPER - 1)
        down(R, 0, H, 0, (FFN_SUPER - 1) % 2, base + FFN_SUPER)
        norm(8)

        pe.wait_ge(sem["res_ready"], 2)
        for b in range(8):
            if b >= 4:
                pe.wait_ge(sem["out_copied"], b - 3)
            t, k0 = b // 4, 4 * (b % 4)
            for k in range(4):
                m = nc.tensor.transpose(PS[b % 4][:, k * P:(k + 1) * P], x[:, k0 + k, t * P:(t + 1) * P], ident)
            m.then_inc(sem["out_psum"], 1)

    @block.scalar
    def _(act):
        def copy(o, i, scale=1.0):
            return nc.scalar.activation(o, i, ACT.Copy, scale=scale)

        def split(R, j, first=False, cols=COLS):
            act.wait_ge(raw_landed[j % RAW], (R * (8 // RAW) + j // RAW) * 16 + 16)
            if not first:
                act.wait_ge(sem["unit_done"], R * 8 + (j - LEAD + 1))
            copy(w_hi[:, j % LEAD, :, 0:cols], w_raw[:, j % RAW, :, 0:cols]).then_inc(sem["hi_ready"], 1)

        def halves(ap):
            return ap.rearrange("p (a b) -> p a b", a=2)

        def store_chunk(s, tile):
            for b in range(2):
                m = copy(arena[:, tile(2 * b), :], halves(SETS[s][b][:]))
            m.then_inc(drained[s], 1)

        def norm(n, src, bias=None):
            tiles, is_split = NORMS[n]
            for k in range(0, tiles, 4):
                nc.scalar.activation(T(NORM_SQ[n] + k, 4), src(k, 4), ACT.Square).then_inc(sem["sq_ready"], 1)
            act.wait_ge(sem["var_ready"], n + 1)
            nc.scalar.activation(std[:], var[:], ACT.Sqrt).then_inc(sem["std_ready"], 1)
            if is_split:
                dst = 8 if n == 2 else 0
                for k in range(tiles):
                    act.wait_ge(sem["normed"], before(n, "normed") + k + 1)
                    t = T(NORM_T[n] + k)
                    if bias is None:
                        m = copy(hop_hi[:, dst + k], t)
                    else:
                        m = nc.scalar.activation(hop_hi[:, dst + k], t, ACT.Identity, bias=bias(k))
                    m.then_inc(sem["hop_hi"], 1)

        def of_x(k, n):
            return x[:, k:k + n]

        def of_arena(t):
            return lambda k, n: T(t + k, n)

        for g, rows in enumerate(VEC_GROUPS):
            for name, k in rows:
                v = a[name]
                v = v if len(v.shape) == 1 else v[0]
                names = "abc"[:len(v.shape)]
                if len(names) > 1:
                    v = v.rearrange(f"{' '.join(names)} -> ({' '.join(names)})")
                act.dma_start(span(48, g * P, P)[VEC[name][1]:VEC[name][1] + k, :],
                              v.rearrange("(r c) -> r c", c=P)).then_inc(sem["vec_in"], 16)
        act.wait_ge(sem["vec_turned"], 1)
        for g, rows in enumerate(VEC_ROWS):
            m = copy(vecs[:, g * P:g * P + rows], PS[0][:, g * P:g * P + rows])
        m.then_inc(sem["vecs_ready"], 1)
        for b in range(KT // 2):
            act.wait_ge(sem["x_turned"], b + 1)
            copy(x[:, 2 * b:2 * b + 2], halves(PS[4 + b % 4][:])).then_inc(sem["x_copied"], 1)
        act.wait_ge(sem["x_copied"], 8)
        act.wait_ge(sem["vecs_ready"], 1)
        act.wait_ge(sem["bias_psum"], 1)
        for h in range(BR_HEADS):
            m = copy(span(32, h * 384, 384), PS[h][:, 0:384])
        m.then_inc(sem["bias_copied"], 1)
        for j in range(LEAD):
            split(0, j, first=True)
        norm(0, of_x)
        nc.scalar.activation(cs[:], vec("c_2", 0, KT), ACT.Silu).then_inc(sem["cs_ready"], 1)
        act.wait_ge(sem["lam_sums"], 1)
        nc.scalar.activation(lam_s[:, 2:4], lam_s[:, 0:2], ACT.Exp).then_inc(sem["lam_exps"], 1)

        with act.Fori(0, 4) as i:
            for j in range(2 * UA):
                split(R_IN + 2 * i, j + LEAD)
                if j % UA == UA - 1:
                    store_chunk(j // UA, lambda o: bass.ds(i * 8 + (4 * (j // UA) + o), 2))

        for h in range(HEADS + 1):
            if h < HEADS:
                act.wait_ge(sem["a_vT_psum"], h + 1)
                copy(T(24 + h), PS[2 + h % 2][:, 0:S]).then_inc(sem["a_vT"], 1)
                act.wait_ge(sem["a_negmax"], h + 1)
                e = span(46, CW * (h % 2), CW)
                for qt, cols in enumerate((slice(0, P), slice(P, CW))):
                    m = nc.scalar.activation(e[:, cols], e[:, cols], ACT.Exp, scale=A_SCALE,
                                             bias=st[:, h % 2, 2 + qt:3 + qt])
                m.then_inc(sem["a_exp"], 1)
            if h >= 1:
                g = h - 1
                act.wait_ge(sem["a_probsT_psum"], g + 1)
                if g >= 2:
                    act.wait_ge(sem["a_out_psum"], g - 1)
                copy(span(49, CW * (g % 2), CW), PS[4 + g % 2][:, 0:CW]).then_inc(sem["a_probsT"], 1)
                act.wait_ge(sem["a_out_psum"], g + 1)
                copy(T(8 + g), PS[6 + g % 2][:, 0:S]).then_inc(sem["a_out"], 1)
        for g in range(4):
            act.wait_ge(sem["pool_psum"], g + 1)
            for f in range(2):
                m = nc.scalar.activation(T(2 * g + f), PS[g][:, f * S:(f + 1) * S], ACT.Copy,
                                         scale=vec("pool_scale", 2 * g + f))
            m.then_inc(sem["pool_ready"], 1)
        act.wait_ge(sem["pool_ready"], 4)
        act.wait_ge(sem["a_out"], HEADS)
        norm(1, of_arena(0))
        norm(2, of_arena(8))
        with act.Fori(0, 2) as i:
            for j in range(2 * UA):
                split(R_OUT + 2 * i, j + LEAD)

        act.wait_ge(drained[0], H_MLP + 1)
        act.wait_ge(drained[1], H_MLP + 1)
        norm(3, of_x)

        def relu(s):
            for b in range(2):
                m = nc.scalar.activation(T(2 * b, 2), halves(SETS[s][b][:]), ACT.Relu)
            m.then_inc(drained[s], 1)

        def hidden_hi(par, sig, count, tile):
            act.wait_ge(sig, count)
            copy(hid_hi[:, par], T(tile, FT)).then_inc(sem["hid_hi"], 1)

        for j in range(UA):
            split(R_MLP, j + LEAD)
        relu(0)
        hidden_hi(0, sem["relu_sq"], 1, 4)
        with act.Fori(0, MLP_SUPER // 2 - 1) as i:
            for j in range(4 * UA):
                split(R_MLP + 1 + 4 * i, j + LEAD)
                if j in (7, 23):
                    relu(1 if j == 7 else 0)
                if j in (8, 24):
                    hidden_hi(1 if j == 8 else 0, sem["relu_sq"], 2 * i + (2 if j == 8 else 3), 4)
        for j in range(3 * UA):
            split(R_MLP + 29, j + LEAD)
            if j == 7:
                relu(1)
            if j == 8:
                hidden_hi(1, sem["relu_sq"], MLP_SUPER, 4)

        act.wait_ge(drained[0], H_IN2 + 1)
        act.wait_ge(drained[1], H_IN2 + 1)
        norm(4, of_x)
        act.wait_ge(sem["normed"], before(5, "normed"))
        norm(5, of_x, lambda k: mod[:, k:k + 1])

        def narrow_wait(c, q):
            if (c, q) in ((3, 0), (3, RAW)):
                act.wait_ge(sem["small_w_in"], 16 * 2 * (q + RAW))

        def projection_unit(c, q):
            ahead = (UA * c + q + LEAD) // UA
            if ahead == 3:
                narrow_wait(ahead, (q + LEAD) % UA)
            split(R_IN2, UA * c + q + LEAD, cols=P if ahead == 3 else COLS)

        tiles_of = [0, 4, 8, None, 12, 16, 20, 24, 28, 32, 36, 40]
        DT, MAG, THR, SIN, HALF = 0, 1, 2, 3, 4
        for c in range(4):
            for q in range(UA):
                projection_unit(c, q)
                if (c, q) == (0, 1):
                    act.wait_ge(sem["small_in"], 16 * N_SMALL)
                    nc.scalar.activation(s5v[:, DT], s5v[:, 15], ACT.Exp).then_inc(sem["s_dt"], 1)
                if (c, q) == (0, 4):
                    act.wait_ge(sem["s_trig"], 1)
                    nc.scalar.activation(s5v[:, MAG], s5v[:, MAG], ACT.Exp).then_inc(sem["s_exp"], 1)
                    nc.scalar.activation(s5v[:, SIN], s5v[:, THR], ACT.Sin)
                    nc.scalar.activation(s5v[:, HALF], s5v[:, THR], ACT.Sin, scale=0.5).then_inc(sem["s_sin"], 1)
            if c < 3:
                store_chunk(c % 2, lambda o: slice(tiles_of[c] + o, tiles_of[c] + o + 2))
        narrow = SETS[1][0]
        copy(gate_rows[:, 0, :], narrow[0:BR_HEADS, 0:S])
        copy(gate_rows[:, 1, :], narrow[32:32 + BR_HEADS, 0:S])
        copy(gla_a, narrow[64:64 + GLA_RANK, 0:S]).then_inc(drained[1], 1)
        act.wait_ge(drained[1], H_IN2 + 3)
        act.sem_inc(sem["gates_ready"], 1)

        rows = BR_HEADS
        for h in range(BR_HEADS):
            c = 4 + h
            for q in range(UA):
                projection_unit(c, q)
                if q == 0:
                    act.wait_ge(sem["d_vT_psum"], h + 1)
                    copy(T(8 + h), PS[6][:, 0:S]).then_inc(sem["d_vT"], 1)
                if q in (1, 2):
                    m = q - 1
                    act.wait_ge(sem["d_negmax"], 2 * h + m + 1)
                    e = span(34, CW * m, CW)
                    for qt, cols in enumerate((slice(0, P), slice(P, CW))):
                        i = nc.scalar.activation(e[:, cols], e[:, cols], ACT.Exp, bias=st[:, 0, 2 * m + qt:2 * m + qt + 1],
                                                 accum_out=st[:, 1, 2 * m + qt:2 * m + qt + 1])
                    i.then_inc(sem["d_exp"], 1)
                if q == 4 and h == 3:
                    act.wait_ge(sem["m_BT"], 1)
                    copy(BT[:].rearrange("p a b -> p (a b)"), PS[7][:, CW:CW + TT * BR_HEADS]).then_inc(sem["m_rows"], 1)
                if q == 5:
                    act.wait_ge(sem["d_probsT_psum"], h + 1)
                    copy(span(37, CW, CW), PS[7][:, 0:CW]).then_inc(sem["d_probsT"], 1)
                if q == 6:
                    act.wait_ge(sem["d_out_psum"], h + 1)
                    copy(T(h), PS[6][:, S:2 * S]).then_inc(sem["d_out"], 1)
                if q == 7 and h == 0:
                    act.wait_ge(sem["m_absz"], 1)
                    nc.scalar.activation(T(42)[0:rows, :], T(42)[0:rows, :], ACT.Exp, scale=-1.0).then_inc(sem["act_chain"], 1)
                    act.wait_ge(sem["act_chain"], 1)
                    nc.scalar.activation(T(42)[0:rows, :], T(42)[0:rows, :], ACT.Ln, bias=1.0).then_inc(sem["m_log"], 1)
            store_chunk(c % 2, lambda o: slice(tiles_of[c] + o, tiles_of[c] + o + 2))
        act.wait_ge(sem["d_out"], BR_HEADS)

        def head_squares(src, sq):
            nc.scalar.activation(T(sq, 4), T(src, 4), ACT.Square).then_inc(sem["hn_sq"], 1)

        def head_root(n, sq):
            act.wait_ge(sem["hn_var"], n + 1)
            nc.scalar.activation(T(sq, 4), T(sq, 4), ACT.Sqrt).then_inc(sem["hn_std"], 1)

        head_squares(0, 34)

        for h in range(BR_HEADS):
            c = 8 + h
            for q in range(UA):
                projection_unit(c, q) if (c, q) < (11, LEAD) else split(R_GATE, UA * (c - 12) + q + LEAD)
                if h == 0 and q == 0:
                    act.wait_ge(sem["m_conv"], 1)
                    nc.scalar.activation(T(44, 8), T(44, 8), ACT.Silu).then_inc(sem["m_silu"], 1)
                    act.wait_ge(drained[1], H_IN2 + 5)
                    nc.scalar.activation(T(24, 4), T(24, 4), ACT.Sigmoid).then_inc(sem["m_sig"], 1)
                if h == 0 and q == 1:
                    head_root(0, 34)
                    act.wait_ge(sem["g_z_psum"], 1)
                    for t in range(2):
                        m = nc.scalar.activation(T(8 + t), PS[4][:, t * S:(t + 1) * S], ACT.Identity, bias=vec("gla_ba_2", t))
                    m.then_inc(sem["g_z"], 1)
                if q == 2:
                    act.wait_ge(sem["m_vT_psum"], h + 1)
                    copy(T(20 + h), PS[6][:, 0:S]).then_inc(sem["m_vT"], 1)
                if q == 3:
                    act.wait_ge(sem["m_A"], h + 1)
                    e = span(52, 0, CW)
                    nc.scalar.activation(st[:, 1, 0:2], st[:, 0, 4:6], ACT.Exp)
                    for qt, cols in enumerate((slice(0, P), slice(P, CW))):
                        m = nc.scalar.activation(e[:, cols], e[:, cols], ACT.Exp, bias=st[:, 0, 2 + qt:3 + qt])
                    m.then_inc(sem["m_E"], 1)
                if q == 6:
                    act.wait_ge(sem["m_ST_psum"], h + 1)
                    copy(span(52, CW, CW), PS[7][:, 0:CW]).then_inc(sem["m_ST"], 1)
                if h == 1 and q == 7:
                    act.wait_ge(sem["g_absz"], 1)
                    nc.scalar.activation(T(10, 2), T(10, 2), ACT.Exp, scale=-1.0).then_inc(sem["act_chain"], 1)
                    act.wait_ge(sem["act_chain"], 2)
                    nc.scalar.activation(T(10, 2), T(10, 2), ACT.Ln, bias=1.0).then_inc(sem["g_log"], 1)
            store_chunk(c % 2, lambda o: slice(tiles_of[c] + o, tiles_of[c] + o + 2))

        def gla_steps(u):
            if u == 0:
                act.wait_ge(sem["g_vT_psum"], 1)
                for b in range(2):
                    m = copy(T(32 + 2 * b, 2), halves(PS[6 + b][:]))
                m.then_inc(sem["g_vT"], 1)
            if u == 0 or u % 4 == 3 and u // 4 + 1 < GLA_STEPS and turned_level(u // 4 + 1):
                n = (u + 1) // 4
                act.wait_ge(sem["g_arg"], n + 1 if n < len(GLA_LEVELS) else GLA_STEPS - 1)
                nc.scalar.activation(T(12, 4), T(12, 4), ACT.Exp).then_inc(sem["g_exp"], 1)
            if u == 34:
                nc.scalar.activation(T(36, 4), T(36, 4), ACT.Silu).then_inc(sem["g_sig"], 1)
                act.wait_ge(sem["g_att_psum"], GLA_STEPS)
                x_att = span(54, 0, BR_HEADS * P).rearrange("p (a b c) -> p b a c", a=2, b=2)
                for par in range(2):
                    m = copy(x_att[:, par], halves(PS[4 + par][:, 0:2 * P]))
                m.then_inc(sem["g_x_copied"], 1)
            if u == 36:
                act.wait_ge(sem["hid_ready"], MLP_SUPER + 1)
                act.wait_ge(sem["g_out_psum"], 1)
                for b in range(2):
                    m = copy(T(2 * b, 2), halves(PS[6 + b][:]), scale=GLA_SCALE)
                m.then_inc(sem["g_out"], 1)
                act.wait_ge(sem["g_out"], 1)
                head_squares(0, 44)
            if u == 38:
                head_root(1, 44)

        def s5_steps(t, u):
            if u == 1:
                if t == 0:
                    act.wait_ge(sem["branch_ready"], 2)
                act.wait_ge(sem["s_turned"], t + 1)
                for part in range(2):
                    m = copy(T(44 + 2 * part, 2), halves(PS[4 + part][:]))
                m.then_inc(sem["s_BT"], 1)
            if u == 3:
                if t >= 1:
                    act.wait_ge(sem["s_x"], t)
                act.wait_ge(sem["s_bu_psum"], t + 1)
                for b in range(4):
                    m = copy(T(24 + 2 * b, 2), halves(PS[(6, 7, 4, 5)[b]][:]))
                m.then_inc(sem["s_bu"], 1)
            if u == 6:
                act.wait_ge(sem["s_cturned"], t + 1)
                for part in range(2):
                    m = copy(T(48 + 2 * part, 2), halves(PS[4 + part][:]), scale=1.0 if part == 0 else -1.0)
                m.then_inc(sem["s_CT"], 1)

        def last_steps(u):
            if u == 0:
                act.wait_ge(sem["s_y"], 4)
                nc.scalar.activation(T(24, 4), T(40, 4), ACT.Gelu_apprx_tanh).then_inc(sem["s_z"], 1)
            if u == 1:
                act.wait_ge(sem["s_glu_psum"], 1)
                for f in range(4):
                    m = nc.scalar.activation(T(28 + f), PS[4 + f // 2][:, (f % 2) * S:(f % 2 + 1) * S], ACT.Sigmoid,
                                             bias=vec("s5_glu_b_2", f))
                m.then_inc(sem["s_glu"], 1)

        for i in range(4):
            source = (0, 4, 0, 24)[i]
            for j in range(40):
                split(R_GATE + 5 * i, j + LEAD)
                if j == (3 if i == 3 else 0):
                    act.wait_ge(sem["branch_ready"], (1, 1, 2, 3)[i])
                    if i == 1:
                        act.wait_ge(sem["m_out"], BR_HEADS)
                    copy(hid_hi[:, 0], T(source, FT)).then_inc(sem["op_hi"], 1)
                if j % 10 == 7:
                    n = j // 10
                    if i == 0:
                        act.wait_ge(sem["x_parked"], 16)
                        o = merged(n)
                    else:
                        if (i, n) == (1, 0):
                            act.wait_ge(sem["hid_ready"], MLP_SUPER + 2)
                        else:
                            act.wait_ge(sem["sig_free"], 4 * (i - 1) + n)
                        o = T(4, FT)
                    for f in range(FT):
                        m = nc.scalar.activation(o[:, f], SETS[0][f // 2][:, (f % 2) * S:(f % 2 + 1) * S],
                                                 ACT.Sigmoid, bias=vec("b_gate_2", i * KT + FT * n + f))
                    m.then_inc(drained[0], 1)
                (gla_steps, lambda u: s5_steps(u // 20, u % 20), lambda u: s5_steps(2 + u // 20, u % 20), last_steps)[i](j)
        for n in range(4):
            act.wait_ge(sem["sig_free"], 8 + n + 1)
            copy(hop_hi[:, FT * n:FT * n + FT], merged(n)).then_inc(sem["merged_hi"], 1)
        with act.Fori(0, 2) as i:
            for j in range(2 * UA):
                split(R_OUT2 + 2 * i, j + LEAD)
                if j % UA == UA - 1:
                    store_chunk(j // UA, lambda o: bass.ds(i * 8 + (4 * (j // UA) + o), 2))
        act.wait_ge(drained[0], H_FFN + 1)
        act.wait_ge(drained[1], H_FFN + 1)
        norm(6, of_arena(0))
        act.wait_ge(sem["res_ready"], 1)
        norm(7, of_x, lambda k: mod[:, 3 * KT + k:3 * KT + k + 1])

        def silu():
            for b in range(2):
                m = nc.scalar.activation(T(16 + 2 * b, 2), halves(SETS[0][b][:]), ACT.Silu)
            m.then_inc(drained[0], 1)

        for j in range(2 * UA):
            split(R_FFN, j + LEAD)
            if j == 7:
                silu()
        hidden_hi(0, drained[1], H_FFN + 2, 20)
        with act.Fori(0, FFN_SUPER // 2) as i:
            for j in range(6 * UA):
                split(R_FFN + 2 + 6 * i, j + LEAD)
                par = j // 24
                if j % 24 == 7:
                    silu()
                if j % 24 == 16:
                    hidden_hi(1 - par, drained[1], 6 * i + (H_FFN + 1 + 3 * par + 2), 20)
        for j in range(UA - LEAD):
            split(R_FFN + 2 + 3 * (FFN_SUPER - 1), j + LEAD)
        act.wait_ge(drained[0], R_END_H + 1)
        act.wait_ge(drained[1], R_END_H + 1)
        norm(8, of_arena(0))
        for b in range(8):
            act.wait_ge(sem["out_psum"], b + 1)
            copy(span(0, b * 512, 512), PS[b % 4][:]).then_inc(sem["out_copied"], 1)

    @block.vector
    def _(dve):
        V = nc.vector
        steps = [0]

        def then(ins):
            steps[0] += 1
            ins.then_inc(sem["dve_chain"], 1)
            dve.wait_ge(sem["dve_chain"], steps[0])

        def stt(o, i0, scalar, i1, op0, op1, **k):
            return V.scalar_tensor_tensor(o, i0, scalar, i1, op0, op1, **k)

        def split(R, j, cols=COLS):
            dve.wait_ge(sem["hi_ready"], R * 8 + (j + 1))
            V.tensor_tensor(w_lo[:, j % LEAD, :, 0:cols], w_raw[:, j % RAW, :, 0:cols],
                            w_hi[:, j % LEAD, :, 0:cols].bitcast(F32), ALU.subtract).then_inc(sem["lo_ready"], 1)

        def halves(ap):
            return ap.rearrange("p (a b) -> p a b", a=2)

        def add_chunk(R, j, s, at, tile):
            dve.wait_ge(sem["unit_done"], R * 8 + (j + 1))
            for b in range(2):
                dst = at[:, tile(2 * b), :]
                m = V.tensor_tensor(dst, halves(SETS[s][b][:]), dst, ALU.add)
            m.then_inc(drained[s], 1)

        def norm(n, src, gain, bias=None, to=None):
            tiles, is_split = NORMS[n]
            dve.wait_ge(sem["sum_ready"], n + 1)
            V.tensor_scalar(var[:], PS[4][:, 0:S], 1.0 / (tiles * P), EPS, ALU.mult, ALU.add).then_inc(sem["var_ready"], 1)
            dve.wait_ge(sem["std_ready"], n + 1)
            then(V.reciprocal(rstd[:], std[:]))
            then(V.tensor_tensor(fix[:], rstd[:], rstd[:], ALU.mult))
            then(V.tensor_tensor(fix[:], fix[:], var[:], ALU.mult))
            then(V.tensor_scalar(fix[:], fix[:], -0.5, 1.5, ALU.mult, ALU.add))
            then(V.tensor_tensor(rstd[:], rstd[:], fix[:], ALU.mult))
            dst, lag = 8 if n == 2 else 0, 2
            for i in range(tiles + lag):
                if i < tiles:
                    o = to[:, i] if to is not None else T(NORM_T[n] + i)
                    stt(o, src(i), gain(i), rstd[:], ALU.mult, ALU.mult).then_inc(sem["normed"], 1)
                k = i - lag
                if is_split and k >= 0:
                    dve.wait_ge(sem["hop_hi"], before(n, "hop") + k + 1)
                    hi, t = hop_hi[:, dst + k].bitcast(F32), T(NORM_T[n] + k)
                    if bias is None:
                        m = V.tensor_tensor(hop_lo[:, dst + k], t, hi, ALU.subtract)
                    else:
                        m = stt(hop_lo[:, dst + k], t, bias(k), hi, ALU.add, ALU.subtract)
                    m.then_inc(sem["hop_ready"], 1)

        def residual(n):
            dve.wait_ge(sem["normed"], before(n + 1, "normed"))
            for k in range(0, KT, 4):
                m = V.tensor_tensor(x[:, k:k + 4], x[:, k:k + 4], T(NORM_T[n] + k, 4), ALU.add)
            m.then_inc(sem["res_ready"], 1)

        def of_x(k):
            return x[:, k]

        def of_arena(t):
            return lambda k: T(t + k)

        QT = (slice(0, P), slice(P, CW))

        V.memset(ones[:], 1.0)
        V.memset(bias_all[:], 1.0).then_inc(sem["dve_chain"], 1)
        steps[0] += 1
        dve.wait_ge(sem["dve_chain"], 1)
        dve.sem_inc(drained[0], 1)
        dve.sem_inc(drained[1], 1)
        dve.sem_inc(sem["table_clear"], 1)
        dve.wait_ge(sem["small_in"], 16 * N_SMALL)
        for h in range(BR_HEADS):
            m = V.tensor_scalar(span(50, h * P, P)[BROWS, :], ones[BROWS, :],
                                bias_table[:, h:h + 1], None, ALU.mult)
        m.then_inc(sem["bias_rows_ready"], 1)
        then(V.tensor_tensor(lam_prod, lam[:, 0::2, :], lam[:, 1::2, :], ALU.mult))
        V.reduce_sum(lam_s[:, 0:2], lam_prod, axis=AX_X).then_inc(sem["lam_sums"], 1)
        for j in range(LEAD):
            split(0, j)
        dve.wait_ge(sem["vecs_ready"], 1)
        norm(0, of_x, lambda k: vec("norm_mix_g", k))
        dve.wait_ge(sem["lam_exps"], 1)
        then(V.tensor_tensor(lam_s[:, 4:5], lam_s[:, 3:4], lam_s[:, 2:3], ALU.subtract))
        then(V.tensor_scalar(lam_s[:, 5:6], lam_s[:, 4:5], -LAM_INIT, None, ALU.add))
        neg_lam = lam_s[:, 5:6]

        def ada(slots, j, g):
            for i, u in enumerate(slots):
                if u == j:
                    k = i % KT
                    slot = k % ADA_RING
                    acc = span(ADA_ACC, 0, ADA_COLS)
                    w = span(ADA_SLOTS, slot * ADA_COLS, ADA_COLS)
                    dve.wait_ge(ada_landed[slot], ((g + i // KT) * (KT // ADA_RING) + (k // ADA_RING + 1)) * 16)
                    if k == 0:
                        m = V.tensor_scalar(acc, w, cs[:, 0:1], None, ALU.mult)
                    else:
                        dve.wait_ge(sem["ada_used"], (g + i // KT) * KT + k)
                        m = stt(acc, w, cs[:, k:k + 1], acc, ALU.mult, ALU.add)
                    m.then_inc(sem["ada_used"], 1)

        def modulation(g):
            dve.wait_ge(sem["mod_psum"], g + 1)
            vg, r, _ = VEC["ada_b_2"]
            cols = bass.ds(g * ADA_F, ADA_F)
            V.tensor_tensor(mod[:, cols], PS[7][:, 0:ADA_F], vecs[:, bass.ds(g * ADA_F + (vg * P + r), ADA_F)],
                            ALU.add).then_inc(sem["mod_ready"], 1)

        dve.wait_ge(sem["cs_ready"], 1)
        with dve.Fori(0, 2) as g:
            for j in range(4 * UA):
                split(R_IN + 4 * g, j + LEAD)
                ada(ADA_ONE, j, g + G_IN)
                if j == 26:
                    modulation(g + G_IN)

        for h in range(HEADS + 1):
            if h < HEADS:
                s, stat = span(46, CW * (h % 2), CW), st[:, h % 2]
                dve.wait_ge(sem["a_scores"], h + 1)
                if h >= 2:
                    dve.wait_ge(sem["a_probsT_psum"], h - 1)
                slope = 2.0 ** (-8.0 * (h + 1) / HEADS)
                stt(s, C("dist"), slope / A_SCALE, PS[h % 2][:, 0:CW], ALU.mult, ALU.add).then_inc(sem["a_masked"], 1)
                dve.wait_ge(sem["a_masked"], h + 1)
                for qt, cols in enumerate(QT):
                    m = V.reduce_max(stat[:, qt:qt + 1], s[:, cols], axis=AX_X)
                then(m)
                V.tensor_scalar(stat[:, 2:4], stat[:, 0:2], -A_SCALE, None, ALU.mult).then_inc(sem["a_negmax"], 1)
            if h >= 1:
                g = h - 1
                p, stat = span(46, CW * (g % 2), CW), st[:, g % 2]
                dve.wait_ge(sem["a_exp"], g + 1)
                for qt, cols in enumerate(QT):
                    m = stt(p[:, cols], p[:, cols], 1.0, C("count")[:, cols], ALU.mult, ALU.mult,
                            accum_out=stat[:, 4 + qt:5 + qt])
                then(m)
                then(V.reciprocal(stat[:, 6:8], stat[:, 4:6]))
                for qt, cols in enumerate(QT):
                    m = V.tensor_scalar(p[:, cols], p[:, cols], stat[:, 6 + qt:7 + qt], None, ALU.mult)
                m.then_inc(sem["a_probs"], 1)
        norm(1, of_arena(0), lambda k: vec("pool_out_norm_g", k))
        norm(2, of_arena(8), lambda k: vec("attn_out_norm_g", k))
        for j in range(4 * UA):
            split(R_OUT, j + LEAD)
            if j == 2 * UA:
                modulation(G_OUT)
            ada(ADA_TWO, j, G_OUT)
            if j % UA == UA - 1:
                add_chunk(R_OUT, j, (j // UA) % 2, x, lambda o: slice(FT * (j // UA) + o, FT * (j // UA) + o + 2))
        modulation(G_OUT + 1)
        dve.wait_ge(drained[0], H_MLP + 1)
        dve.wait_ge(drained[1], H_MLP + 1)
        norm(3, of_x, lambda k: vec("norm_mlp_g", k))

        def square(s, H):
            dve.wait_ge(drained[s], H + 2)
            V.tensor_tensor(T(4, FT), T(0, FT), T(0, FT), ALU.mult).then_inc(sem["relu_sq"], 1)

        def hidden_lo(par, count, tile):
            dve.wait_ge(sem["hid_hi"], count)
            V.tensor_tensor(hid_lo[:, par], T(tile, FT), hid_hi[:, par].bitcast(F32),
                            ALU.subtract).then_inc(sem["hid_ready"], 1)

        def down_ends(R, j, j0, s0, at):
            q = j - j0
            if 0 <= q < 4 * UB and q % UB == UB - 1:
                n = q // UB
                add_chunk(R, j, (s0 + n) % 2, at, lambda o: slice(FT * n + o, FT * n + o + 2))

        for j in range(UA):
            split(R_MLP, j + LEAD)
        square(0, H_MLP)
        hidden_lo(0, 1, 4)
        with dve.Fori(0, MLP_SUPER // 2 - 1) as i:
            R, H = R_MLP + 1 + 4 * i, H_MLP + 5 * i
            for j in range(4 * UA):
                split(R, j + LEAD)
                if j == 7:
                    square(1, H)
                if j == 23:
                    square(0, H + 3)
                if j in (9, 25):
                    hidden_lo(1 if j == 9 else 0, 2 * i + (2 if j == 9 else 3), 4)
                down_ends(R, j, 8, 0, x)
                down_ends(R, j, 24, 1, x)
                ada(ADA_ONE, j, i + G_MLP)
                if j == 26:
                    modulation(i + G_MLP)
        for j in range(3 * UA):
            split(R_MLP + 29, j + LEAD)
            if j == 7:
                square(1, H_MLP + 35)
            if j == 9:
                hidden_lo(1, MLP_SUPER, 4)
            down_ends(R_MLP + 29, j, 8, 0, x)
            down_ends(R_MLP + 29, j, 16, 0, x)
            ada(ADA_TAIL, j, G_MLP + MLP_SUPER // 2 - 1)
        modulation(G_MLP + MLP_SUPER // 2 - 1)
        dve.wait_ge(drained[0], H_IN2 + 1)
        dve.wait_ge(drained[1], H_IN2 + 1)

        norm(4, of_x, lambda k: vec("norm_final_g", k), to=x)
        dve.wait_ge(sem["mod_ready"], G_IN2)
        then(stt(gain5[:], mod[:, KT:2 * KT], 1.0, vec("norm_g_2", 0, KT), ALU.add, ALU.mult))
        then(V.tensor_tensor(gain6[:], mod[:, 2 * KT:3 * KT], vec("norm_g_2", KT, KT), ALU.mult))
        norm(5, of_x, lambda k: gain5[:, k:k + 1], bias=lambda k: mod[:, k:k + 1])

        DT, MAG, THR, SIN, HALF, COS, RE, IM, DEN, FRE, FIM, T0, T1, K = range(14)
        are, aim = vec("s5_a_re_2", 0, 16), vec("s5_a_im_2", 0, 16)

        def v(i):
            return s5v[:, i]

        def s5_angle():
            dve.wait_ge(sem["s_dt"], 1)
            then(V.tensor_tensor(v(MAG), v(DT), are, ALU.mult))
            then(V.tensor_tensor(v(THR), v(DT), aim, ALU.mult))
            then(V.tensor_scalar(v(K), v(THR), float(1 / (2 * np.pi)), ROUND, ALU.mult, ALU.add))
            then(V.tensor_scalar(v(K), v(K), -ROUND, None, ALU.add))
            for part in TWO_PI:
                then(stt(v(THR), v(K), -part, v(THR), ALU.mult, ALU.add))
            V.tensor_scalar(v(THR), v(THR), -PI_BELOW, PI_BELOW, ALU.max, ALU.min).then_inc(sem["s_trig"], 1)

        def s5_discrete():
            dve.wait_ge(sem["s_sin"], 1)
            then(V.tensor_tensor(v(COS), v(HALF), v(HALF), ALU.mult))
            then(V.tensor_scalar(v(COS), v(COS), -2.0, 1.0, ALU.mult, ALU.add))
            then(V.tensor_tensor(v(RE), v(MAG), v(COS), ALU.mult))
            then(V.tensor_tensor(v(IM), v(MAG), v(SIN), ALU.mult))
            then(V.tensor_scalar(v(RE), v(RE), -1.0, None, ALU.add))
            then(V.tensor_tensor(v(DEN), are, are, ALU.mult))
            then(V.tensor_tensor(v(T0), aim, aim, ALU.mult))
            then(V.tensor_tensor(v(DEN), v(DEN), v(T0), ALU.add))
            then(V.reciprocal(v(DEN), v(DEN)))

        def s5_factor():
            for o, p0, p1, op in ((FRE, (RE, are), (IM, aim), ALU.add), (FIM, (IM, are), (RE, aim), ALU.subtract)):
                then(V.tensor_tensor(v(T0), v(p0[0]), p0[1], ALU.mult))
                then(V.tensor_tensor(v(T1), v(p1[0]), p1[1], ALU.mult))
                then(V.tensor_tensor(v(o), v(T0), v(T1), op))
                then(V.tensor_tensor(v(o), v(o), v(DEN), ALU.mult))

        def s5_inputs():
            wide = [P, 16, S5_CH]
            fre, fim = (v(i).unsqueeze(2).to_broadcast(wide) for i in (FRE, FIM))
            by_im = [T(i).rearrange("p (i c) -> p i c", c=S5_CH) for i in (40, 41)]
            then(V.tensor_tensor(by_im[0], s5b[1][:], fim, ALU.mult))
            then(V.tensor_tensor(by_im[1], s5b[0][:], fim, ALU.mult))
            for o, t, op in ((s5b[0], by_im[0], ALU.subtract), (s5b[1], by_im[1], ALU.add)):
                then(V.tensor_tensor(o[:], o[:], fre, ALU.mult))
                then(V.tensor_tensor(o[:], o[:], t, op))

        def s5_powers(levels):
            for l in levels:
                c1, s1 = s5pow[0][:, l], s5pow[1][:, l]
                if l == 0:
                    then(V.tensor_copy(c1, v(COS)))
                    then(V.tensor_copy(s1, v(SIN)))
                    continue
                c0, s0 = s5pow[0][:, l - 1], s5pow[1][:, l - 1]
                then(V.tensor_tensor(v(T0), s0, s0, ALU.mult))
                then(V.tensor_tensor(c1, c0, c0, ALU.mult))
                then(V.tensor_tensor(c1, c1, v(T0), ALU.subtract))
                then(stt(s1, c0, 2.0, s0, ALU.mult, ALU.mult))

        coefficients = {2: s5_angle, 6: s5_discrete, 8: s5_factor, 10: s5_inputs,
                        12: lambda: s5_powers(range(3)), 14: lambda: s5_powers(range(3, 6)),
                        16: lambda: s5_powers(range(6, 8))}

        def projection_unit(c, q):
            ahead = (UA * c + q + LEAD) // UA
            split(R_IN2, UA * c + q + LEAD, cols=P if ahead == 3 else COLS)

        for j in range(4 * UA):
            projection_unit(j // UA, j % UA)
            ada(ADA_ONE, j, G_IN2)
            if j in coefficients:
                coefficients[j]()
        dve.sem_inc(sem["s_pow"], 1)
        modulation(G_IN2)

        def attention_scores(h, m):
            s = span(34, CW * m, CW)
            if (h, m) == (0, 0):
                dve.wait_ge(sem["bias_in"], 32)
            dve.wait_ge(sem["d_scores"], 2 * h + m + 1)
            stt(s, PS[4 + m][:, 0:CW], DA_SCALE, span(28, h * CW, CW), ALU.mult, ALU.add).then_inc(sem["d_masked"], 1)
            dve.wait_ge(sem["d_masked"], 2 * h + m + 1)
            for qt, cols in enumerate(QT):
                i = V.reduce_max(st[:, 0, 4 + 2 * m + qt:5 + 2 * m + qt], s[:, cols], axis=AX_X)
            then(i)
            V.tensor_scalar(st[:, 0, 2 * m:2 * m + 2], st[:, 0, 4 + 2 * m:6 + 2 * m], -1.0, None,
                            ALU.mult).then_inc(sem["d_negmax"], 1)

        def attention_probs(h):
            dve.wait_ge(sem["d_exp"], 2 * h + 2)
            then(V.reciprocal(st[:, 1, 4:8], st[:, 1, 0:4]))
            then(V.tensor_scalar(st[:, 1, 6:8], st[:, 1, 6:8], neg_lam, None, ALU.mult))
            e0, e1, p = span(34, 0, CW), span(34, CW, CW), span(37, 0, CW)
            for qt, cols in enumerate(QT):
                i = V.tensor_scalar(e0[:, cols], e0[:, cols], st[:, 1, 4 + qt:5 + qt], None, ALU.mult)
            then(i)
            if h >= 1:
                dve.wait_ge(sem["d_probsT_psum"], h)
            for qt, cols in enumerate(QT):
                i = stt(p[:, cols], e1[:, cols], st[:, 1, 6 + qt:7 + qt], e0[:, cols], ALU.mult, ALU.add)
            i.then_inc(sem["d_probs"], 1)

        def head_variance(n, sq):
            dve.wait_ge(sem["hn_sum"], n + 1)
            for b in range(2):
                m = V.tensor_scalar(T(sq + 2 * b, 2), halves(PS[6 + b][:]), 1.0 / P, EPS, ALU.mult, ALU.add)
            m.then_inc(sem["hn_var"], 1)

        def head_inverse(n, sq):
            dve.wait_ge(sem["hn_std"], n + 1)
            then(V.reciprocal(T(sq, 4), T(sq, 4)))

        rows = BR_HEADS
        ig, z, b = gate_rows[:, 0, :], gate_rows[:, 1, :], T(43)[0:rows, :]
        soft, a_row = T(42)[0:rows, :], T(40)[0:rows, :]

        for h in range(BR_HEADS):
            for q in range(UA):
                projection_unit(4 + h, q)
                if q < 2:
                    attention_scores(h, q)
                if q == 3:
                    attention_probs(h)
                if h == 0 and q == 4:
                    dve.wait_ge(sem["gates_ready"], 1)
                    then(V.tensor_scalar(z, z, gate_b[:, 1:2], None, ALU.add))
                    stt(soft, z, -1.0, z, ALU.mult, ALU.max).then_inc(sem["m_absz"], 1)
                if h == 1 and q == 4:
                    dve.wait_ge(sem["m_log"], 1)
                    then(stt(soft, z, 0.0, soft, ALU.min, ALU.subtract))
                    then(V.tensor_tensor_scan(b, ones[0:rows, 0:1].to_broadcast([rows, S]), soft, 0.0, ALU.mult, ALU.add))
                    stt(a_row, ig, gate_b[:, 0:1], b, ALU.add, ALU.subtract).then_inc(sem["m_rows"], 1)

        def mlstm_weights(h):
            dve.wait_ge(sem["m_bc"], h + 1)
            if h >= 1:
                dve.wait_ge(sem["m_ST_psum"], h)
            e = span(52, 0, CW)
            V.tensor_tensor(e[:, 0:P], PS[4][:, 0:P], C("causal"), ALU.add)
            V.tensor_copy(e[:, P:S], PS[4][:, 0:P])
            then(V.tensor_tensor(e[:, S:CW], PS[4][:, P:S], C("causal"), ALU.add))
            for qt, cols in enumerate(QT):
                m = V.reduce_max(st[:, 0, qt:qt + 1], e[:, cols], axis=AX_X)
            then(m)
            then(V.tensor_scalar(st[:, 0, 0:2], st[:, 0, 0:2], 0.0, None, ALU.max))
            if h == 0:
                dve.wait_ge(sem["m_rows"], 2)
            V.tensor_scalar(st[:, 0, 2:4], st[:, 0, 0:2], -1.0, None, ALU.mult)
            stt(st[:, 0, 4:6], st[:, 0, 0:2], -1.0, BT[:, :, h], ALU.mult, ALU.subtract).then_inc(sem["m_A"], 1)

        def mlstm_scores(h):
            e = span(52, 0, CW)
            dve.wait_ge(sem["m_qk"], h + 1)
            dve.wait_ge(sem["m_E"], h + 1)
            for qt, cols in enumerate(QT):
                m = stt(e[:, cols], PS[5][:, cols], ML_SCALE, e[:, cols], ALU.mult, ALU.mult,
                        accum_out=st[:, 1, 4 + qt:5 + qt])
            then(m)
            then(stt(st[:, 1, 4:6], st[:, 1, 4:6], -1.0, st[:, 1, 4:6], ALU.mult, ALU.max))
            then(V.tensor_tensor(st[:, 1, 4:6], st[:, 1, 4:6], st[:, 1, 0:2], ALU.max))
            then(V.reciprocal(st[:, 1, 6:8], st[:, 1, 4:6]))
            for qt, cols in enumerate(QT):
                m = V.tensor_scalar(e[:, cols], e[:, cols], st[:, 1, 6 + qt:7 + qt], None, ALU.mult)
            m.then_inc(sem["m_S"], 1)

        run = span(16, 0, 2 * (S + 1)).rearrange("p (a b) -> p a b", a=2)
        la = T(8, 2)
        arg = T(12, 4)

        def level_args(level):
            nb = S // level
            now = run[:, :, 1:S + 1].rearrange("p a (n l) -> p a n l", l=level)
            to = arg.rearrange("p (w a) (n l) -> p w a n l", w=2, l=level)
            start = run[:, :, 0:S].rearrange("p a (n l) -> p a n l", l=level)[:, :, :, 0:1]
            end = now[:, :, :, level - 1:level]
            for t in range(2):
                V.tensor_tensor(to[:, 0, t], now[:, t], start[:, t].to_broadcast([P, nb, level]), ALU.subtract)
                m = V.tensor_tensor(to[:, 1, t], end[:, t].to_broadcast([P, nb, level]), now[:, t], ALU.subtract)
            m.then_inc(sem["g_arg"], 1)

        for h in range(BR_HEADS):
            for q in range(UA):
                projection_unit(8 + h, q) if (h, q) < (3, LEAD) else split(R_GATE, UA * (h - 4) + q + LEAD)
                if h == 0 and q == 0:
                    head_variance(0, 34)
                if h == 0 and q == 1:
                    head_inverse(0, 34)
                    stt(T(0, 4), T(0, 4), 1.0 - LAM_INIT, T(34, 4), ALU.mult, ALU.mult).then_inc(sem["branch_ready"], 1)
                if q == 2:
                    mlstm_weights(h)
                if q == 4:
                    mlstm_scores(h)
                if h == 1 and q == 5:
                    dve.wait_ge(sem["g_z"], 1)
                    stt(T(10, 2), la, -1.0, la, ALU.mult, ALU.max).then_inc(sem["g_absz"], 1)
                if h == 2 and q == 5:
                    dve.wait_ge(sem["g_log"], 1)
                    dve.wait_ge(sem["m_conv"], 1)
                    then(stt(la, la, 0.0, T(10, 2), ALU.min, ALU.subtract))
                    then(V.tensor_scalar(la, la, 1.0 / GLA_TAU, None, ALU.mult))
                    then(V.memset(run[:, :, 0:1], 0.0))
                    for t in range(2):
                        m = V.tensor_tensor_scan(run[:, t, 1:S + 1], ones[:, 0:1].to_broadcast([P, S]), la[:, t], 0.0,
                                                 ALU.mult, ALU.add)
                    then(m)
                if h == 3 and q == 6:
                    level_args(turned_level(0))
                if q == 7:
                    dve.wait_ge(sem["m_sig"], 1)
                    dve.wait_ge(sem["m_out_psum"], h + 1)
                    V.tensor_tensor(T(4 + h), PS[6][:, S:2 * S], T(24 + h), ALU.mult).then_inc(sem["m_out"], 1)

        def gla_steps(u):
            n = u // 4
            if u % 4 == 0 and n < GLA_STEPS and turned_level(n):
                dve.wait_ge(sem["g_exp"], n + 1 if n < len(GLA_LEVELS) else GLA_STEPS - 1)
                if n >= 1:
                    dve.wait_ge(sem["g_att_psum"], n)
                V.tensor_tensor(T(44, 2), arg[:, 0:2], T(28, 2), ALU.mult)
                V.tensor_tensor(T(46, 2), arg[:, 2:4], T(30, 2), ALU.mult).then_inc(sem["g_qk"], 1)
            if u % 4 == 2 and n < GLA_STEPS - 1:
                level = turned_level(n)
                dve.wait_ge(sem["g_att_psum"], n + 1)
                mask = (C("levels", lo=n * P, n=P) if level else ident).unsqueeze(1).to_broadcast([P, 4, P])
                accs = [span(48 + 2 * par, 0, 512).rearrange("p (a b) -> p a b", a=4) for par in range(2)]
                tmps = [span((52, 56)[par], 0, 512).rearrange("p (a b) -> p a b", a=4) for par in range(2)]
                if n == 0:
                    dve.wait_ge(sem["m_ST_psum"], BR_HEADS)
                for par in range(2):
                    m = V.tensor_tensor(tmps[par] if n else accs[par], PS[4 + par][:].rearrange("p (a b) -> p a b", a=4),
                                        mask, ALU.mult)
                m.then_inc(sem["g_att_read"], 1)
                dve.wait_ge(sem["g_att_read"], n + 1)
                if n:
                    for par in range(2):
                        m = V.tensor_tensor(accs[par], accs[par], tmps[par], ALU.add)
                    if n == GLA_STEPS - 2:
                        m.then_inc(sem["g_att"], 1)
                    else:
                        then(m)
            if u % 4 == 3 and n + 1 < GLA_STEPS and turned_level(n + 1):
                level_args(turned_level(n + 1))
            if u == 38:
                head_variance(1, 44)
            if u == 39:
                head_inverse(1, 44)
                dve.wait_ge(sem["g_sig"], 1)
                then(V.tensor_tensor(T(0, 4), T(0, 4), T(44, 4), ALU.mult))
                V.tensor_tensor(T(0, 4), T(0, 4), T(36, 4), ALU.mult).then_inc(sem["branch_ready"], 1)

        bu, rot = (T(24, 4), T(28, 4)), (T(32, 4), T(36, 4))

        def s5_steps(t, u):
            cosT, sinT = rotation(t)

            def scan(part):
                for ii in range(4):
                    m = V.tensor_tensor_scan(bu[part][:, ii], v(MAG)[:, 4 * t + ii:4 * t + ii + 1].to_broadcast([P, S]),
                                             rot[part][:, ii], 0.0, ALU.mult, ALU.add)
                return m

            if u == 4:
                dve.wait_ge(sem["s_table"], t + 1)
                dve.wait_ge(sem["s_bu"], t + 1)
                if t >= 1:
                    dve.wait_ge(sem["s_y_psum"], t)
                then(V.tensor_tensor(rot[0], bu[0], cosT, ALU.mult))
            elif u == 5:
                then(V.tensor_tensor(rot[1], bu[1], sinT, ALU.mult))
            elif u == 6:
                then(V.tensor_tensor(rot[0], rot[0], rot[1], ALU.add))
            elif u == 7:
                then(V.tensor_tensor(rot[1], bu[1], cosT, ALU.mult))
            elif u == 8:
                then(V.tensor_tensor(bu[0], bu[0], sinT, ALU.mult))
                then(V.tensor_tensor(rot[1], rot[1], bu[0], ALU.subtract))
            elif u in (10, 11):
                then(scan(u - 10))
            elif u == 12:
                then(V.tensor_tensor(rot[0], bu[0], cosT, ALU.mult))
            elif u == 13:
                then(V.tensor_tensor(rot[1], bu[1], sinT, ALU.mult))
            elif u == 14:
                then(V.tensor_tensor(rot[0], rot[0], rot[1], ALU.subtract))
            elif u == 15:
                then(V.tensor_tensor(rot[1], bu[0], sinT, ALU.mult))
            elif u == 16:
                then(V.tensor_tensor(bu[1], bu[1], cosT, ALU.mult))
            elif u == 17:
                V.tensor_tensor(rot[1], rot[1], bu[1], ALU.add).then_inc(sem["s_x"], 1)
            elif u == 19:
                dve.wait_ge(sem["s_y_psum"], t + 1)
                stt(T(40 + t), T(40 + t), vec("s5_d_2", t), PS[6][:, 0:S], ALU.mult, ALU.add).then_inc(sem["s_y"], 1)

        def last_steps(u):
            if u == 2:
                dve.wait_ge(sem["s_glu"], 1)
                V.tensor_tensor(T(24, 4), T(24, 4), T(28, 4), ALU.mult).then_inc(sem["branch_ready"], 1)
            for g in range(2):
                if u == ADA_GATE[KT * g + KT - 1] + 1:
                    modulation(G_GATE + g)
            ada(ADA_GATE, u, G_GATE)

        for i in range(4):
            R, H = R_GATE + 5 * i, H_GATE + 4 * i
            source = (0, 4, 0, 24)[i]
            for j in range(40):
                split(R, j + LEAD)
                if j == (4 if i == 3 else 1):
                    dve.wait_ge(sem["op_hi"], i + 1)
                    V.tensor_tensor(hid_lo[:, 0], T(source, FT), hid_hi[:, 0].bitcast(F32),
                                    ALU.subtract).then_inc(sem["hid_ready"], 1)
                if j % 10 == 9:
                    n = j // 10
                    sig = T(4, FT) if i else merged(n)
                    dve.wait_ge(drained[0], H + (n + 2))
                    dve.wait_ge(sem["unit_done"], R * 8 + (j + 1))
                    for b in range(2):
                        m = V.tensor_tensor(sig[:, 2 * b:2 * b + 2], halves(SETS[1][b][:]), sig[:, 2 * b:2 * b + 2], ALU.mult)
                    m.then_inc(drained[1], 1)
                    dve.wait_ge(drained[1], H + (n + 2))
                    if i:
                        V.tensor_tensor(merged(n), merged(n), sig, ALU.add).then_inc(sem["sig_free"], 1)
                        if i < 3:
                            dve.wait_ge(sem["sig_free"], 4 * (i - 1) + n + 1)
                (gla_steps, lambda u: s5_steps(u // 20, u % 20), lambda u: s5_steps(2 + u // 20, u % 20), last_steps)[i](j)
        for n in range(4):
            dve.wait_ge(sem["merged_hi"], n + 1)
            V.tensor_tensor(hop_lo[:, FT * n:FT * n + FT], merged(n), hop_hi[:, FT * n:FT * n + FT].bitcast(F32),
                            ALU.subtract).then_inc(sem["merged_ready"], 1)
        for j in range(4 * UA):
            split(R_OUT2, j + LEAD)
            ada(ADA_ONE, j, G_OUT2)
            if j == 26:
                modulation(G_OUT2)
        dve.wait_ge(sem["mod_ready"], ADA_GROUPS)
        then(stt(gain7[:], mod[:, 4 * KT:5 * KT], 1.0, vec("norm_g_2", 2 * KT, KT), ALU.add, ALU.mult))
        then(V.tensor_tensor(gain8[:], mod[:, 5 * KT:6 * KT], vec("norm_g_2", 3 * KT, KT), ALU.mult))
        norm(6, of_arena(0), lambda k: gain6[:, k:k + 1])
        dve.wait_ge(sem["x_back"], 16)
        residual(6)
        dve.wait_ge(sem["res_ready"], 1)
        norm(7, of_x, lambda k: gain7[:, k:k + 1], bias=lambda k: mod[:, 3 * KT + k:3 * KT + k + 1])

        then(V.memset(T(0, KT), 0.0))

        def product(H):
            dve.wait_ge(drained[0], H + 2)
            for b in range(2):
                m = V.tensor_tensor(T(20 + 2 * b, 2), halves(SETS[1][b][:]), T(16 + 2 * b, 2), ALU.mult)
            m.then_inc(drained[1], 1)

        base = MLP_SUPER
        for j in range(2 * UA):
            split(R_FFN, j + LEAD)
        dve.wait_ge(sem["unit_done"], R_FFN * 8 + 2 * UA)
        product(H_FFN)
        hidden_lo(0, base + 1, 20)
        with dve.Fori(0, FFN_SUPER // 2) as i:
            R, H = R_FFN + 2 + 6 * i, H_FFN + 1 + 6 * i
            for j in range(6 * UA):
                split(R, j + LEAD)
                par = j // 24
                if j % 24 == 15:
                    dve.wait_ge(sem["unit_done"], R * 8 + (j + 1))
                    product(H + 3 * par)
                if j % 24 == 17:
                    hidden_lo(1 - par, 2 * i + (base + par + 2), 20)
                down_ends(R, j, 24 * par + 16, 0, arena)
        R = R_FFN + 2 + 3 * (FFN_SUPER - 1)
        for j in range(UA):
            if j < UA - LEAD:
                split(R, j + LEAD)
            down_ends(R, j, 0, 0, arena)
        dve.wait_ge(drained[0], R_END_H + 1)
        dve.wait_ge(drained[1], R_END_H + 1)
        norm(8, of_arena(0), lambda k: gain8[:, k:k + 1])
        residual(8)

    @block.gpsimd
    def _(pool):
        G = nc.gpsimd
        steps = [0]

        def then(ins):
            steps[0] += 1
            ins.then_inc(sem["pool_chain"], 1)
            pool.wait_ge(sem["pool_chain"], steps[0])

        def small(o, i):
            pool.dma_start(o, i).then_inc(sem["small_in"], 16)

        pool.wait_ge(sem["table_clear"], 1)
        small(bias_all[64:64 + N_BUCKETS, :], a["rel_bias_2"])
        small(lam, a["diff_lambda_2"][0].partition_broadcast(P))
        with nc.allow_non_contiguous_dma(reason="a few words"):
            small(gate_b[:], a["ml_gate_b_2"][0].rearrange("w h -> h w"))
            log_dt = a["s5_log_dt_2"]
            for half in range(2):
                small(s5v[64 * half:64 * half + 64, 15, :],
                      bass.AP(log_dt.tensor, log_dt.offset + half, [[0, S5_STATE], [2, 16], [1, 1]]).rearrange("p a b -> p (a b)"))
        small(wa2, a["gla_wa2_2"][0])
        for o, name in ((s5b[0], "s5_b_re_2"), (s5b[1], "s5_b_im_2")):
            small(o[:], a[name][0].rearrange("(i h) s c -> (h s) i c", h=2))
        for o, name in ((s5c[0], "s5_c_re_2"), (s5c[1], "s5_c_im_2")):
            small(o[:], a[name][0].rearrange("(t g) c s -> (g c) t s", t=4))
        pool.wait_ge(sem["bias_copied"], 1)
        pool.dma_start(bias_scratch[:].rearrange("h p j -> p h j"),
                       span(32, 0, BR_HEADS * 384).rearrange("p (h j) -> p h j", h=BR_HEADS)).then_inc(sem["bias_out"], 16)
        pool.wait_ge(sem["bias_out"], 16)
        pool.dma_start(T(32, 8), a["pool_w"][0].rearrange("g (c p) f -> p (g c) f", p=P)).then_inc(sem["pool_w_in"], 16)

        pad = POOL_PAD
        bufs = [span(40 + 3 * i, 0, 2 * (pad + S)).rearrange("p (a b) -> p a b", a=2) for i in range(2)]
        head = span(54, 0, 2 * pad).rearrange("p (a b) -> p a b", a=2)
        for b in bufs:
            then(G.memset(b, 0.0))
        for s in range(2):
            pool.wait_ge(drained[s], H_OUT + 1)
        for g, w in enumerate(POOL_WINDOWS):
            u = T(2 * g, 2)
            cur = 0
            then(G.tensor_copy(bufs[0][:, :, pad:], u))
            lag = 1
            while lag < w:
                src, dst = bufs[cur], bufs[1 - cur]
                then(G.tensor_tensor(dst[:, :, pad:], src[:, :, pad:], src[:, :, pad - lag:pad + S - lag], ALU.add))
                cur, lag = 1 - cur, 2 * lag
            tail = bufs[cur]
            scale = C("poolfix", lo=g * pad, n=pad).unsqueeze(1).to_broadcast([P, 2, pad])
            then(G.tensor_tensor(head, tail[:, :, pad:2 * pad], scale, ALU.mult))
            then(G.tensor_tensor(head, head, u[:, :, 0:pad], ALU.subtract))
            then(G.tensor_scalar(tail[:, :, pad:], tail[:, :, pad:], 1.0 / w, None, ALU.mult))
            then(G.tensor_tensor(u, tail[:, :, pad:], u, ALU.subtract))
            then(G.tensor_copy(u[:, :, 0:pad], head))
            pool.sem_inc(sem["pooled"], 1)

        pool.wait_ge(sem["normed"], before(5, "normed"))
        pool.dma_start(x_scratch[:], x[:]).then_inc(sem["x_parked"], 16)
        pool.wait_ge(sem["hop_ready"], before(6, "hop"))
        tensor = bias_scratch
        at = [[383, P], [P * 384, BR_HEADS]]
        bias = span(28, 0, BR_HEADS * CW).rearrange("p (h j) -> p h j", h=BR_HEADS)
        pool.dma_start(bias[:, :, 0:P], bass.AP(tensor, P - 1 + P, at + [[1, P]])).then_inc(sem["bias_in"], 16)
        pool.dma_start(bias[:, :, P:CW], bass.AP(tensor, P - 1, at + [[1, S]])).then_inc(sem["bias_in"], 16)

        pool.wait_ge(sem["mod_ready"], G_IN2 + 1)
        for i in range(2):
            pool.wait_ge(drained[i], H_IN2 + 4)
            src, o, tap_of = T(12 + 4 * i, 4), T(44 + 4 * i, 4), T(59, 4)
            for f in range(4):
                m = G.tensor_scalar(o[:, f], src[:, f], vec("ml_conv_2", 3 * 8 + 4 * i + f), None, ALU.mult)
            then(m)
            for tap in (2, 1, 0):
                lag = 3 - tap
                for f in range(4):
                    m = G.tensor_scalar(tap_of[:, f], src[:, f], vec("ml_conv_2", tap * 8 + 4 * i + f), None, ALU.mult)
                then(m)
                then(G.tensor_tensor(o[:, :, lag:S], o[:, :, lag:S], tap_of[:, :, 0:S - lag], ALU.add))
        pool.sem_inc(sem["m_conv"], 1)

        mask = C("s5b").rearrange("p (i g) -> p i g", i=4).unsqueeze(3).to_broadcast([P, 4, 8, S5_CH])
        pool.wait_ge(sem["s_pow"], 1)
        pool.wait_ge(sem["g_arg"], GLA_STEPS - 1)

        def table(t):
            cosT, sinT = rotation(t)
            G.memset(cosT[:, :, 0:1], 1.0)
            then(G.memset(sinT[:, :, 0:1], 0.0))
            for l in range(8):
                n = 1 << l
                c1, s1 = (s5pow[i][:, l, 4 * t:4 * t + 4].unsqueeze(2).to_broadcast([P, 4, n]) for i in range(2))
                c0, s0 = cosT[:, :, 0:n], sinT[:, :, 0:n]
                cn, sn = cosT[:, :, n:2 * n], sinT[:, :, n:2 * n]
                tmp = span(70, 0, 512).rearrange("p (i n) -> p i n", i=4)[:, :, 0:n]
                G.tensor_tensor(tmp, s0, s1, ALU.mult)
                then(G.tensor_tensor(cn, c0, c1, ALU.mult))
                then(G.tensor_tensor(cn, cn, tmp, ALU.subtract))
                G.tensor_tensor(tmp, c0, s1, ALU.mult)
                then(G.tensor_tensor(sn, s0, c1, ALU.mult))
                then(G.tensor_tensor(sn, sn, tmp, ALU.add))
            pool.sem_inc(sem["s_table"], 1)

        def spread_inputs(t):
            if t == 0:
                pool.wait_ge(sem["g_out"], 1)
            else:
                pool.wait_ge(sem["s_turned"], t)
            for part in range(2):
                m = G.tensor_tensor(span(52 + 2 * part, 0, 512).rearrange("p (i g c) -> p i g c", i=4, g=8),
                                    s5b[part][:, 4 * t:4 * t + 4].unsqueeze(2).to_broadcast([P, 4, 8, S5_CH]), mask, ALU.mult)
            m.then_inc(sem["s_pad"], 1)

        def spread_outputs(t):
            if t >= 1:
                pool.wait_ge(sem["s_cturned"], t)
            for part in range(2):
                m = G.tensor_tensor(span(66 + 2 * part, 0, 512).rearrange("p (h s) -> p h s", h=8),
                                    s5c[part][:, t:t + 1].to_broadcast([P, 8, S5_STATE]),
                                    C("s5c").unsqueeze(2).to_broadcast([P, 8, S5_STATE]), ALU.mult)
            m.then_inc(sem["s_cpad"], 1)

        for t in range(4):
            if t >= 2:
                pool.wait_ge(sem["s_x"], t - 1)
            table(t)
            spread_inputs(t)
            spread_outputs(t)
        pool.wait_ge(sem["s_x"], 3)
        pool.dma_start(flat(T(16, 8)).rearrange("p (k n) -> p k n", k=4),
                       a["s5_glu_w_2"][0].rearrange("(k p) n -> p k n", p=P)).then_inc(sem["glu_w_in"], 16)
        pool.wait_ge(sem["x_parked"], 16)
        pool.wait_ge(sem["merged_ready"], 4)
        pool.dma_start(x[:], x_scratch[:]).then_inc(sem["x_back"], 16)
    ctx.close()


INPUTS = """x norm_mix_g w_in pool_w pool_scale pool_out_norm_g attn_out_norm_g w_out norm_mlp_g w_up w_down norm_final_g
c_2 ada_w_2 ada_b_2 norm_g_2 w_in_2 rel_bias_2 diff_lambda_2 ml_conv_2 ml_gate_b_2 gla_wa2_2 gla_ba_2 s5_a_re_2 s5_a_im_2
s5_log_dt_2 s5_b_re_2 s5_b_im_2 s5_c_re_2 s5_c_im_2 s5_d_2 s5_glu_w_2 s5_glu_b_2 w_branch_2 w_gate_2 b_gate_2 w_out_2
ffn_w_in_2 ffn_w_out_2""".split()


def kernel(**inputs):
    import concourse.bacc as bacc
    from concourse.bass_utils import run_bass_kernel_spmd

    nc = bacc.Bacc("TRN2", target_bir_lowering=False, num_devices=1)
    arrays, aps = {}, {}
    for name in INPUTS:
        v = np.ascontiguousarray(inputs[name])
        arrays[f"in_{name}"] = v
        aps[name] = nc.dram_tensor(f"in_{name}", v.shape, mybir.dt.from_np(v.dtype), kind="ExternalInput").ap()
    arrays["in_constants"] = shape_constants()
    consts = nc.dram_tensor("in_constants", arrays["in_constants"].shape, F32, kind="ExternalInput").ap()
    out = nc.dram_tensor("out_0", (1, S, D), F32, kind="ExternalOutput").ap()
    two_blocks(nc, aps, consts, out)
    r = run_bass_kernel_spmd(nc, [arrays], core_ids=[0])
    return r.results[0]["out_0"]
```

```python
from contextlib import ExitStack

import numpy as np
import concourse.bass as bass
from concourse import mybir

F32 = mybir.dt.float32
F32R = mybir.dt.float32r
ALU = mybir.AluOpType
ACT = mybir.ActivationFunctionType
AX_X = mybir.AxisListType.X

P = 128
S = 256
D = 2048
KT = D // P
TT = S // P
EPS = 1e-6
NEG = -1e30

UK = 2
COLS = 512
FT = COLS // P
RAW = 4
LEAD = 4
UA = KT // UK
UB = FT // UK
D_FF = 4 * D
FFN = 5632
MLP_SUPER = D_FF // COLS
FFN_SUPER = FFN // COLS
R_IN, R_OUT, R_MLP, R_IN2, R_GATE, R_OUT2, R_FFN = 0, 8, 12, 44, 56, 76, 80
H_IN, H_OUT, H_MLP, H_IN2, H_GATE, H_OUT2, H_FFN = 0, 4, 6, 46, 52, 68, 70
OUT_ORDER = [(c, UA // 2 * half + q) for half in range(2) for c in range(2) for q in range(UA // 2)]
OUT_ORDER += [(c, q) for c in range(2, 4) for q in range(UA)]
OUT_LAST = [OUT_ORDER.index((c, UA - 1)) for c in range(4)]
R_END_H = H_FFN + 3 * FFN_SUPER

POOL_WINDOWS = (2, 4, 8, 16)
POOL_PAD = max(POOL_WINDOWS)
HEADS = 8
DILATED_PATTERNS = ((128, 1), (512, 4), (2048, 16))
A_SCALE = float(P) ** -0.5
IN_ORDER = (2, 4, 6, 3, 5, 1, 0, 7)
POOL_ORDER = (2, 3, 0, 1)
SCORES_AT = (25, 28, 31, 34, 41, 44, 47, 50)
TURN_LATER = 4

BR_HEADS = 4
DA_DIM = 64
DA_SCALE = float(DA_DIM) ** -0.5
N_BUCKETS, MAX_DISTANCE = 32, 128
LAM_INIT = 0.8 - 0.6 * float(np.exp(-0.3 * 0))
ML_SCALE = float(P) ** -0.5
GLA_DK = 64
GLA_SCALE = float(GLA_DK) ** -0.5
GLA_TAU = 16.0
GLA_RANK = 16
GLA_LEVELS = (64, 32, 16, 8, 4, 2, 1)
S5_STATE, S5_CH = 64, 16
ROUND = 1.5 * 2.0 ** 23
_two_pi = 2 * np.pi
_c1 = float(np.floor(_two_pi * 2 ** 8) / 2 ** 8)
_c2 = float(np.floor((_two_pi - _c1) * 2 ** 20) / 2 ** 20)
TWO_PI = (_c1, _c2, float(_two_pi - _c1 - _c2))
PI_BELOW = 3.1415925
N_SMALL = 10
COL_GATES, COL_GLA, COL_GLA_A, COL_S5 = 3584, 3592, 5128, 5144
ADA_COLS = 768
ADA_F = ADA_COLS // P
ADA_GROUPS = 6 * D // ADA_COLS
ADA_RING = 4
ADA_ACC, ADA_SLOTS = 56, 59
G_IN, G_OUT, G_MLP, G_IN2, G_GATE, G_OUT2 = 0, 2, 4, 12, 13, 15
ADA_AHEAD = 4
ADA_FIRST = [6 + k * 18 // 15 for k in range(KT)]
ADA_ONE = [j for j in range(24) if j % 3 != 2]
ADA_TAIL = [k + k // 4 for k in range(KT)]
ADA_TWO = [g * 16 + k * (12 - g) // 15 for g in range(2) for k in range(KT)]
ADA_GATE = [2 + 18 * g + k for g in range(2) for k in range(KT)]

CW = P + S

CONST = {}
_at = 0
for _n, _w in (("ident", P), ("dist", CW), ("count", CW), ("causal", P), ("levels", len(GLA_LEVELS) * P),
               ("poolfix", len(POOL_WINDOWS) * POOL_PAD), ("s5b", 32), ("s5c", 8), ("rowsel", BR_HEADS * P)):
    CONST[_n] = (_at, _w)
    _at += _w
CONST_COLS = _at

VEC_GROUPS = [
    [("norm_mix_g", 16), ("pool_scale", 8), ("pool_out_norm_g", 8), ("attn_out_norm_g", 8), ("norm_mlp_g", 16),
     ("norm_final_g", 16), ("c_2", 16), ("gla_ba_2", 2), ("s5_d_2", 4), ("s5_glu_b_2", 4), ("s5_a_re_2", 16)],
    [("norm_g_2", 64), ("b_gate_2", 64)],
    [("ada_b_2", 96), ("ml_conv_2", 32)],
    [("s5_a_im_2", 16)],
]
VEC = {}
for _g, _rows in enumerate(VEC_GROUPS):
    _r = 0
    for _n, _k in _rows:
        VEC[_n] = (_g, _r, _k)
        _r += _k
VEC_ROWS = [sum(k for _, k in rows) for rows in VEC_GROUPS]
N_VEC_DMAS = sum(len(rows) for rows in VEC_GROUPS) - 1


def shape_constants():
    c = {n: np.zeros((P, w), np.float32) for n, (_, w) in CONST.items()}
    c["ident"][:] = np.eye(P)
    p = np.arange(P)[:, None]
    for qt, (at, keys) in enumerate(((0, P), (P, S))):
        d = qt * P + p - np.arange(keys)[None, :]
        n = np.zeros(d.shape)
        for window, dil in DILATED_PATTERNS:
            n += (d >= 0) & (d <= window) & (d % dil == 0)
        c["count"][:, at:at + keys] = n
        c["dist"][:, at:at + keys] = np.where(n > 0, -d, NEG)
    j, t = np.arange(P)[:, None], np.arange(P)[None, :]
    for i, level in enumerate(GLA_LEVELS):
        c["levels"][:, i * P:(i + 1) * P] = ((t // level) % 2 == 1) & (j // level == t // level - 1)
    c["causal"][:] = np.where(j >= t, 0.0, NEG)
    for g, w in enumerate(POOL_WINDOWS):
        c["poolfix"][:, g * POOL_PAD:(g + 1) * POOL_PAD] = 1.0 / np.minimum(np.arange(POOL_PAD) + 1, w)
    for ii in range(4):
        for g in range(8):
            c["s5b"][:, ii * 8 + g] = (g == 2 * ii + np.arange(P) // S5_STATE)
    for g in range(8):
        c["s5c"][:, g] = np.arange(P) // S5_CH == g
    for h in range(BR_HEADS):
        c["rowsel"][h, h * P:(h + 1) * P] = 1.0
    n = S - 1 - np.arange(384)
    exact = N_BUCKETS // 2
    large = exact + (np.log(np.maximum(n, 1) / exact) / np.log(MAX_DISTANCE / exact) * (N_BUCKETS - exact)).astype(int)
    bucket = np.where(n < exact, n, np.minimum(large, N_BUCKETS - 1))
    for i in range(384):
        if n[i] >= 0:
            c["rowsel"][64 + bucket[i], i] = 1.0
        else:
            c["rowsel"][64 + N_BUCKETS, i] = NEG
    return np.concatenate([c[n] for n in CONST], axis=1)


SEMS = """const_in ident_in gain_in gain_turned vec_in small_in x_turned x_copied vec_turned vecs_ready cs_ready
lam_sums lam_exps bias_rows_ready bias_psum bias_copied bias_out bias_in
hi_ready lo_ready unit_done drained0 drained1
sq_ready sq_folded sum_ready var_ready std_ready normed hop_hi hop_ready
pool_w_in pooled pool_psum pool_ready
a_scores a_masked a_negmax a_exp a_probs a_probsT_psum a_probsT a_vT_psum a_vT a_out_psum a_out
relu_scaled relu_sq hid_hi hid_ready
ada_used mod_psum mod_ready
small_w_in gates_ready
d_scores d_masked d_negmax d_exp d_probs d_probsT_psum d_probsT d_vT_psum d_vT d_out_psum d_out branch_ready
hn_sq hn_sum hn_var hn_std
m_conv m_silu m_absz m_log m_rows m_bc m_BT m_qk m_vT_psum m_vT m_A m_E m_S m_ST_psum m_ST m_out_psum m_out m_sig
g_z_psum g_z g_absz g_log g_arg g_exp g_qk g_att_psum g_att_read g_vT_psum g_vT g_att g_x g_x_copied g_out_psum g_out g_sig
s_dt s_exp s_trig s_sin s_pow s_table s_pad s_turned s_BT s_bu_psum s_bu s_x s_cpad s_cturned s_CT s_y_psum s_y s_z s_glu_psum s_glu
glu_w_in table_clear sum_clear x_normed x_parked x_back
op_hi gated sig_free merged_hi merged_ready
res_ready out_psum out_copied stored
act_chain dve_chain pool_chain""".split()


def two_blocks(nc, a, consts, out):
    ctx = ExitStack()

    def sb(name, shape, dt=F32):
        return ctx.enter_context(nc.sbuf_tensor(name, shape, dt))

    sem = {n: ctx.enter_context(nc.semaphore(n)) for n in SEMS}
    x_in = [ctx.enter_context(nc.semaphore(f"x_in{i}")) for i in range(4)]
    raw_landed = [ctx.enter_context(nc.semaphore(f"raw_landed{i}")) for i in range(RAW)]
    ada_landed = [ctx.enter_context(nc.semaphore(f"ada_landed{i}")) for i in range(ADA_RING)]
    drained = [sem["drained0"], sem["drained1"]]

    const = sb("const", [P, CONST_COLS])
    vecs = sb("vecs", [P, (len(VEC_GROUPS) - 1) * P + VEC_ROWS[-1]])
    x = sb("x", [P, KT, S])
    hop_hi = sb("hop_hi_part", [P, KT, S], F32R)
    hop_lo = sb("hop_lo_part", [P, KT, S], F32R)
    hid_hi = sb("hid_hi_part", [P, 2, FT, S], F32R)
    hid_lo = sb("hid_lo_part", [P, 2, FT, S], F32R)
    w_raw = sb("w_raw", [P, RAW, UK, COLS])
    w_hi = sb("w_hi", [P, LEAD, UK, COLS], F32R)
    w_lo = sb("w_lo", [P, LEAD, UK, COLS], F32R)
    NT = 72
    arena = sb("arena", [P, NT, S])
    ones = sb("ones", [P, P])
    var, std, rstd = (sb(n, [P, S]) for n in ("var", "std", "rstd"))
    fix = std
    cs = sb("cs", [P, KT])
    mod = sb("mod", [P, 6 * KT])
    gain5, gain6, gain7, gain8 = (sb(n, [P, KT]) for n in ("gain5", "gain6", "gain7", "gain8"))
    gain0 = gain8
    st = sb("st", [P, 2, 16])
    lam = arena[:, 52, :].rearrange("p (a b) -> p a b", a=4)
    lam_prod = arena[:, 53, 0:2 * DA_DIM].rearrange("p (a b) -> p a b", a=2)
    lam_s = sb("lam_s", [P, 8])
    bias_all = sb("bias_table", [P, BR_HEADS])
    BROWS = slice(64, 64 + N_BUCKETS + 1)
    bias_table = bias_all[BROWS, :]
    gate_b = sb("gate_b", [BR_HEADS, 2])
    row_store = sb("row_store", [P, 2, S])
    gate_rows = row_store[0:BR_HEADS]
    gla_a, wa2 = (row_store[64:64 + GLA_RANK, i, :] for i in range(2))
    BT = sb("BT", [P, TT, BR_HEADS])
    gate_bias = sb("gate_bias", [P, KT])
    s5b = [sb(n, [P, 16, S5_CH]) for n in ("s5b_re", "s5b_im")]
    s5c = [sb(n, [P, 4, S5_STATE]) for n in ("s5c_re", "s5c_im")]
    s5v = sb("s5v", [P, 16, 16])
    s5pow = [std[:, i * P:(i + 1) * P].rearrange("p (l i) -> p l i", l=8) for i in range(2)]
    x_scratch = nc.dram_tensor("x_scratch", [P, KT, S], F32, kind="Internal")
    bias_scratch = nc.dram_tensor("bias_scratch", [BR_HEADS, P, 384], F32, kind="Internal")

    PS = [ctx.enter_context(nc.psum_tensor(f"ps{i}", [P, 512], F32)) for i in range(8)]
    SETS = [(PS[0], PS[1]), (PS[2], PS[3])]

    def C(name, rows=P, lo=0, n=None):
        at, w = CONST[name]
        return const[0:rows, at + lo:at + (w if n is None else lo + n)]

    def vec(name, i=0, n=1):
        g, r, k = VEC[name]
        return vecs[:, g * P + r + i:g * P + r + i + n]

    def T(t, n=None):
        return arena[:, t, :] if n is None else arena[:, t:t + n, :]

    def flat(ap):
        return ap.rearrange("p a b -> p (a b)")

    ident = C("ident")

    def merged(n):
        return x[:, FT * n:FT * n + FT]

    def rotation(t):
        return T((16, 58)[t % 2], 4), T((20, 62)[t % 2], 4)

    def turned_level(n):
        return (GLA_LEVELS + (0, P))[n]

    GLA_STEPS = len(GLA_LEVELS) + 2

    def head_guess(n):
        return T((66, 48)[n], 4)

    def span(t, off, n):
        return arena[:, :, :].rearrange("p a b -> p (a b)")[:, t * S + off:t * S + off + n]

    def units(w):
        return w.rearrange("(q k p) n -> q p k n", p=P, k=UK)

    w_in, w_out, w_up, w_down = (units(a[n][0]) for n in ("w_in", "w_out", "w_up", "w_down"))
    w_in2, w_out2, w_ffn_in, w_ffn_out = (units(a[n][0]) for n in ("w_in_2", "w_out_2", "ffn_w_in_2", "ffn_w_out_2"))
    w_gate = a["w_gate_2"][0].rearrange("i (q k p) n -> i q p k n", p=P, k=UK)
    w_branch = a["w_branch_2"][0].rearrange("i (q k p) n -> i q p k n", p=P, k=UK)
    ada_w = a["ada_w_2"][0].rearrange("(k p) n -> k p n", p=P)

    NORMS = [(16, 1), (8, 1), (8, 1), (16, 1), (16, 0), (16, 1), (16, 0), (16, 1), (16, 0)]

    def before(n, what):
        return sum({"sq": k // 4, "normed": k * (i != 4), "hop": k * split}[what] for i, (k, split) in enumerate(NORMS[:n]))

    NORM_SQ = [0, 16, 32, 0, 0, 32, 16, 16, 16]
    NORM_T = [16, 0, 8, 16, None, 16, 32, 16, 32]

    def norm_bank(n):
        return PS[5 if n == 5 else 4][:, 0:S]

    def sq_count(n, g):
        if n in (4, 5):
            return before(4, "sq") + 2 * g + (n - 4) + 1
        return before(n, "sq") + g + 1

    FOLDED = [(0, 0), (0, 1), (0, 2), (0, 3), (3, 0), (3, 1), (3, 2), (3, 3), (4, 0), (5, 0), (4, 1), (5, 1),
              (6, 0), (6, 1), (6, 2), (8, 0), (8, 1)]

    block = ctx.enter_context(nc.Block())

    @block.sync
    def _(sp):
        def load_x(i):
            cols = slice(i * 512, (i + 1) * 512)
            sp.dma_start(flat(T(32, 16)).rearrange("p (t d) -> p t d", t=TT)[:, :, cols],
                         a["x"][0][:, cols].rearrange("(t p) d -> p t d", p=P)).then_inc(x_in[i], 16)

        load_x(0)
        sp.dma_start(const[:, 0:P], consts[:, 0:P]).then_inc(sem["ident_in"], 16)

        def load_vector(name, done):
            g, r, k = VEC[name]
            v = a[name]
            v = v if len(v.shape) == 1 else v[0]
            names = "abc"[:len(v.shape)]
            if len(names) > 1:
                v = v.rearrange(f"{' '.join(names)} -> ({' '.join(names)})")
            sp.dma_start(span(48, g * P, P)[r:r + k, :], v.rearrange("(r c) -> r c", c=P)).then_inc(done, 16)

        load_vector("norm_mix_g", sem["gain_in"])
        for i in range(1, 4):
            load_x(i)

        def load(R, j, src, cond=True):
            if cond:
                sp.wait_ge(sem["lo_ready"], R * 8 + (j - RAW + 1))
            sp.dma_start(w_raw[:, j % RAW], src).then_inc(raw_landed[j % RAW], 16)

        def ada(slots, j, g, col):
            for i, u in enumerate(slots):
                if u + ADA_AHEAD == j:
                    k = i % KT
                    more = (g if isinstance(g, int) else 1) + i // KT > 0 or k >= ADA_RING
                    if more:
                        sp.wait_ge(sem["ada_used"], (g + i // KT) * KT + (k - ADA_RING + 1))
                    sp.dma_start(span(ADA_SLOTS, (k % ADA_RING) * ADA_COLS, ADA_COLS),
                                 ada_w[k, :, col(i // KT)]).then_inc(ada_landed[k % ADA_RING], 16)

        def ada_cols(g):
            return lambda i: slice((g + i) * ADA_COLS, (g + i + 1) * ADA_COLS)

        for q in range(RAW):
            load(0, q, w_in[q, :, :, IN_ORDER[0] * COLS:(IN_ORDER[0] + 1) * COLS], cond=False)
        for name in VEC:
            if name != "norm_mix_g":
                load_vector(name, sem["vec_in"])
        sp.dma_start(const[:, P:], consts[:, P:]).then_inc(sem["const_in"], 16)
        for g in range(2):
            for j in range(4 * UA):
                if g == 0 and j < RAW:
                    continue
                ada(ADA_ONE if g else ADA_FIRST, j, G_IN + g, ada_cols(G_IN + g))
                c = IN_ORDER[4 * g + j // UA]
                load(R_IN + 4 * g, j, w_in[j % UA, :, :, c * COLS:(c + 1) * COLS])
        for j in range(4 * UA):
            ada(ADA_TWO, j, G_OUT, ada_cols(G_OUT))
            c, q = OUT_ORDER[j]
            load(R_OUT, j, w_out[q, :, :, c * COLS:(c + 1) * COLS])

        for q in range(UA):
            load(R_MLP, q, w_up[q, :, :, 0:COLS])
        with sp.Fori(0, MLP_SUPER // 2 - 1) as i:
            ada_col = sp.snap(i * ADA_COLS + G_MLP * ADA_COLS)
            cols = [sp.snap(i * (2 * COLS) + (1 + par) * COLS) for par in range(2)]
            rows = [sp.snap(i * (2 * UB) + k) for k in range(2 * UB)]
            for j in range(4 * UA):
                par, u = j // (2 * UA), j % (2 * UA)
                ada(ADA_ONE, j, i + G_MLP, lambda _: bass.ds(ada_col, ADA_COLS))
                if u < UA:
                    load(R_MLP + 1 + 4 * i, j, w_up[u, :, :, bass.ds(cols[par], COLS)])
                else:
                    n, k = (u - UA) // UB, (u - UA) % UB
                    load(R_MLP + 1 + 4 * i, j, w_down[bass.ds(rows[UB * par + k], 1), :, :, n * COLS:(n + 1) * COLS]
                         .rearrange("a p k n -> (a p) k n"))
        for j in range(3 * UA):
            g = G_MLP + MLP_SUPER // 2 - 1
            ada(ADA_TAIL, j, g, ada_cols(g))
            if j < UA:
                load(R_IN2 - 3, j, w_up[j, :, :, (MLP_SUPER - 1) * COLS:])
            else:
                c, n, k = MLP_SUPER - 3 + j // UA, j % UA // UB, j % UB
                load(R_IN2 - 3, j, w_down[UB * c + k, :, :, n * COLS:(n + 1) * COLS])

        for c in range(12):
            for q in range(UA):
                ada(ADA_ONE, UA * c + q, G_IN2, ada_cols(G_IN2))
                if c == 3:
                    sp.wait_ge(sem["lo_ready"], (R_IN2 + 3) * 8 + q - RAW + 1)
                    for at, col in ((0, COL_GATES), (32, COL_GATES + BR_HEADS)):
                        sp.dma_start(w_raw[:, q % RAW, :, at:at + BR_HEADS],
                                     w_in2[q, :, :, col:col + BR_HEADS]).then_inc(sem["small_w_in"], 16)
                    sp.dma_start(w_raw[:, q % RAW, :, 64:64 + GLA_RANK],
                                 w_in2[q, :, :, COL_GLA_A:COL_GLA_A + GLA_RANK]).then_inc(raw_landed[q % RAW], 16)
                else:
                    col = c * COLS if c < 3 else (c - 1) * COLS if c < 8 else COL_GLA + (c - 8) * COLS
                    col = COL_S5 if c == 11 else col
                    load(R_IN2 + c, q, w_in2[q, :, :, col:col + COLS])

        for i in range(4):
            for j in range(40):
                if i == 3:
                    ada(ADA_GATE, j, G_GATE, ada_cols(G_GATE))
                n, q = j // 10, j % 10
                w = w_gate[i, q] if q < UA else w_branch[i, q - UA]
                load(R_GATE + 5 * i, j, w[:, :, n * COLS:(n + 1) * COLS])
        for j in range(4 * UA):
            ada(ADA_ONE, j, G_OUT2, ada_cols(G_OUT2))
            load(R_OUT2, j, w_out2[j % UA, :, :, (j // UA) * COLS:(j // UA + 1) * COLS])

        for q in range(2 * UA):
            col = 0 if q < UA else FFN
            load(R_FFN, q, w_ffn_in[q % UA, :, :, col:col + COLS])
        with sp.Fori(0, FFN_SUPER - 1) as c:
            ca = sp.snap(c * COLS + COLS)
            cg = sp.snap(c * COLS + (FFN + COLS))
            rows = [sp.snap(c * UB + k) for k in range(UB)]
            for q in range(2 * UA):
                load(R_FFN + 2 + 3 * c, q, w_ffn_in[q % UA, :, :, bass.ds(ca if q < UA else cg, COLS)])
            for n in range(4):
                for k in range(UB):
                    load(R_FFN + 2 + 3 * c, 2 * UA + UB * n + k,
                         w_ffn_out[bass.ds(rows[k], 1), :, :, n * COLS:(n + 1) * COLS].rearrange("a p k n -> (a p) k n"))
        for n in range(4):
            for k in range(UB):
                load(R_FFN + 3 * FFN_SUPER - 1, UB * n + k, w_ffn_out[UB * (FFN_SUPER - 1) + k, :, :, n * COLS:(n + 1) * COLS])

        for b in range(8):
            k0, t = b // 2, b % 2
            sp.wait_ge(sem["out_copied"], b + 1)
            sp.dma_start(out[0, t * P:(t + 1) * P, k0 * 512:(k0 + 1) * 512], span(48, b * 512, 512)).then_inc(sem["stored"], 16)
        sp.wait_ge(sem["stored"], 16 * 8)

    @block.tensor
    def _(pe):
        def mm(o, w, r, start=True, stop=True):
            return nc.tensor.matmul(o, w, r, start=start, stop=stop, skip_group_check=True)

        def unit(R, j, s, hi, lo, k0, first, last, ftiles=FT):
            pe.wait_ge(sem["lo_ready"], R * 8 + (j + 1))
            slot = j % LEAD
            for f in range(ftiles):
                o = SETS[s][f // 2][:, (f % 2) * S:(f % 2 + 1) * S]
                cols = slice(f * P, (f + 1) * P)
                for k in range(UK):
                    mm(o, w_hi[:, slot, k, cols], hi[:, k0 + k], start=first and k == 0 and f % 2 == 0, stop=False)
                    mm(o, w_hi[:, slot, k, cols], lo[:, k0 + k], start=False, stop=False)
                    m = mm(o, w_lo[:, slot, k, cols], hi[:, k0 + k], start=False, stop=last and k == UK - 1)
            m.then_inc(sem["unit_done"], 1)

        def chunk(R, j0, H, s, hi=hop_hi, lo=hop_lo, nu=UA, ftiles=FT, ready=None, between=None):
            pe.wait_ge(drained[s], H + 1)
            for q in range(nu):
                if ready:
                    ready(q)
                unit(R, j0 + q, s, hi, lo, UK * q, q == 0, q == nu - 1, ftiles)
                if between:
                    between(j0 + q)

        def norm_sum(n, groups):
            tiles = NORMS[n][0]
            sq = T(NORM_SQ[n], tiles)
            for g in groups:
                if (n, g) in FOLDED:
                    pe.wait_ge(sem["sq_folded"], FOLDED.index((n, g)) + 1)
                    ks = [4 * g]
                else:
                    pe.wait_ge(sem["sq_ready"], sq_count(n, g))
                    ks = range(4 * g, 4 * g + 4)
                for k in ks:
                    m = mm(norm_bank(n), ones[:], sq[:, k], start=k == 0, stop=4 * g + 4 == tiles and k == ks[-1])
            if 4 * groups[-1] + 4 == tiles:
                m.then_inc(sem["sum_ready"], 1)

        def normed(n):
            return lambda q: pe.wait_ge(sem["hop_ready"], before(n + 1, "hop") - KT + UK * (q + 1))

        def scores(o, q, k):
            mm(o[:, 0:P], q[:, 0:P], k[:, 0:P])
            return mm(o[:, P:CW], q[:, P:S], k[:, 0:S])

        def turn_probs(o, p):
            for b in range(3):
                m = nc.tensor.transpose(o[:, b * P:(b + 1) * P], p[:, b * P:(b + 1) * P], ident)
            return m

        def weighted_values(o, v, pt):
            mm(o[:, 0:S], v[:, 0:P], pt[:, 0:S], stop=False)
            return mm(o[:, P:S], v[:, P:S], pt[:, S:CW], start=False)

        def turn_pair(o, src):
            nc.tensor.transpose(o[:, 0:P], src[:, 0:P], ident)
            return nc.tensor.transpose(o[:, P:S], src[:, P:S], ident)

        pe.wait_ge(sem["ident_in"], 16)
        pe.wait_ge(sem["gain_in"], 16)
        nc.tensor.transpose(PS[0][:, 0:KT], span(48, 0, P)[0:KT, :], ident[0:KT, 0:KT]).then_inc(sem["gain_turned"], 1)
        for b in range(KT // 2):
            if b % 2 == 0:
                pe.wait_ge(x_in[b // 2], 16)
            if b >= 4:
                pe.wait_ge(sem["x_copied"], b - 3)
            for k in range(2):
                for t in range(TT):
                    m = nc.tensor.transpose(PS[4 + b % 4][:, (k * TT + t) * P:(k * TT + t + 1) * P],
                                            span(32, t * D + (2 * b + k) * P, P), ident)
            m.then_inc(sem["x_turned"], 1)
        def modulation(used):
            pe.wait_ge(sem["ada_used"], used)
            for f in range(ADA_F):
                m = mm(PS[7][:, f:f + 1], span(ADA_ACC, f * P, P), ones[:, 0:1])
            m.then_inc(sem["mod_psum"], 1)

        def stored(p):
            pe.wait_ge(drained[p % 2], H_IN + p // 2 + 2)

        def pool_product(groups, banks):
            pool_w = T(32, 8)
            pe.wait_ge(sem["pool_w_in"], 16)
            for g, bank in zip(groups, banks):
                pe.wait_ge(sem["pooled"], POOL_ORDER.index(g) + 1)
                for f in range(2):
                    for c in range(2):
                        m = mm(PS[bank][:, f * S:(f + 1) * S], pool_w[:, 2 * g + c, f * P:(f + 1) * P], T(2 * g + c),
                               start=c == 0 and f == 0, stop=c == 1)
                m.then_inc(sem["pool_psum"], 1)

        def first_mixer(u):
            if u == 2:
                pe.wait_ge(sem["vec_in"], 16 * N_VEC_DMAS)
                pe.wait_ge(sem["x_copied"], 8)
                for g, rows in enumerate(VEC_ROWS):
                    m = nc.tensor.transpose(PS[7][:, g * P:g * P + rows], span(48, g * P, P)[0:rows, :],
                                            ident[0:rows, 0:rows])
                m.then_inc(sem["vec_turned"], 1)
            if u == 5:
                norm_sum(0, range(4))
            if u == 7:
                pe.wait_ge(sem["var_ready"], 1)
                pe.wait_ge(sem["vecs_ready"], 1)
                pe.wait_ge(sem["const_in"], 16)
                pe.wait_ge(sem["bias_rows_ready"], 1)
                for h in range(BR_HEADS):
                    m = mm(PS[4 + h][:, 0:384], span(50, h * P, P)[BROWS, :], C("rowsel", n=384)[BROWS, :])
                m.then_inc(sem["bias_psum"], 1)
            for g in range(2):
                if u == (27, 57)[g]:
                    if g == 0:
                        pe.wait_ge(sem["bias_copied"], 1)
                    else:
                        pe.wait_ge(sem["a_out"], HEADS // 2)
                    modulation((G_IN + g + 1) * KT)
            for h in range(HEADS):
                if u == SCORES_AT[h]:
                    for p in ((0, 1, 2) if h == 0 else (3, 4) if h == 4 else ()):
                        stored(p)
                    if h >= 1:
                        pe.wait_ge(sem["a_masked"], h)
                    scores(PS[4], T(8 + h), T(16 + h)).then_inc(sem["a_scores"], 1)
                    if h < HEADS // 2:
                        if h >= 1:
                            pe.wait_ge(sem["a_vT"], h)
                        turn_pair(PS[5], T(24 + h)).then_inc(sem["a_vT_psum"], 1)
                if u == SCORES_AT[h] + TURN_LATER:
                    pe.wait_ge(sem["a_probs"], h + 1)
                    if h >= 1:
                        pe.wait_ge(sem["a_probsT"], h)
                    turn_probs(PS[6], span(46, CW * (h % 2), CW)).then_inc(sem["a_probsT_psum"], 1)
                if h < HEADS // 2 and u == SCORES_AT[h] + TURN_LATER + 1:
                    pe.wait_ge(sem["a_probsT"], h + 1)
                    pe.wait_ge(sem["a_vT"], h + 1)
                    if h == 0:
                        pe.wait_ge(sem["mod_ready"], G_IN + 1)
                    else:
                        pe.wait_ge(sem["a_out"], h)
                    weighted_values(PS[7], T(24 + h), span(49, CW * h, CW)).then_inc(sem["a_out_psum"], 1)
            if u == 57:
                pe.wait_ge(sem["a_masked"], HEADS)
                pe.wait_ge(sem["a_vT"], HEADS // 2)
                pool_product(POOL_ORDER[0:2], (4, 5))
            if u == 59:
                pe.wait_ge(sem["a_probsT"], HEADS)
                pe.wait_ge(sem["mod_ready"], G_IN + 2)
                pool_product(POOL_ORDER[2:4], (6, 7))
            if u == 61:
                pe.wait_ge(sem["pool_ready"], 4)
                norm_sum(1, range(2))

        for p in range(8):
            chunk(R_IN, UA * p, H_IN + p // 2, p % 2, ready=normed(0) if p == 0 else None, between=first_mixer)

        def last_heads(u):
            pairs = (5, 6)
            if u == 0:
                stored(7)
                for i, bank in enumerate(pairs):
                    for h in range(2):
                        m = turn_pair(PS[bank][:, h * S:(h + 1) * S], T(28 + 2 * i + h))
                    m.then_inc(sem["a_vT_psum"], 1)
            if u in (1, 2):
                i = u - 1
                pe.wait_ge(sem["a_vT"], HEADS // 2 + (1 if i == 0 else 2))
                for h in range(2):
                    g = 2 * i + h
                    m = weighted_values(PS[(7, 5)[i]][:, h * S:(h + 1) * S], T(28 + g), span(49, CW * g, CW))
                m.then_inc(sem["a_out_psum"], 1)
            if u == 3:
                norm_sum(2, range(2))
            for c in range(3):
                if u == OUT_LAST[c] + 5:
                    norm_sum(3, [c])
            for g in range(2):
                if u == 16 * g + 15:
                    if g == 0:
                        pe.wait_ge(sem["a_out"], HEADS // 2 + 1)
                    modulation((G_OUT + g + 1) * KT)

        for j, (c, q) in enumerate(OUT_ORDER):
            if q == 0:
                pe.wait_ge(drained[c % 2], H_OUT + c // 2 + 1)
            if c == 0:
                normed(2)(q)
            unit(R_OUT, j, c % 2, hop_hi, hop_lo, UK * q, q == 0, q == UA - 1)
            last_heads(j)

        def down(R, j0, H, s0, par, ready, between=None):
            pe.wait_ge(sem["hid_ready"], ready)
            for n in range(4):
                s = (s0 + n) % 2
                chunk(R, j0 + UB * n, H + (s0 + n) // 2, s, hid_hi[:, par], hid_lo[:, par], UB, between=between)

        def last_sum(u):
            if u == 4:
                norm_sum(3, [3])

        chunk(R_MLP, 0, H_MLP, 0, ready=normed(3), between=last_sum)
        with pe.Fori(0, MLP_SUPER // 2 - 1) as i:
            R, H = R_MLP + 1 + 4 * i, H_MLP + 5 * i

            def group_sum(u):
                if u == 26:
                    modulation((i + (G_MLP + 1)) * KT)

            chunk(R, 0, H, 1)
            down(R, 8, H + 1, 0, 0, 2 * i + 1)
            chunk(R, 16, H + 3, 0)
            down(R, 24, H + 3, 1, 1, 2 * i + 2, between=group_sum)
        R, H = R_MLP + 29, H_MLP + 35
        chunk(R, 0, H, 1)
        down(R, 8, H + 1, 0, 0, MLP_SUPER - 1)

        def chunk_sums(norms, at):
            def steps(u):
                if u == at + 4 * UB - 1:
                    for n in norms:
                        norm_sum(n, range(3))
            return steps

        down(R, 16, H + 3, 0, 1, MLP_SUPER, between=chunk_sums((4, 5), 16))
        modulation((G_MLP + MLP_SUPER // 2) * KT)

        norm_sum(4, [3])
        norm_sum(5, [3])
        for c in range(4):
            chunk(R_IN2, UA * c, H_IN2 + c // 2, c % 2, ftiles=1 if c == 3 else FT, ready=normed(5) if c == 0 else None)
        modulation((G_IN2 + 1) * KT)

        def attention_steps(h):
            def steps(u):
                q = u % UA
                if q == 0:
                    for c in range(2):
                        pe.wait_ge(drained[c], H_IN2 + 3 - c)
                    if h >= 1:
                        pe.wait_ge(sem["d_masked"], 2 * h)
                    for m in range(2):
                        scores(PS[4 + m], T(h)[64 * m:64 * m + 64], T(4 + h)[64 * m:64 * m + 64]).then_inc(sem["d_scores"], 1)
                    if h >= 1:
                        pe.wait_ge(sem["d_out"], h)
                    turn_pair(PS[6][:, 0:S], T(8 + h)).then_inc(sem["d_vT_psum"], 1)
                if q == 3 and h == 3:
                    pe.wait_ge(sem["m_rows"], 1)
                    pe.wait_ge(sem["d_probsT"], h)
                    for t in range(TT):
                        m = mm(PS[7][:, CW + t * BR_HEADS:CW + (t + 1) * BR_HEADS], span(43, t * P, P)[0:BR_HEADS, :],
                               ident[0:BR_HEADS, 0:BR_HEADS])
                    m.then_inc(sem["m_BT"], 1)
                if q == 5:
                    if h == 0:
                        pe.wait_ge(sem["mod_ready"], G_IN2 + 1)
                    elif h < 3:
                        pe.wait_ge(sem["d_probsT"], h)
                    else:
                        pe.wait_ge(sem["m_rows"], 2)
                    pe.wait_ge(sem["d_probs"], h + 1)
                    turn_probs(PS[7], span(37, 0, CW)).then_inc(sem["d_probsT_psum"], 1)
                if q == 6:
                    pe.wait_ge(sem["d_probsT"], h + 1)
                    pe.wait_ge(sem["d_vT"], h + 1)
                    if h >= 1:
                        pe.wait_ge(sem["d_out"], h)
                    weighted_values(PS[6][:, S:2 * S], T(8 + h), span(37, CW, CW)).then_inc(sem["d_out_psum"], 1)
            return steps

        for h in range(BR_HEADS):
            c = 4 + h
            chunk(R_IN2, UA * c, H_IN2 + c // 2, c % 2, between=attention_steps(h))

        def head_norm(n):
            pe.wait_ge(sem["hn_sq"], n + 1)
            for b in range(2):
                m = mm(PS[6 + b][:, :], ones[:], flat(T((34, 44)[n] + 2 * b, 2)))
            m.then_inc(sem["hn_sum"], 1)

        def mlstm_steps(h):
            def steps(u):
                q = u % UA
                if h == 0 and q == 0:
                    head_norm(0)
                if h == 0 and q == 1:
                    pe.wait_ge(sem["d_masked"], 2 * BR_HEADS)
                    for t in range(2):
                        m = mm(PS[4][:, t * S:(t + 1) * S], wa2[:, t * P:(t + 1) * P], gla_a, start=t == 0)
                    m.then_inc(sem["g_z_psum"], 1)
                if q == 2:
                    if h == 0:
                        pe.wait_ge(sem["g_z"], 1)
                        pe.wait_ge(sem["hn_var"], 1)
                        pe.wait_ge(sem["m_silu"], 1)
                    else:
                        pe.wait_ge(sem["m_A"], h)
                        pe.wait_ge(sem["m_S"], h)
                        pe.wait_ge(sem["m_out"], h)
                    mm(PS[4][:, 0:S], C("rowsel", BR_HEADS, h * P, P), T(40)[0:BR_HEADS, :]).then_inc(sem["m_bc"], 1)
                    scores(PS[5], T(44 + h), T(48 + h)).then_inc(sem["m_qk"], 1)
                    turn_pair(PS[6][:, 0:S], T(20 + h)).then_inc(sem["m_vT_psum"], 1)
                if q == 6:
                    pe.wait_ge(sem["m_S"], h + 1)
                    if h >= 1:
                        pe.wait_ge(sem["m_ST"], h)
                    turn_probs(PS[7], span(52, 0, CW)).then_inc(sem["m_ST_psum"], 1)
                if q == 7:
                    pe.wait_ge(sem["m_ST"], h + 1)
                    pe.wait_ge(sem["m_vT"], h + 1)
                    if h >= 1:
                        pe.wait_ge(sem["m_out"], h)
                    weighted_values(PS[6][:, S:2 * S], T(20 + h), span(52, CW, CW)).then_inc(sem["m_out_psum"], 1)
            return steps

        for h in range(BR_HEADS):
            c = 8 + h
            chunk(R_IN2, UA * c, H_IN2 + c // 2, c % 2, between=mlstm_steps(h))

        def gla_steps(u):
            if u == 0:
                pe.wait_ge(sem["m_out"], BR_HEADS)
                pe.wait_ge(sem["m_ST"], BR_HEADS)
                for h in range(BR_HEADS):
                    m = turn_pair(PS[6 + h // 2][:, (h % 2) * S:(h % 2 + 1) * S], T(32 + h))
                m.then_inc(sem["g_vT_psum"], 1)
            if u % 4 == 2 and u // 4 < GLA_STEPS:
                n = u // 4
                level = turned_level(n)
                if level:
                    pe.wait_ge(sem["g_qk"], n + 1 if level < P else GLA_STEPS - 1)
                if n >= 1:
                    pe.wait_ge(sem["g_att_read"], n)
                q0, k0 = (28, 30) if level == 0 else (44, 46)
                for h in range(BR_HEADS):
                    rows = slice(64 * (h % 2), 64 * (h % 2) + 64)
                    q, k = T(q0 + h // 2)[rows], T(k0 + h // 2)[rows]
                    o = PS[4 + h % 2]
                    if level == P:
                        m = mm(o[:, (h // 2) * P:(h // 2 + 1) * P], k[:, 0:P], q[:, P:S])
                    else:
                        for t in range(TT):
                            m = mm(o[:, (h // 2) * S + t * P:(h // 2) * S + (t + 1) * P],
                                   k[:, t * P:(t + 1) * P], q[:, t * P:(t + 1) * P])
                m.then_inc(sem["g_att_psum"], 1)
            if u == 36:
                pe.wait_ge(sem["g_att"], 1)
                pe.wait_ge(sem["g_x_copied"], 1)
                pe.wait_ge(sem["g_vT"], 1)
                for h in range(BR_HEADS):
                    o = PS[6 + h // 2][:, (h % 2) * S:(h % 2 + 1) * S]
                    att = span(48 + 2 * (h % 2), (h // 2) * S, S)
                    v = T(32 + h)
                    mm(o[:, 0:P], v[:, 0:P], att[:, 0:P], start=h % 2 == 0)
                    mm(o[:, P:S], v[:, 0:P], span(54, h * P, P), start=False, stop=False)
                    m = mm(o[:, P:S], v[:, P:S], att[:, P:S], start=False)
                m.then_inc(sem["g_out_psum"], 1)
            if u == 38:
                head_norm(1)

        def s5_steps(t, u):
            if u == 1:
                pe.wait_ge(sem["s_pad"], t + 1)
                if t == 0:
                    pe.wait_ge(sem["g_x_copied"], 1)
                else:
                    pe.wait_ge(sem["s_CT"], t)
                for part in range(2):
                    for ii in range(4):
                        m = nc.tensor.transpose(PS[4 + part][:, ii * P:(ii + 1) * P], span(52 + 2 * part, ii * P, P), ident)
                m.then_inc(sem["s_turned"], 1)
            if u == 3:
                pe.wait_ge(sem["s_BT"], t + 1)
                if t == 0:
                    pe.wait_ge(sem["hn_var"], 2)
                else:
                    pe.wait_ge(sem["s_y"], t)
                for part in range(2):
                    for ii in range(4):
                        m = mm(PS[6 - 2 * part + ii // 2][:, (ii % 2) * S:(ii % 2 + 1) * S], span(44 + 2 * part, ii * P, P),
                               T(40 + t), start=ii % 2 == 0)
                m.then_inc(sem["s_bu_psum"], 1)
            if u == 6:
                pe.wait_ge(sem["s_cpad"], t + 1)
                pe.wait_ge(sem["s_bu"], t + 1)
                for part in range(2):
                    for ii in range(4):
                        m = nc.tensor.transpose(PS[4 + part][:, ii * P:(ii + 1) * P], span(66 + 2 * part, ii * P, P), ident)
                m.then_inc(sem["s_cturned"], 1)
            if u == 19:
                pe.wait_ge(sem["s_CT"], t + 1)
                pe.wait_ge(sem["s_x"], t + 1)
                for part in range(2):
                    for ii in range(4):
                        m = mm(PS[6][:, 0:S], span(48 + 2 * part, ii * P, P), T(32 + 4 * part + ii),
                               start=part == 0 and ii == 0, stop=part == 1 and ii == 3)
                m.then_inc(sem["s_y_psum"], 1)

        def last_steps(u):
            if u == 2:
                pe.wait_ge(sem["s_z"], 1)
                pe.wait_ge(sem["glu_w_in"], 16)
                glu = flat(T(16, 8)).rearrange("p (k n) -> p k n", k=4)
                for f in range(4):
                    for k in range(4):
                        m = mm(PS[4 + f // 2][:, (f % 2) * S:(f % 2 + 1) * S], glu[:, k, f * P:(f + 1) * P], T(24 + k),
                               start=f % 2 == 0 and k == 0, stop=k == 3)
                m.then_inc(sem["s_glu_psum"], 1)
            for g in range(2):
                if u == ADA_GATE[KT * g + KT - 1] + 2:
                    modulation((G_GATE + g + 1) * KT)

        for i in range(4):
            R, H = R_GATE + 5 * i, H_GATE + 4 * i
            steps = (gla_steps, lambda u: s5_steps(u // 20, u % 20), lambda u: s5_steps(2 + u // 20, u % 20), last_steps)[i]
            for n in range(4):
                chunk(R, 10 * n, H + n, 0, between=steps)
                if n == 0:
                    pe.wait_ge(sem["hid_ready"], i + (MLP_SUPER + 1))
                chunk(R, 10 * n + UA, H + n, 1, hid_hi[:, 0], hid_lo[:, 0], UB, between=steps)

        def mix_sums(u):
            if u == 26:
                modulation((G_OUT2 + 1) * KT)
            for c in range(3):
                if u == UA * (c + 1) + 2:
                    norm_sum(6, [c])

        def merged_split(q):
            pe.wait_ge(sem["merged_ready"], q // 2 + 1)

        for c in range(4):
            chunk(R_OUT2, UA * c, H_OUT2 + c // 2, c % 2, ready=merged_split if c == 0 else None, between=mix_sums)
        norm_sum(6, [3])
        norm_sum(7, range(4))

        base = MLP_SUPER + 4
        for s in range(2):
            chunk(R_FFN, UA * s, H_FFN, s, ready=normed(7) if s == 0 else None)
        with pe.Fori(0, FFN_SUPER // 2) as i:
            R, H = R_FFN + 2 + 6 * i, H_FFN + 1 + 6 * i
            for par in range(2):
                for s in range(2):
                    chunk(R, 24 * par + UA * s, H + 3 * par, s)
                down(R, 24 * par + 16, H + 3 * par + 1, 0, par, 2 * i + (base + par + 1))
        R, H = R_FFN + 2 + 3 * (FFN_SUPER - 1), H_FFN + 1 + 3 * (FFN_SUPER - 1)
        down(R, 0, H, 0, (FFN_SUPER - 1) % 2, base + FFN_SUPER, between=chunk_sums((8,), 0))
        norm_sum(8, [3])

        for b in range(8):
            k0, t = 4 * (b // 2), b % 2
            if t == 0:
                pe.wait_ge(sem["res_ready"], 4 + b // 2 + 1)
            if b >= 4:
                pe.wait_ge(sem["out_copied"], b - 3)
            for k in range(4):
                m = nc.tensor.transpose(PS[b % 4][:, k * P:(k + 1) * P], x[:, k0 + k, t * P:(t + 1) * P], ident)
            m.then_inc(sem["out_psum"], 1)

    @block.scalar
    def _(act):
        def copy(o, i, scale=1.0):
            return nc.scalar.activation(o, i, ACT.Copy, scale=scale)

        def split(R, j, first=False, cols=COLS):
            act.wait_ge(raw_landed[j % RAW], (R * (8 // RAW) + j // RAW) * 16 + 16)
            if not first:
                act.wait_ge(sem["unit_done"], R * 8 + (j - LEAD + 1))
            copy(w_hi[:, j % LEAD, :, 0:cols], w_raw[:, j % RAW, :, 0:cols]).then_inc(sem["hi_ready"], 1)

        def halves(ap):
            return ap.rearrange("p (a b) -> p a b", a=2)

        def store_chunk(s, tile):
            for b in range(2):
                m = copy(arena[:, tile(2 * b), :], halves(SETS[s][b][:]))
            m.then_inc(drained[s], 1)

        def squares(n, g, src):
            nc.scalar.activation(T(NORM_SQ[n] + 4 * g, 4), src(4 * g, 4), ACT.Square).then_inc(sem["sq_ready"], 1)

        chained = [0]

        def then(ins):
            chained[0] += 1
            ins.then_inc(sem["act_chain"], 1)
            act.wait_ge(sem["act_chain"], chained[0])

        def inverse_root(o, v):
            return nc.scalar.activation(o, v, ACT.Abs_reciprocal_sqrt)

        def norm(n, bias=None):
            tiles, is_split = NORMS[n]
            guess(n)
            if is_split:
                dst = 8 if n == 2 else 0
                for k in range(tiles):
                    act.wait_ge(sem["normed"], before(n, "normed") + k + 1)
                    t = T(NORM_T[n] + k)
                    if bias is None:
                        m = copy(hop_hi[:, dst + k], t)
                    else:
                        m = nc.scalar.activation(hop_hi[:, dst + k], t, ACT.Identity, bias=bias(k))
                    m.then_inc(sem["hop_hi"], 1)

        def of_x(k, n):
            return x[:, k:k + n]

        def of_arena(t):
            return lambda k, n: T(t + k, n)

        def hi_pair(n, b):
            act.wait_ge(sem["normed"], before(n, "normed") + 2 * (b + 1))
            copy(hop_hi[:, 2 * b:2 * b + 2], T(NORM_T[n] + 2 * b, 2)).then_inc(sem["hop_hi"], 2)

        def guess(n):
            act.wait_ge(sem["var_ready"], n + 1)
            inverse_root(std[:], var[:]).then_inc(sem["std_ready"], 1)

        for b in range(KT // 2):
            act.wait_ge(sem["x_turned"], b + 1)
            copy(x[:, 2 * b:2 * b + 2], halves(PS[4 + b % 4][:])).then_inc(sem["x_copied"], 1)
            if b >= 1:
                hi_pair(0, b - 1)
            if b >= 4:
                split(0, b - 4, first=True)
        hi_pair(0, KT // 2 - 1)

        def first_mixer(u):
            if u == 2:
                act.wait_ge(sem["vec_turned"], 1)
                for g, rows in enumerate(VEC_ROWS):
                    m = copy(vecs[:, g * P:g * P + rows], PS[7][:, g * P:g * P + rows])
                m.then_inc(sem["vecs_ready"], 1)
                act.wait_ge(sem["vecs_ready"], 1)
                nc.scalar.activation(cs[:], vec("c_2", 0, KT), ACT.Silu).then_inc(sem["cs_ready"], 1)
            if u == 6:
                guess(0)
            if u == 7:
                act.wait_ge(sem["bias_psum"], 1)
                for h in range(BR_HEADS):
                    m = copy(span(32, h * 384, 384), PS[4 + h][:, 0:384])
                m.then_inc(sem["bias_copied"], 1)
                act.wait_ge(sem["lam_sums"], 1)
                nc.scalar.activation(lam_s[:, 2:4], lam_s[:, 0:2], ACT.Exp).then_inc(sem["lam_exps"], 1)
            for h in range(HEADS):
                if h < HEADS // 2 and u == SCORES_AT[h]:
                    act.wait_ge(sem["a_vT_psum"], h + 1)
                    copy(T(24 + h), PS[5][:, 0:S]).then_inc(sem["a_vT"], 1)
                if u == SCORES_AT[h] + 1:
                    act.wait_ge(sem["a_negmax"], h + 1)
                    e = span(46, CW * (h % 2), CW)
                    for qt, cols in enumerate((slice(0, P), slice(P, CW))):
                        m = nc.scalar.activation(e[:, cols], e[:, cols], ACT.Exp, scale=A_SCALE,
                                                 bias=st[:, h % 2, 2 + qt:3 + qt])
                    m.then_inc(sem["a_exp"], 1)
                if u == SCORES_AT[h] + TURN_LATER:
                    act.wait_ge(sem["a_probsT_psum"], h + 1)
                    if h >= HEADS // 2:
                        act.wait_ge(sem["a_out_psum"], h - HEADS // 2 + 1)
                    copy(span(49, CW * (h % 4), CW), PS[6][:, 0:CW]).then_inc(sem["a_probsT"], 1)
                if h < HEADS // 2 and u == SCORES_AT[h] + TURN_LATER + 1:
                    act.wait_ge(sem["a_out_psum"], h + 1)
                    copy(T(8 + h), PS[7][:, 0:S]).then_inc(sem["a_out"], 1)
            for i, first in enumerate((0, 2)):
                if u == (57, 59)[i]:
                    for g, bank in zip(POOL_ORDER[first:first + 2], ((4, 5), (6, 7))[i]):
                        act.wait_ge(sem["pool_psum"], POOL_ORDER.index(g) + 1)
                        for f in range(2):
                            m = nc.scalar.activation(T(2 * g + f), PS[bank][:, f * S:(f + 1) * S], ACT.Copy,
                                                     scale=vec("pool_scale", 2 * g + f))
                        m.then_inc(sem["pool_ready"], 1)
            if u == 60:
                act.wait_ge(sem["pool_ready"], 4)
                for g in range(2):
                    squares(1, g, of_arena(0))

        for j in range(8 * UA):
            split(R_IN, j + LEAD)
            first_mixer(j)
            if j == 61:
                norm(1)

        for j in range(4 * UA):
            split(R_OUT, j + LEAD)
            if j == 0:
                for i in range(2):
                    act.wait_ge(sem["a_vT_psum"], HEADS // 2 + i + 1)
                    copy(T(28 + 2 * i, 2), halves(PS[5 + i][:])).then_inc(sem["a_vT"], 1)
                act.wait_ge(sem["a_out"], HEADS // 2)
                squares(2, 0, of_arena(8))
            if j in (1, 2):
                act.wait_ge(sem["a_out_psum"], HEADS // 2 + j)
                copy(T(10 + 2 * j, 2), halves(PS[(7, 5)[j - 1]][:])).then_inc(sem["a_out"], 1)
            if j == 2:
                act.wait_ge(sem["a_out"], HEADS // 2 + 2)
                squares(2, 1, of_arena(8))
            if j == 3:
                norm(2)
            for c in range(3):
                if j == OUT_LAST[c] + 1:
                    act.wait_ge(drained[c % 2], H_OUT + c // 2 + 2)
                    squares(3, c, of_x)

        for b in range(KT // 2):
            hi_pair(3, b)
        act.wait_ge(drained[1], H_MLP + 1)
        squares(3, 3, of_x)

        def relu(s):
            for b in range(2):
                m = nc.scalar.activation(T(2 * b, 2), halves(SETS[s][b][:]), ACT.Relu)
            m.then_inc(drained[s], 1)

        def hidden_hi(par, sig, count, tile):
            act.wait_ge(sig, count)
            copy(hid_hi[:, par], T(tile, FT)).then_inc(sem["hid_hi"], 1)

        for j in range(UA):
            split(R_MLP, j + LEAD)
            if j == 5:
                guess(3)
        relu(0)
        hidden_hi(0, sem["relu_sq"], 1, 4)
        with act.Fori(0, MLP_SUPER // 2 - 1) as i:
            for j in range(4 * UA):
                split(R_MLP + 1 + 4 * i, j + LEAD)
                if j in (7, 23):
                    relu(1 if j == 7 else 0)
                if j in (8, 24):
                    hidden_hi(1 if j == 8 else 0, sem["relu_sq"], 2 * i + (2 if j == 8 else 3), 4)
        def both_squares(c):
            act.wait_ge(drained[c % 2], H_IN2 - 2 + c // 2 + 2)
            squares(4, c, of_x)
            for k in range(4 * c, 4 * c + 4):
                m = nc.scalar.activation(T(NORM_SQ[5] + k), x[:, k], ACT.Square, scale=vec("norm_final_g", k))
            m.then_inc(sem["sq_ready"], 1)

        for j in range(3 * UA):
            split(R_MLP + 29, j + LEAD)
            if j == 7:
                relu(1)
            if j == 8:
                hidden_hi(1, sem["relu_sq"], MLP_SUPER, 4)
            if j in (18, 20, 22):
                both_squares((j - 18) // 2)

        both_squares(3)
        act.wait_ge(sem["var_ready"], 5)
        inverse_root(T(53), T(54)).then_inc(sem["std_ready"], 1)
        norm(5, lambda k: mod[:, k:k + 1])

        def narrow_wait(c, q):
            if (c, q) in ((3, 0), (3, RAW)):
                act.wait_ge(sem["small_w_in"], 16 * 2 * (q + RAW))

        def projection_unit(c, q):
            ahead = (UA * c + q + LEAD) // UA
            if ahead == 3:
                narrow_wait(ahead, (q + LEAD) % UA)
            split(R_IN2, UA * c + q + LEAD, cols=P if ahead == 3 else COLS)

        tiles_of = [0, 4, 8, None, 12, 16, 20, 24, 28, 32, 36, 40]
        DT, MAG, THR, SIN, HALF = 0, 1, 2, 3, 4
        for c in range(4):
            for q in range(UA):
                projection_unit(c, q)
                if (c, q) == (0, 1):
                    act.wait_ge(sem["small_in"], 16 * N_SMALL)
                    nc.scalar.activation(s5v[:, DT], s5v[:, 15], ACT.Exp).then_inc(sem["s_dt"], 1)
                if (c, q) == (0, 4):
                    act.wait_ge(sem["s_trig"], 1)
                    nc.scalar.activation(s5v[:, MAG], s5v[:, MAG], ACT.Exp).then_inc(sem["s_exp"], 1)
                    nc.scalar.activation(s5v[:, SIN], s5v[:, THR], ACT.Sin)
                    nc.scalar.activation(s5v[:, HALF], s5v[:, THR], ACT.Sin, scale=0.5).then_inc(sem["s_sin"], 1)
            if c < 3:
                store_chunk(c % 2, lambda o: slice(tiles_of[c] + o, tiles_of[c] + o + 2))
        narrow = SETS[1][0]
        copy(gate_rows[:, 0, :], narrow[0:BR_HEADS, 0:S])
        copy(gate_rows[:, 1, :], narrow[32:32 + BR_HEADS, 0:S])
        copy(gla_a, narrow[64:64 + GLA_RANK, 0:S]).then_inc(drained[1], 1)
        act.wait_ge(drained[1], H_IN2 + 3)
        act.sem_inc(sem["gates_ready"], 1)

        rows = BR_HEADS
        for h in range(BR_HEADS):
            c = 4 + h
            for q in range(UA):
                projection_unit(c, q)
                if q == 0:
                    act.wait_ge(sem["d_vT_psum"], h + 1)
                    copy(T(8 + h), PS[6][:, 0:S]).then_inc(sem["d_vT"], 1)
                if q in (1, 2):
                    m = q - 1
                    act.wait_ge(sem["d_negmax"], 2 * h + m + 1)
                    e = span(34, CW * m, CW)
                    for qt, cols in enumerate((slice(0, P), slice(P, CW))):
                        i = nc.scalar.activation(e[:, cols], e[:, cols], ACT.Exp, bias=st[:, 0, 2 * m + qt:2 * m + qt + 1],
                                                 accum_out=st[:, 1, 2 * m + qt:2 * m + qt + 1])
                    i.then_inc(sem["d_exp"], 1)
                if q == 4 and h == 3:
                    act.wait_ge(sem["m_BT"], 1)
                    copy(BT[:].rearrange("p a b -> p (a b)"), PS[7][:, CW:CW + TT * BR_HEADS]).then_inc(sem["m_rows"], 1)
                if q == 5:
                    act.wait_ge(sem["d_probsT_psum"], h + 1)
                    copy(span(37, CW, CW), PS[7][:, 0:CW]).then_inc(sem["d_probsT"], 1)
                if q == 6:
                    act.wait_ge(sem["d_out_psum"], h + 1)
                    copy(T(h), PS[6][:, S:2 * S]).then_inc(sem["d_out"], 1)
                if q == 7 and h == 0:
                    act.wait_ge(sem["m_absz"], 1)
                    then(nc.scalar.activation(T(42)[0:rows, :], T(42)[0:rows, :], ACT.Exp, scale=-1.0))
                    nc.scalar.activation(T(42)[0:rows, :], T(42)[0:rows, :], ACT.Ln, bias=1.0).then_inc(sem["m_log"], 1)
            store_chunk(c % 2, lambda o: slice(tiles_of[c] + o, tiles_of[c] + o + 2))
        act.wait_ge(sem["d_out"], BR_HEADS)

        def head_squares(src, sq):
            nc.scalar.activation(T(sq, 4), T(src, 4), ACT.Square).then_inc(sem["hn_sq"], 1)

        def head_root(n, sq):
            act.wait_ge(sem["hn_var"], n + 1)
            inverse_root(head_guess(n), T(sq, 4)).then_inc(sem["hn_std"], 1)

        head_squares(0, 34)

        for h in range(BR_HEADS):
            c = 8 + h
            for q in range(UA):
                projection_unit(c, q) if (c, q) < (11, LEAD) else split(R_GATE, UA * (c - 12) + q + LEAD)
                if h == 0 and q == 0:
                    act.wait_ge(sem["m_conv"], 1)
                    nc.scalar.activation(T(44, 8), T(44, 8), ACT.Silu).then_inc(sem["m_silu"], 1)
                    act.wait_ge(drained[1], H_IN2 + 5)
                    nc.scalar.activation(T(24, 4), T(24, 4), ACT.Sigmoid).then_inc(sem["m_sig"], 1)
                if h == 0 and q == 1:
                    act.wait_ge(sem["g_z_psum"], 1)
                    for t in range(2):
                        m = nc.scalar.activation(T(8 + t), PS[4][:, t * S:(t + 1) * S], ACT.Identity, bias=vec("gla_ba_2", t))
                    m.then_inc(sem["g_z"], 1)
                    head_root(0, 34)
                if q == 2:
                    act.wait_ge(sem["m_vT_psum"], h + 1)
                    copy(T(20 + h), PS[6][:, 0:S]).then_inc(sem["m_vT"], 1)
                if q == 3:
                    act.wait_ge(sem["m_A"], h + 1)
                    e = span(52, 0, CW)
                    nc.scalar.activation(st[:, 1, 0:2], st[:, 0, 4:6], ACT.Exp)
                    for qt, cols in enumerate((slice(0, P), slice(P, CW))):
                        m = nc.scalar.activation(e[:, cols], e[:, cols], ACT.Exp, bias=st[:, 0, 2 + qt:3 + qt])
                    m.then_inc(sem["m_E"], 1)
                if q == 6:
                    act.wait_ge(sem["m_ST_psum"], h + 1)
                    copy(span(52, CW, CW), PS[7][:, 0:CW]).then_inc(sem["m_ST"], 1)
                if h == 1 and q == 7:
                    act.wait_ge(sem["g_absz"], 1)
                    then(nc.scalar.activation(T(10, 2), T(10, 2), ACT.Exp, scale=-1.0))
                    nc.scalar.activation(T(10, 2), T(10, 2), ACT.Ln, bias=1.0).then_inc(sem["g_log"], 1)
            store_chunk(c % 2, lambda o: slice(tiles_of[c] + o, tiles_of[c] + o + 2))

        def gla_steps(u):
            if u == 0:
                act.wait_ge(sem["g_vT_psum"], 1)
                for b in range(2):
                    m = copy(T(32 + 2 * b, 2), halves(PS[6 + b][:]))
                m.then_inc(sem["g_vT"], 1)
            if u == 0 or u % 4 == 2 and u // 4 + 1 < GLA_STEPS and turned_level(u // 4 + 1):
                n = (u + 2) // 4
                act.wait_ge(sem["g_arg"], n + 1 if n < len(GLA_LEVELS) else GLA_STEPS - 1)
                nc.scalar.activation(T(12, 4), T(12, 4), ACT.Exp).then_inc(sem["g_exp"], 1)
            if u == 34:
                nc.scalar.activation(T(36, 4), T(36, 4), ACT.Silu).then_inc(sem["g_sig"], 1)
                act.wait_ge(sem["g_att_psum"], GLA_STEPS)
                x_att = span(54, 0, BR_HEADS * P).rearrange("p (a b c) -> p b a c", a=2, b=2)
                for par in range(2):
                    m = copy(x_att[:, par], halves(PS[4 + par][:, 0:2 * P]))
                m.then_inc(sem["g_x_copied"], 1)
            if u == 36:
                act.wait_ge(sem["hid_ready"], MLP_SUPER + 1)
                act.wait_ge(sem["g_out_psum"], 1)
                for b in range(2):
                    m = copy(T(2 * b, 2), halves(PS[6 + b][:]), scale=GLA_SCALE)
                m.then_inc(sem["g_out"], 1)
                act.wait_ge(sem["g_out"], 1)
                head_squares(0, 44)
            if u == 38:
                head_root(1, 44)

        def s5_steps(t, u):
            if u == 1:
                if t == 0:
                    act.wait_ge(sem["branch_ready"], 2)
                act.wait_ge(sem["s_turned"], t + 1)
                for part in range(2):
                    m = copy(T(44 + 2 * part, 2), halves(PS[4 + part][:]))
                m.then_inc(sem["s_BT"], 1)
            if u == 3:
                if t >= 1:
                    act.wait_ge(sem["s_x"], t)
                act.wait_ge(sem["s_bu_psum"], t + 1)
                for b in range(4):
                    m = copy(T(24 + 2 * b, 2), halves(PS[(6, 7, 4, 5)[b]][:]))
                m.then_inc(sem["s_bu"], 1)
            if u == 6:
                act.wait_ge(sem["s_cturned"], t + 1)
                for part in range(2):
                    m = copy(T(48 + 2 * part, 2), halves(PS[4 + part][:]), scale=1.0 if part == 0 else -1.0)
                m.then_inc(sem["s_CT"], 1)

        def last_steps(u):
            if u == 0:
                act.wait_ge(sem["s_y"], 4)
                nc.scalar.activation(T(24, 4), T(40, 4), ACT.Gelu_apprx_tanh).then_inc(sem["s_z"], 1)
            if u == 2:
                act.wait_ge(sem["s_glu_psum"], 1)
                for f in range(4):
                    m = nc.scalar.activation(T(28 + f), PS[4 + f // 2][:, (f % 2) * S:(f % 2 + 1) * S], ACT.Sigmoid,
                                             bias=vec("s5_glu_b_2", f))
                m.then_inc(sem["s_glu"], 1)

        for i in range(4):
            source = (0, 4, 0, 24)[i]
            for j in range(40):
                split(R_GATE + 5 * i, j + LEAD)
                if j == (4 if i == 3 else 0):
                    act.wait_ge(sem["branch_ready"], (1, 1, 2, 3)[i])
                    if i == 1:
                        act.wait_ge(sem["m_out"], BR_HEADS)
                    copy(hid_hi[:, 0], T(source, FT)).then_inc(sem["op_hi"], 1)
                if j % 10 == 7:
                    n = j // 10
                    if i == 0:
                        act.wait_ge(sem["x_parked"], 16)
                        o = merged(n)
                    else:
                        if (i, n) == (1, 0):
                            act.wait_ge(sem["hid_ready"], MLP_SUPER + 2)
                        else:
                            act.wait_ge(sem["sig_free"], 4 * (i - 1) + n)
                        o = T(4, FT)
                    for f in range(FT):
                        m = nc.scalar.activation(o[:, f], SETS[0][f // 2][:, (f % 2) * S:(f % 2 + 1) * S],
                                                 ACT.Sigmoid, bias=vec("b_gate_2", i * KT + FT * n + f))
                    m.then_inc(drained[0], 1)
                (gla_steps, lambda u: s5_steps(u // 20, u % 20), lambda u: s5_steps(2 + u // 20, u % 20), last_steps)[i](j)
                if i == 3 and j >= 37:
                    for n in ((0, 1), (2,), (3,))[j - 37]:
                        act.wait_ge(sem["sig_free"], 8 + n + 1)
                        copy(hop_hi[:, FT * n:FT * n + FT], merged(n)).then_inc(sem["merged_hi"], 1)
        for j in range(4 * UA):
            split(R_OUT2, j + LEAD)
            if j % UA == UA - 1:
                c = j // UA
                for b in range(2):
                    m = nc.scalar.activation(T(NORM_SQ[6] + FT * c + 2 * b, 2), halves(SETS[c % 2][b][:]), ACT.Square)
                m.then_inc(sem["sq_ready"], 1)
                store_chunk(c % 2, lambda o: slice(FT * c + o, FT * c + o + 2))
        norm(6)
        for g in range(4):
            act.wait_ge(sem["res_ready"], g + 1)
            squares(7, g, of_x)
        norm(7, lambda k: mod[:, 3 * KT + k:3 * KT + k + 1])

        def silu():
            for b in range(2):
                m = nc.scalar.activation(T(16 + 2 * b, 2), halves(SETS[0][b][:]), ACT.Silu)
            m.then_inc(drained[0], 1)

        for j in range(2 * UA):
            split(R_FFN, j + LEAD)
            if j == 7:
                silu()
        hidden_hi(0, drained[1], H_FFN + 2, 20)
        with act.Fori(0, FFN_SUPER // 2) as i:
            for j in range(6 * UA):
                split(R_FFN + 2 + 6 * i, j + LEAD)
                par = j // 24
                if j % 24 == 7:
                    silu()
                if j % 24 == 16:
                    hidden_hi(1 - par, drained[1], 6 * i + (H_FFN + 1 + 3 * par + 2), 20)
        for j in range(UA - LEAD):
            split(R_FFN + 2 + 3 * (FFN_SUPER - 1), j + LEAD)
        for c in range(4):
            act.wait_ge(drained[c % 2], R_END_H - 2 + c // 2 + 2)
            squares(8, c, of_arena(0))
        norm(8)
        for b in range(8):
            act.wait_ge(sem["out_psum"], b + 1)
            copy(span(48, b * 512, 512), PS[b % 4][:]).then_inc(sem["out_copied"], 1)

    @block.vector
    def _(dve):
        V = nc.vector
        steps = [0]

        def then(ins):
            steps[0] += 1
            ins.then_inc(sem["dve_chain"], 1)
            dve.wait_ge(sem["dve_chain"], steps[0])

        def stt(o, i0, scalar, i1, op0, op1, **k):
            return V.scalar_tensor_tensor(o, i0, scalar, i1, op0, op1, **k)

        def split(R, j, cols=COLS):
            dve.wait_ge(sem["hi_ready"], R * 8 + (j + 1))
            V.tensor_tensor(w_lo[:, j % LEAD, :, 0:cols], w_raw[:, j % RAW, :, 0:cols],
                            w_hi[:, j % LEAD, :, 0:cols].bitcast(F32), ALU.subtract).then_inc(sem["lo_ready"], 1)

        def halves(ap):
            return ap.rearrange("p (a b) -> p a b", a=2)

        def add_chunk(R, j, s, at, tile):
            dve.wait_ge(sem["unit_done"], R * 8 + (j + 1))
            for b in range(2):
                dst = at[:, tile(2 * b), :]
                m = V.tensor_tensor(dst, halves(SETS[s][b][:]), dst, ALU.add)
            m.then_inc(drained[s], 1)

        def newton(o, v, guess):
            then(stt(v, v, -0.5, guess, ALU.mult, ALU.mult))
            then(V.tensor_tensor(v, v, guess, ALU.mult))
            return stt(o, v, 1.5, guess, ALU.add, ALU.mult)

        def inverse_root(n, o=rstd[:]):
            dve.wait_ge(sem["std_ready"], n + 1)
            then(newton(o, var[:], std[:]))

        def norm(n, src, gain, bias=None, midway=None):
            tiles, is_split = NORMS[n]
            dve.wait_ge(sem["sum_ready"], n + 1)
            V.tensor_scalar(var[:], norm_bank(n), 1.0 / (tiles * P), EPS, ALU.mult, ALU.add).then_inc(sem["var_ready"], 1)
            inverse_root(n)
            scale_tiles(n, src, gain, bias, midway=midway)

        def scale_tiles(n, src, gain, bias=None, add_to=None, midway=None):
            tiles, is_split = NORMS[n]
            dst, lag = 8 if n == 2 else 0, 1
            for i in range(tiles + lag):
                if midway is not None and i == 4:
                    midway()
                if i < tiles:
                    stt(T(NORM_T[n] + i), src(i), gain(i), rstd[:], ALU.mult, ALU.mult).then_inc(sem["normed"], 1)
                k = i - lag
                if is_split and k >= 0:
                    dve.wait_ge(sem["hop_hi"], before(n, "hop") + k + 1)
                    hi, t = hop_hi[:, dst + k].bitcast(F32), T(NORM_T[n] + k)
                    if bias is None:
                        m = V.tensor_tensor(hop_lo[:, dst + k], t, hi, ALU.subtract)
                    else:
                        m = stt(hop_lo[:, dst + k], t, bias(k), hi, ALU.add, ALU.subtract)
                    m.then_inc(sem["hop_ready"], 1)
                if add_to is not None and k >= 0 and k % 4 == 3:
                    dve.wait_ge(sem["normed"], before(n, "normed") + k + 1)
                    V.tensor_tensor(add_to[:, k - 3:k + 1], add_to[:, k - 3:k + 1], T(NORM_T[n] + k - 3, 4),
                                    ALU.add).then_inc(sem["res_ready"], 1)

        def of_x(k):
            return x[:, k]

        def of_arena(t):
            return lambda k: T(t + k)

        QT = (slice(0, P), slice(P, CW))

        V.memset(ones[:], 1.0)
        V.memset(bias_all[:], 1.0).then_inc(sem["dve_chain"], 1)
        steps[0] += 1
        dve.wait_ge(sem["dve_chain"], 1)
        dve.sem_inc(drained[0], 1)
        dve.sem_inc(drained[1], 1)
        dve.sem_inc(sem["table_clear"], 1)
        def scale_pair(n, b, gain):
            for k in (2 * b, 2 * b + 1):
                V.tensor_scalar(T(NORM_T[n] + k), x[:, k], gain(k), None, ALU.mult).then_inc(sem["normed"], 1)

        def lo_pair(n, b):
            dve.wait_ge(sem["hop_hi"], before(n, "hop") + 2 * (b + 1))
            V.tensor_tensor(hop_lo[:, 2 * b:2 * b + 2], T(NORM_T[n] + 2 * b, 2), hop_hi[:, 2 * b:2 * b + 2].bitcast(F32),
                            ALU.subtract).then_inc(sem["hop_ready"], 2)

        def variance(n):
            dve.wait_ge(sem["sum_ready"], n + 1)
            V.tensor_scalar(var[:], norm_bank(n), 1.0 / (NORMS[n][0] * P), EPS, ALU.mult, ALU.add).then_inc(sem["var_ready"], 1)

        def by_token(ap, tiles):
            return ap.unsqueeze(1).to_broadcast([P, tiles, S])

        dve.wait_ge(sem["gain_turned"], 1)
        then(V.tensor_copy(gain0[:], PS[0][:, 0:KT]))
        for b in range(KT // 2):
            dve.wait_ge(sem["x_copied"], b + 1)
            scale_pair(0, b, lambda k: gain0[:, k:k + 1])
            if b >= 1:
                lo_pair(0, b - 1)
            if b >= 4:
                split(0, b - 4)
        lo_pair(0, KT // 2 - 1)

        def bias_rows():
            dve.wait_ge(sem["small_in"], 16 * N_SMALL)
            for h in range(BR_HEADS):
                m = V.tensor_scalar(span(50, h * P, P)[BROWS, :], ones[BROWS, :],
                                    bias_table[:, h:h + 1], None, ALU.mult)
            m.then_inc(sem["bias_rows_ready"], 1)
            then(V.tensor_tensor(lam_prod, lam[:, 0::2, :], lam[:, 1::2, :], ALU.mult))
            V.reduce_sum(lam_s[:, 0:2], lam_prod, axis=AX_X).then_inc(sem["lam_sums"], 1)

        def negative_lambda():
            dve.wait_ge(sem["lam_exps"], 1)
            then(V.tensor_tensor(lam_s[:, 4:5], lam_s[:, 3:4], lam_s[:, 2:3], ALU.subtract))
            then(V.tensor_scalar(lam_s[:, 5:6], lam_s[:, 4:5], -LAM_INIT, None, ALU.add))

        neg_lam = lam_s[:, 5:6]

        def ada(slots, j, g):
            for i, u in enumerate(slots):
                if u == j:
                    k = i % KT
                    slot = k % ADA_RING
                    acc = span(ADA_ACC, 0, ADA_COLS)
                    w = span(ADA_SLOTS, slot * ADA_COLS, ADA_COLS)
                    dve.wait_ge(ada_landed[slot], ((g + i // KT) * (KT // ADA_RING) + (k // ADA_RING + 1)) * 16)
                    if k == 0:
                        m = V.tensor_scalar(acc, w, cs[:, 0:1], None, ALU.mult)
                    else:
                        dve.wait_ge(sem["ada_used"], (g + i // KT) * KT + k)
                        m = stt(acc, w, cs[:, k:k + 1], acc, ALU.mult, ALU.add)
                    m.then_inc(sem["ada_used"], 1)

        def modulation(g):
            dve.wait_ge(sem["mod_psum"], g + 1)
            vg, r, _ = VEC["ada_b_2"]
            cols = bass.ds(g * ADA_F, ADA_F)
            V.tensor_tensor(mod[:, cols], PS[7][:, 0:ADA_F], vecs[:, bass.ds(g * ADA_F + (vg * P + r), ADA_F)],
                            ALU.add).then_inc(sem["mod_ready"], 1)

        def first_mixer(u):
            for h in range(HEADS):
                s, stat = span(46, CW * (h % 2), CW), st[:, h % 2]
                if u == SCORES_AT[h]:
                    dve.wait_ge(sem["a_scores"], h + 1)
                    if h >= 2:
                        dve.wait_ge(sem["a_probsT_psum"], h - 1)
                    slope = 2.0 ** (-8.0 * (h + 1) / HEADS)
                    stt(s, C("dist"), slope / A_SCALE, PS[4][:, 0:CW], ALU.mult, ALU.add).then_inc(sem["a_masked"], 1)
                    dve.wait_ge(sem["a_masked"], h + 1)
                    for qt, cols in enumerate(QT):
                        m = V.reduce_max(stat[:, qt:qt + 1], s[:, cols], axis=AX_X)
                    then(m)
                    V.tensor_scalar(stat[:, 2:4], stat[:, 0:2], -A_SCALE, None, ALU.mult).then_inc(sem["a_negmax"], 1)
                if u == SCORES_AT[h] + 2:
                    dve.wait_ge(sem["a_exp"], h + 1)
                    for qt, cols in enumerate(QT):
                        m = stt(s[:, cols], s[:, cols], 1.0, C("count")[:, cols], ALU.mult, ALU.mult,
                                accum_out=stat[:, 4 + qt:5 + qt])
                    then(m)
                    then(V.reciprocal(stat[:, 6:8], stat[:, 4:6]))
                    for qt, cols in enumerate(QT):
                        m = V.tensor_scalar(s[:, cols], s[:, cols], stat[:, 6 + qt:7 + qt], None, ALU.mult)
                    m.then_inc(sem["a_probs"], 1)

        def scaled_chunk(p):
            dve.wait_ge(sem["unit_done"], R_IN * 8 + UA * (p + 1))
            for b in range(2):
                m = V.tensor_tensor(T(4 * IN_ORDER[p] + 2 * b, 2), halves(SETS[p % 2][b][:]), by_token(inv0, 2), ALU.mult)
            m.then_inc(drained[p % 2], 1)

        inv0 = T(45)
        for j in range(8 * UA):
            split(R_IN, j + LEAD)
            if j == 5:
                bias_rows()
            if j == 6:
                variance(0)
                dve.wait_ge(sem["cs_ready"], 1)
            if j == 7:
                inverse_root(0, inv0)
            if j == 9:
                negative_lambda()
            if j % UA == UA - 1 and j // UA < 7:
                scaled_chunk(j // UA)
            ada(ADA_ONE if j >= 32 else ADA_FIRST, j % 32, G_IN + j // 32)
            if j in (28, 58):
                modulation(G_IN + j // 32)
            first_mixer(j)
            if j == 61:
                norm(1, of_arena(0), lambda k: vec("pool_out_norm_g", k), midway=lambda: scaled_chunk(7))
        for j in range(4 * UA):
            split(R_OUT, j + LEAD)
            if j == 3:
                norm(2, of_arena(8), lambda k: vec("attn_out_norm_g", k))
            if j == 2 * UA:
                modulation(G_OUT)
            ada(ADA_TWO, j, G_OUT)
            if j == 4 * UA - 1:
                lo_pair(3, 0)
            for c in range(4):
                if j == OUT_LAST[c]:
                    add_chunk(R_OUT, j, c % 2, x, lambda o: slice(FT * c + o, FT * c + o + 2))
                if c < 3 and j == OUT_LAST[c] + 1:
                    dve.wait_ge(drained[c % 2], H_OUT + c // 2 + 2)
                    for b in range(2):
                        scale_pair(3, 2 * c + b, lambda k: vec("norm_mlp_g", k))
        lo_pair(3, 1)
        dve.wait_ge(drained[1], H_MLP + 1)
        for b in range(2):
            scale_pair(3, 6 + b, lambda k: vec("norm_mlp_g", k))
        for b in range(2, 8):
            lo_pair(3, b)
        modulation(G_OUT + 1)

        inv_sq = fix

        def square(s, H, count):
            dve.wait_ge(drained[s], H + 2)
            V.tensor_tensor(T(4, FT), T(0, FT), by_token(inv_sq[:], FT), ALU.mult).then_inc(sem["relu_scaled"], 1)
            dve.wait_ge(sem["relu_scaled"], count)
            V.tensor_tensor(T(4, FT), T(4, FT), T(0, FT), ALU.mult).then_inc(sem["relu_sq"], 1)

        def hidden_lo(par, count, tile):
            dve.wait_ge(sem["hid_hi"], count)
            V.tensor_tensor(hid_lo[:, par], T(tile, FT), hid_hi[:, par].bitcast(F32),
                            ALU.subtract).then_inc(sem["hid_ready"], 1)

        def down_ends(R, j, j0, s0, at):
            q = j - j0
            if 0 <= q < 4 * UB and q % UB == UB - 1:
                n = q // UB
                add_chunk(R, j, (s0 + n) % 2, at, lambda o: slice(FT * n + o, FT * n + o + 2))

        for j in range(UA):
            split(R_MLP, j + LEAD)
            if j == 5:
                variance(3)
            if j == 6:
                inverse_root(3)
                then(V.tensor_tensor(inv_sq[:], rstd[:], rstd[:], ALU.mult))
        square(0, H_MLP, 1)
        hidden_lo(0, 1, 4)
        with dve.Fori(0, MLP_SUPER // 2 - 1) as i:
            R, H = R_MLP + 1 + 4 * i, H_MLP + 5 * i
            for j in range(4 * UA):
                split(R, j + LEAD)
                if j == 7:
                    square(1, H, 2 * i + 2)
                if j == 23:
                    square(0, H + 3, 2 * i + 3)
                if j in (9, 25):
                    hidden_lo(1 if j == 9 else 0, 2 * i + (2 if j == 9 else 3), 4)
                down_ends(R, j, 8, 0, x)
                down_ends(R, j, 24, 1, x)
                ada(ADA_ONE, j, i + G_MLP)
                if j == 28:
                    modulation(i + G_MLP)
        for j in range(3 * UA):
            split(R_MLP + 29, j + LEAD)
            if j == 7:
                square(1, H_MLP + 35, MLP_SUPER)
            if j == 9:
                hidden_lo(1, MLP_SUPER, 4)
            down_ends(R_MLP + 29, j, 8, 0, x)
            down_ends(R_MLP + 29, j, 16, 0, x)
            ada(ADA_TAIL, j, G_MLP + MLP_SUPER // 2 - 1)
        modulation(G_MLP + MLP_SUPER // 2 - 1)
        dve.wait_ge(drained[0], H_IN2 + 1)
        dve.wait_ge(drained[1], H_IN2 + 1)

        dve.wait_ge(sem["mod_ready"], G_IN2)
        then(stt(gain5[:], mod[:, KT:2 * KT], 1.0, vec("norm_g_2", 0, KT), ALU.add, ALU.mult))
        then(V.tensor_tensor(gain5[:], gain5[:], vec("norm_final_g", 0, KT), ALU.mult))
        then(V.tensor_tensor(gain6[:], mod[:, 2 * KT:3 * KT], vec("norm_g_2", KT, KT), ALU.mult))
        inv4, var4 = T(53), T(54)
        dve.wait_ge(sem["sum_ready"], 5)
        V.tensor_scalar(var4, PS[4][:, 0:S], 1.0 / D, EPS, ALU.mult, ALU.add).then_inc(sem["var_ready"], 1)
        dve.wait_ge(sem["var_ready"], 5)
        then(V.tensor_scalar(var[:], var4, EPS, None, ALU.mult))
        dve.wait_ge(sem["sum_ready"], 6)
        stt(var[:], PS[5][:, 0:S], 1.0 / D, var[:], ALU.mult, ALU.add).then_inc(sem["var_ready"], 1)
        inverse_root(5)
        scale_tiles(5, of_x, lambda k: gain5[:, k:k + 1], bias=lambda k: mod[:, k:k + 1])
        then(newton(inv4, var4, inv4))

        DT, MAG, THR, SIN, HALF, COS, RE, IM, DEN, FRE, FIM, T0, T1, K = range(14)
        are, aim = vec("s5_a_re_2", 0, 16), vec("s5_a_im_2", 0, 16)

        def v(i):
            return s5v[:, i]

        def s5_angle():
            dve.wait_ge(sem["s_dt"], 1)
            then(V.tensor_tensor(v(MAG), v(DT), are, ALU.mult))
            then(V.tensor_tensor(v(THR), v(DT), aim, ALU.mult))
            then(V.tensor_scalar(v(K), v(THR), float(1 / (2 * np.pi)), ROUND, ALU.mult, ALU.add))
            then(V.tensor_scalar(v(K), v(K), -ROUND, None, ALU.add))
            for part in TWO_PI:
                then(stt(v(THR), v(K), -part, v(THR), ALU.mult, ALU.add))
            V.tensor_scalar(v(THR), v(THR), -PI_BELOW, PI_BELOW, ALU.max, ALU.min).then_inc(sem["s_trig"], 1)

        def s5_discrete():
            dve.wait_ge(sem["s_sin"], 1)
            then(V.tensor_tensor(v(COS), v(HALF), v(HALF), ALU.mult))
            then(V.tensor_scalar(v(COS), v(COS), -2.0, 1.0, ALU.mult, ALU.add))
            then(V.tensor_tensor(v(RE), v(MAG), v(COS), ALU.mult))
            then(V.tensor_tensor(v(IM), v(MAG), v(SIN), ALU.mult))
            then(V.tensor_scalar(v(RE), v(RE), -1.0, None, ALU.add))
            then(V.tensor_tensor(v(DEN), are, are, ALU.mult))
            then(V.tensor_tensor(v(T0), aim, aim, ALU.mult))
            then(V.tensor_tensor(v(DEN), v(DEN), v(T0), ALU.add))
            then(V.reciprocal(v(DEN), v(DEN)))

        def s5_factor():
            for o, p0, p1, op in ((FRE, (RE, are), (IM, aim), ALU.add), (FIM, (IM, are), (RE, aim), ALU.subtract)):
                then(V.tensor_tensor(v(T0), v(p0[0]), p0[1], ALU.mult))
                then(V.tensor_tensor(v(T1), v(p1[0]), p1[1], ALU.mult))
                then(V.tensor_tensor(v(o), v(T0), v(T1), op))
                then(V.tensor_tensor(v(o), v(o), v(DEN), ALU.mult))

        def s5_inputs():
            wide = [P, 16, S5_CH]
            fre, fim = (v(i).unsqueeze(2).to_broadcast(wide) for i in (FRE, FIM))
            by_im = [T(i).rearrange("p (i c) -> p i c", c=S5_CH) for i in (40, 41)]
            then(V.tensor_tensor(by_im[0], s5b[1][:], fim, ALU.mult))
            then(V.tensor_tensor(by_im[1], s5b[0][:], fim, ALU.mult))
            for o, t, op in ((s5b[0], by_im[0], ALU.subtract), (s5b[1], by_im[1], ALU.add)):
                then(V.tensor_tensor(o[:], o[:], fre, ALU.mult))
                then(V.tensor_tensor(o[:], o[:], t, op))

        def s5_powers(levels):
            for l in levels:
                c1, s1 = s5pow[0][:, l], s5pow[1][:, l]
                if l == 0:
                    then(V.tensor_copy(c1, v(COS)))
                    then(V.tensor_copy(s1, v(SIN)))
                    continue
                c0, s0 = s5pow[0][:, l - 1], s5pow[1][:, l - 1]
                then(V.tensor_tensor(v(T0), s0, s0, ALU.mult))
                then(V.tensor_tensor(c1, c0, c0, ALU.mult))
                then(V.tensor_tensor(c1, c1, v(T0), ALU.subtract))
                then(stt(s1, c0, 2.0, s0, ALU.mult, ALU.mult))

        coefficients = {2: s5_angle, 6: s5_discrete, 8: s5_factor, 10: s5_inputs,
                        12: lambda: s5_powers(range(3)), 14: lambda: s5_powers(range(3, 6)),
                        16: lambda: s5_powers(range(6, 8))}

        def projection_unit(c, q):
            ahead = (UA * c + q + LEAD) // UA
            split(R_IN2, UA * c + q + LEAD, cols=P if ahead == 3 else COLS)

        for j in range(4 * UA):
            projection_unit(j // UA, j % UA)
            ada(ADA_ONE, j, G_IN2)
            if j in coefficients:
                coefficients[j]()
        dve.sem_inc(sem["s_pow"], 1)
        modulation(G_IN2)

        def attention_scores(h, m):
            s = span(34, CW * m, CW)
            if (h, m) == (0, 0):
                dve.wait_ge(sem["bias_in"], 32)
            dve.wait_ge(sem["d_scores"], 2 * h + m + 1)
            stt(s, PS[4 + m][:, 0:CW], DA_SCALE, span(28, h * CW, CW), ALU.mult, ALU.add).then_inc(sem["d_masked"], 1)
            dve.wait_ge(sem["d_masked"], 2 * h + m + 1)
            for qt, cols in enumerate(QT):
                i = V.reduce_max(st[:, 0, 4 + 2 * m + qt:5 + 2 * m + qt], s[:, cols], axis=AX_X)
            then(i)
            V.tensor_scalar(st[:, 0, 2 * m:2 * m + 2], st[:, 0, 4 + 2 * m:6 + 2 * m], -1.0, None,
                            ALU.mult).then_inc(sem["d_negmax"], 1)

        def attention_probs(h):
            dve.wait_ge(sem["d_exp"], 2 * h + 2)
            then(V.reciprocal(st[:, 1, 4:8], st[:, 1, 0:4]))
            then(V.tensor_scalar(st[:, 1, 6:8], st[:, 1, 6:8], neg_lam, None, ALU.mult))
            e0, e1, p = span(34, 0, CW), span(34, CW, CW), span(37, 0, CW)
            for qt, cols in enumerate(QT):
                i = V.tensor_scalar(e0[:, cols], e0[:, cols], st[:, 1, 4 + qt:5 + qt], None, ALU.mult)
            then(i)
            if h >= 1:
                dve.wait_ge(sem["d_probsT_psum"], h)
            for qt, cols in enumerate(QT):
                i = stt(p[:, cols], e1[:, cols], st[:, 1, 6 + qt:7 + qt], e0[:, cols], ALU.mult, ALU.add)
            i.then_inc(sem["d_probs"], 1)

        def head_variance(n, sq):
            dve.wait_ge(sem["hn_sum"], n + 1)
            for b in range(2):
                m = V.tensor_scalar(T(sq + 2 * b, 2), halves(PS[6 + b][:]), 1.0 / P, EPS, ALU.mult, ALU.add)
            m.then_inc(sem["hn_var"], 1)

        def head_inverse(n, sq):
            dve.wait_ge(sem["hn_std"], n + 1)
            then(newton(head_guess(n), T(sq, 4), head_guess(n)))

        rows = BR_HEADS
        ig, z, b = gate_rows[:, 0, :], gate_rows[:, 1, :], T(43)[0:rows, :]
        soft, a_row = T(42)[0:rows, :], T(40)[0:rows, :]

        for h in range(BR_HEADS):
            for q in range(UA):
                projection_unit(4 + h, q)
                if q < 2:
                    attention_scores(h, q)
                if q == 3:
                    attention_probs(h)
                if q == 6:
                    for k in range(4 * h, 4 * h + 4):
                        m = stt(x[:, k], x[:, k], vec("norm_final_g", k), inv4, ALU.mult, ALU.mult)
                    m.then_inc(sem["x_normed"], 1)
                if h == 0 and q == 4:
                    dve.wait_ge(sem["gates_ready"], 1)
                    then(V.tensor_scalar(z, z, gate_b[:, 1:2], None, ALU.add))
                    stt(soft, z, -1.0, z, ALU.mult, ALU.max).then_inc(sem["m_absz"], 1)
                if h == 1 and q == 4:
                    dve.wait_ge(sem["m_log"], 1)
                    then(stt(soft, z, 0.0, soft, ALU.min, ALU.subtract))
                    then(V.tensor_tensor_scan(b, ones[0:rows, 0:1].to_broadcast([rows, S]), soft, 0.0, ALU.mult, ALU.add))
                    stt(a_row, ig, gate_b[:, 0:1], b, ALU.add, ALU.subtract).then_inc(sem["m_rows"], 1)

        def mlstm_weights(h):
            dve.wait_ge(sem["m_bc"], h + 1)
            if h >= 1:
                dve.wait_ge(sem["m_ST_psum"], h)
            e = span(52, 0, CW)
            V.tensor_tensor(e[:, 0:P], PS[4][:, 0:P], C("causal"), ALU.add)
            V.tensor_copy(e[:, P:S], PS[4][:, 0:P])
            then(V.tensor_tensor(e[:, S:CW], PS[4][:, P:S], C("causal"), ALU.add))
            for qt, cols in enumerate(QT):
                m = V.reduce_max(st[:, 0, qt:qt + 1], e[:, cols], axis=AX_X)
            then(m)
            then(V.tensor_scalar(st[:, 0, 0:2], st[:, 0, 0:2], 0.0, None, ALU.max))
            if h == 0:
                dve.wait_ge(sem["m_rows"], 2)
            V.tensor_scalar(st[:, 0, 2:4], st[:, 0, 0:2], -1.0, None, ALU.mult)
            stt(st[:, 0, 4:6], st[:, 0, 0:2], -1.0, BT[:, :, h], ALU.mult, ALU.subtract).then_inc(sem["m_A"], 1)

        def mlstm_scores(h):
            e = span(52, 0, CW)
            dve.wait_ge(sem["m_qk"], h + 1)
            dve.wait_ge(sem["m_E"], h + 1)
            for qt, cols in enumerate(QT):
                m = stt(e[:, cols], PS[5][:, cols], ML_SCALE, e[:, cols], ALU.mult, ALU.mult,
                        accum_out=st[:, 1, 4 + qt:5 + qt])
            then(m)
            then(stt(st[:, 1, 4:6], st[:, 1, 4:6], -1.0, st[:, 1, 4:6], ALU.mult, ALU.max))
            then(V.tensor_tensor(st[:, 1, 4:6], st[:, 1, 4:6], st[:, 1, 0:2], ALU.max))
            then(V.reciprocal(st[:, 1, 6:8], st[:, 1, 4:6]))
            for qt, cols in enumerate(QT):
                m = V.tensor_scalar(e[:, cols], e[:, cols], st[:, 1, 6 + qt:7 + qt], None, ALU.mult)
            m.then_inc(sem["m_S"], 1)

        run = span(16, 0, 2 * (S + 1)).rearrange("p (a b) -> p a b", a=2)
        la = T(8, 2)
        arg = T(12, 4)

        def level_args(level):
            nb = S // level
            now = run[:, :, 1:S + 1].rearrange("p a (n l) -> p a n l", l=level)
            to = arg.rearrange("p (w a) (n l) -> p w a n l", w=2, l=level)
            start = run[:, :, 0:S].rearrange("p a (n l) -> p a n l", l=level)[:, :, :, 0:1]
            end = now[:, :, :, level - 1:level]
            for t in range(2):
                V.tensor_tensor(to[:, 0, t], now[:, t], start[:, t].to_broadcast([P, nb, level]), ALU.subtract)
                m = V.tensor_tensor(to[:, 1, t], end[:, t].to_broadcast([P, nb, level]), now[:, t], ALU.subtract)
            m.then_inc(sem["g_arg"], 1)

        for h in range(BR_HEADS):
            for q in range(UA):
                projection_unit(8 + h, q) if (h, q) < (3, LEAD) else split(R_GATE, UA * (h - 4) + q + LEAD)
                if h == 0 and q == 0:
                    head_variance(0, 34)
                if h == 0 and q == 1:
                    head_inverse(0, 34)
                    stt(T(0, 4), T(0, 4), 1.0 - LAM_INIT, head_guess(0), ALU.mult, ALU.mult).then_inc(sem["branch_ready"], 1)
                if q == 2:
                    mlstm_weights(h)
                if q == 4:
                    mlstm_scores(h)
                if h == 1 and q == 5:
                    dve.wait_ge(sem["g_z"], 1)
                    stt(T(10, 2), la, -1.0, la, ALU.mult, ALU.max).then_inc(sem["g_absz"], 1)
                if h == 2 and q == 5:
                    dve.wait_ge(sem["g_log"], 1)
                    dve.wait_ge(sem["m_conv"], 1)
                    then(stt(la, la, 0.0, T(10, 2), ALU.min, ALU.subtract))
                    then(V.tensor_scalar(la, la, 1.0 / GLA_TAU, None, ALU.mult))
                    then(V.memset(run[:, :, 0:1], 0.0))
                    for t in range(2):
                        m = V.tensor_tensor_scan(run[:, t, 1:S + 1], ones[:, 0:1].to_broadcast([P, S]), la[:, t], 0.0,
                                                 ALU.mult, ALU.add)
                    then(m)
                if h == 3 and q == 6:
                    level_args(turned_level(0))
                if q == 7:
                    dve.wait_ge(sem["m_sig"], 1)
                    dve.wait_ge(sem["m_out_psum"], h + 1)
                    V.tensor_tensor(T(4 + h), PS[6][:, S:2 * S], T(24 + h), ALU.mult).then_inc(sem["m_out"], 1)

        def gla_steps(u):
            n = u // 4
            if u % 4 == 0 and n < GLA_STEPS and turned_level(n):
                dve.wait_ge(sem["g_exp"], n + 1 if n < len(GLA_LEVELS) else GLA_STEPS - 1)
                if n >= 1:
                    dve.wait_ge(sem["g_att_psum"], n)
                V.tensor_tensor(T(44, 2), arg[:, 0:2], T(28, 2), ALU.mult)
                V.tensor_tensor(T(46, 2), arg[:, 2:4], T(30, 2), ALU.mult).then_inc(sem["g_qk"], 1)
            if u % 4 == 3 and n < GLA_STEPS - 1:
                level = turned_level(n)
                dve.wait_ge(sem["g_att_psum"], n + 1)
                mask = (C("levels", lo=n * P, n=P) if level else ident).unsqueeze(1).to_broadcast([P, 4, P])
                accs = [span(48 + 2 * par, 0, 512).rearrange("p (a b) -> p a b", a=4) for par in range(2)]
                tmps = [span((52, 56)[par], 0, 512).rearrange("p (a b) -> p a b", a=4) for par in range(2)]
                if n == 0:
                    dve.wait_ge(sem["m_ST_psum"], BR_HEADS)
                for par in range(2):
                    m = V.tensor_tensor(tmps[par] if n else accs[par], PS[4 + par][:].rearrange("p (a b) -> p a b", a=4),
                                        mask, ALU.mult)
                m.then_inc(sem["g_att_read"], 1)
                dve.wait_ge(sem["g_att_read"], n + 1)
                if n:
                    for par in range(2):
                        m = V.tensor_tensor(accs[par], accs[par], tmps[par], ALU.add)
                    if n == GLA_STEPS - 2:
                        m.then_inc(sem["g_att"], 1)
                    else:
                        then(m)
            if u % 4 == 1 and n + 1 < GLA_STEPS and turned_level(n + 1):
                dve.wait_ge(sem["g_qk"], min(n + 1, len(GLA_LEVELS)))
                level_args(turned_level(n + 1))
            if u == 38:
                head_variance(1, 44)
            if u == 39:
                head_inverse(1, 44)
                dve.wait_ge(sem["g_sig"], 1)
                then(V.tensor_tensor(T(0, 4), T(0, 4), head_guess(1), ALU.mult))
                V.tensor_tensor(T(0, 4), T(0, 4), T(36, 4), ALU.mult).then_inc(sem["branch_ready"], 1)

        bu, rot = (T(24, 4), T(28, 4)), (T(32, 4), T(36, 4))

        def s5_steps(t, u):
            cosT, sinT = rotation(t)

            def scan(part):
                for ii in range(4):
                    m = V.tensor_tensor_scan(bu[part][:, ii], v(MAG)[:, 4 * t + ii:4 * t + ii + 1].to_broadcast([P, S]),
                                             rot[part][:, ii], 0.0, ALU.mult, ALU.add)
                return m

            if u == 4:
                dve.wait_ge(sem["s_table"], t + 1)
                dve.wait_ge(sem["s_bu"], t + 1)
                if t >= 1:
                    dve.wait_ge(sem["s_y_psum"], t)
                then(V.tensor_tensor(rot[0], bu[0], cosT, ALU.mult))
            elif u == 5:
                then(V.tensor_tensor(rot[1], bu[1], sinT, ALU.mult))
            elif u == 6:
                then(V.tensor_tensor(rot[0], rot[0], rot[1], ALU.add))
            elif u == 7:
                then(V.tensor_tensor(rot[1], bu[1], cosT, ALU.mult))
            elif u == 8:
                then(V.tensor_tensor(bu[0], bu[0], sinT, ALU.mult))
                then(V.tensor_tensor(rot[1], rot[1], bu[0], ALU.subtract))
            elif u in (10, 11):
                then(scan(u - 10))
            elif u == 12:
                then(V.tensor_tensor(rot[0], bu[0], cosT, ALU.mult))
            elif u == 13:
                then(V.tensor_tensor(rot[1], bu[1], sinT, ALU.mult))
            elif u == 14:
                then(V.tensor_tensor(rot[0], rot[0], rot[1], ALU.subtract))
            elif u == 15:
                then(V.tensor_tensor(rot[1], bu[0], sinT, ALU.mult))
            elif u == 16:
                then(V.tensor_tensor(bu[1], bu[1], cosT, ALU.mult))
            elif u == 17:
                V.tensor_tensor(rot[1], rot[1], bu[1], ALU.add).then_inc(sem["s_x"], 1)
            elif u == 0 and t >= 1:
                s5_output(t - 1)

        def s5_output(t):
            dve.wait_ge(sem["s_y_psum"], t + 1)
            stt(T(40 + t), T(40 + t), vec("s5_d_2", t), PS[6][:, 0:S], ALU.mult, ALU.add).then_inc(sem["s_y"], 1)

        def last_steps(u):
            if u == 0:
                s5_output(3)
            if u == 3:
                dve.wait_ge(sem["s_glu"], 1)
                V.tensor_tensor(T(24, 4), T(24, 4), T(28, 4), ALU.mult).then_inc(sem["branch_ready"], 1)
            for g in range(2):
                if u == ADA_GATE[KT * g + KT - 1] + 3:
                    modulation(G_GATE + g)
            ada(ADA_GATE, u, G_GATE)

        for i in range(4):
            R, H = R_GATE + 5 * i, H_GATE + 4 * i
            source = (0, 4, 0, 24)[i]
            for j in range(40):
                split(R, j + LEAD)
                if j == (5 if i == 3 else 1):
                    dve.wait_ge(sem["op_hi"], i + 1)
                    V.tensor_tensor(hid_lo[:, 0], T(source, FT), hid_hi[:, 0].bitcast(F32),
                                    ALU.subtract).then_inc(sem["hid_ready"], 1)
                if j % 10 == 9:
                    n = j // 10
                    sig = T(4, FT) if i else merged(n)
                    dve.wait_ge(drained[0], H + (n + 2))
                    dve.wait_ge(sem["unit_done"], R * 8 + (j + 1))
                    for b in range(2):
                        m = V.tensor_tensor(sig[:, 2 * b:2 * b + 2], halves(SETS[1][b][:]), sig[:, 2 * b:2 * b + 2], ALU.mult)
                    m.then_inc(drained[1], 1)
                    dve.wait_ge(drained[1], H + (n + 2))
                    if i:
                        V.tensor_tensor(merged(n), merged(n), sig, ALU.add).then_inc(sem["sig_free"], 1)
                        if i < 3:
                            dve.wait_ge(sem["sig_free"], 4 * (i - 1) + n + 1)
                (gla_steps, lambda u: s5_steps(u // 20, u % 20), lambda u: s5_steps(2 + u // 20, u % 20), last_steps)[i](j)
                if i == 3 and j >= 38:
                    for n in ((0, 1), (2, 3))[j - 38]:
                        dve.wait_ge(sem["merged_hi"], n + 1)
                        V.tensor_tensor(hop_lo[:, FT * n:FT * n + FT], merged(n), hop_hi[:, FT * n:FT * n + FT].bitcast(F32),
                                        ALU.subtract).then_inc(sem["merged_ready"], 1)
        for j in range(4 * UA):
            split(R_OUT2, j + LEAD)
            ada(ADA_ONE, j, G_OUT2)
            if j == 28:
                modulation(G_OUT2)
        dve.wait_ge(sem["mod_ready"], ADA_GROUPS)
        then(stt(gain7[:], mod[:, 4 * KT:5 * KT], 1.0, vec("norm_g_2", 2 * KT, KT), ALU.add, ALU.mult))
        then(V.tensor_tensor(gain8[:], mod[:, 5 * KT:6 * KT], vec("norm_g_2", 3 * KT, KT), ALU.mult))
        def add_norm(n, gain):
            dve.wait_ge(sem["sum_ready"], n + 1)
            V.tensor_scalar(var[:], norm_bank(n), 1.0 / D, EPS, ALU.mult, ALU.add).then_inc(sem["var_ready"], 1)
            inverse_root(n)
            scale_tiles(n, of_arena(0), lambda k: gain[:, k:k + 1], add_to=x)

        dve.wait_ge(sem["x_back"], 16)
        add_norm(6, gain6)
        dve.wait_ge(sem["res_ready"], 4)
        norm(7, of_x, lambda k: gain7[:, k:k + 1], bias=lambda k: mod[:, 3 * KT + k:3 * KT + k + 1])

        def product(H):
            dve.wait_ge(drained[0], H + 2)
            for b in range(2):
                m = V.tensor_tensor(T(20 + 2 * b, 2), halves(SETS[1][b][:]), T(16 + 2 * b, 2), ALU.mult)
            m.then_inc(drained[1], 1)

        base = MLP_SUPER
        for j in range(2 * UA):
            split(R_FFN, j + LEAD)
        dve.wait_ge(sem["sum_clear"], 1)
        dve.wait_ge(sem["unit_done"], R_FFN * 8 + 2 * UA)
        product(H_FFN)
        hidden_lo(0, base + 1, 20)
        with dve.Fori(0, FFN_SUPER // 2) as i:
            R, H = R_FFN + 2 + 6 * i, H_FFN + 1 + 6 * i
            for j in range(6 * UA):
                split(R, j + LEAD)
                par = j // 24
                if j % 24 == 15:
                    dve.wait_ge(sem["unit_done"], R * 8 + (j + 1))
                    product(H + 3 * par)
                if j % 24 == 17:
                    hidden_lo(1 - par, 2 * i + (base + par + 2), 20)
                down_ends(R, j, 24 * par + 16, 0, arena)
        R = R_FFN + 2 + 3 * (FFN_SUPER - 1)
        for j in range(UA):
            if j < UA - LEAD:
                split(R, j + LEAD)
            down_ends(R, j, 0, 0, arena)
        dve.wait_ge(drained[0], R_END_H + 1)
        dve.wait_ge(drained[1], R_END_H + 1)
        add_norm(8, gain8)

    @block.gpsimd
    def _(pool):
        G = nc.gpsimd
        steps = [0]

        def then(ins):
            steps[0] += 1
            ins.then_inc(sem["pool_chain"], 1)
            pool.wait_ge(sem["pool_chain"], steps[0])

        def small(o, i):
            pool.dma_start(o, i).then_inc(sem["small_in"], 16)

        pool.wait_ge(sem["table_clear"], 1)
        small(bias_all[64:64 + N_BUCKETS, :], a["rel_bias_2"])
        small(lam, a["diff_lambda_2"][0].partition_broadcast(P))
        with nc.allow_non_contiguous_dma(reason="a few words"):
            small(gate_b[:], a["ml_gate_b_2"][0].rearrange("w h -> h w"))
            log_dt = a["s5_log_dt_2"]
            for half in range(2):
                small(s5v[64 * half:64 * half + 64, 15, :],
                      bass.AP(log_dt.tensor, log_dt.offset + half, [[0, S5_STATE], [2, 16], [1, 1]]).rearrange("p a b -> p (a b)"))
        small(wa2, a["gla_wa2_2"][0])
        for o, name in ((s5b[0], "s5_b_re_2"), (s5b[1], "s5_b_im_2")):
            small(o[:], a[name][0].rearrange("(i h) s c -> (h s) i c", h=2))
        for o, name in ((s5c[0], "s5_c_re_2"), (s5c[1], "s5_c_im_2")):
            small(o[:], a[name][0].rearrange("(t g) c s -> (g c) t s", t=4))
        def fold(norms):
            for n, g in FOLDED:
                if n in norms:
                    pool.wait_ge(sem["sq_ready"], sq_count(n, g))
                    sq = T(NORM_SQ[n] + 4 * g, 4)
                    then(G.tensor_tensor(sq[:, 0:2], sq[:, 0:2], sq[:, 2:4], ALU.add))
                    G.tensor_tensor(sq[:, 0], sq[:, 0], sq[:, 1], ALU.add).then_inc(sem["sq_folded"], 1)

        for b in range(KT // 2):
            pool.wait_ge(sem["x_copied"], b + 1)
            m = G.tensor_tensor(T(NORM_SQ[0] + 2 * b, 2), x[:, 2 * b:2 * b + 2], x[:, 2 * b:2 * b + 2], ALU.mult)
            if b % 2 == 1:
                m.then_inc(sem["sq_ready"], 1)
        fold((0,))
        pool.wait_ge(sem["bias_copied"], 1)
        pool.dma_start(bias_scratch[:].rearrange("h p j -> p h j"),
                       span(32, 0, BR_HEADS * 384).rearrange("p (h j) -> p h j", h=BR_HEADS)).then_inc(sem["bias_out"], 16)
        pool.wait_ge(sem["bias_out"], 16)
        pool.dma_start(T(32, 8), a["pool_w"][0].rearrange("g (c p) f -> p (g c) f", p=P)).then_inc(sem["pool_w_in"], 16)

        pad = POOL_PAD
        bufs = [span(40, 2 * (pad + S) * i, 2 * (pad + S)).rearrange("p (a b) -> p a b", a=2) for i in range(2)]
        head = span(55, 0, 2 * pad).rearrange("p (a b) -> p a b", a=2)
        for b in bufs:
            then(G.memset(b, 0.0))
        for g in POOL_ORDER:
            w = POOL_WINDOWS[g]
            p = IN_ORDER.index(g // 2)
            pool.wait_ge(drained[p % 2], H_IN + p // 2 + 2)
            u = T(2 * g, 2)
            cur = 1
            G.tensor_copy(bufs[1][:, :, pad:pad + 1], u[:, :, 0:1])
            then(G.tensor_tensor(bufs[1][:, :, pad + 1:], u[:, :, 1:], u[:, :, 0:S - 1], ALU.add))
            lag = 2
            while lag < w:
                src, dst = bufs[cur], bufs[1 - cur]
                then(G.tensor_tensor(dst[:, :, pad:], src[:, :, pad:], src[:, :, pad - lag:pad + S - lag], ALU.add))
                cur, lag = 1 - cur, 2 * lag
            tail = bufs[cur]
            scale = C("poolfix", lo=g * pad, n=pad).unsqueeze(1).to_broadcast([P, 2, pad])
            then(G.tensor_tensor(head, tail[:, :, pad:2 * pad], scale, ALU.mult))
            then(G.tensor_tensor(head, head, u[:, :, 0:pad], ALU.subtract))
            then(G.tensor_scalar(tail[:, :, pad:], tail[:, :, pad:], 1.0 / w, None, ALU.mult))
            then(G.tensor_tensor(u, tail[:, :, pad:], u, ALU.subtract))
            then(G.tensor_copy(u[:, :, 0:pad], head))
            pool.sem_inc(sem["pooled"], 1)

        fold((3, 4, 5))

        pool.wait_ge(sem["hop_ready"], before(6, "hop"))
        tensor = bias_scratch
        at = [[383, P], [P * 384, BR_HEADS]]
        bias = span(28, 0, BR_HEADS * CW).rearrange("p (h j) -> p h j", h=BR_HEADS)
        pool.dma_start(bias[:, :, 0:P], bass.AP(tensor, P - 1 + P, at + [[1, P]])).then_inc(sem["bias_in"], 16)
        pool.dma_start(bias[:, :, P:CW], bass.AP(tensor, P - 1, at + [[1, S]])).then_inc(sem["bias_in"], 16)

        pool.wait_ge(sem["mod_ready"], G_IN2 + 1)
        for i in range(2):
            pool.wait_ge(drained[i], H_IN2 + 4)
            src, o, tap_of = T(12 + 4 * i, 4), T(44 + 4 * i, 4), T(59, 4)
            for f in range(4):
                m = G.tensor_scalar(o[:, f], src[:, f], vec("ml_conv_2", 3 * 8 + 4 * i + f), None, ALU.mult)
            then(m)
            for tap in (2, 1, 0):
                lag = 3 - tap
                for f in range(4):
                    m = G.tensor_scalar(tap_of[:, f], src[:, f], vec("ml_conv_2", tap * 8 + 4 * i + f), None, ALU.mult)
                then(m)
                then(G.tensor_tensor(o[:, :, lag:S], o[:, :, lag:S], tap_of[:, :, 0:S - lag], ALU.add))
        pool.sem_inc(sem["m_conv"], 1)

        pool.wait_ge(sem["x_normed"], 4)
        pool.dma_start(x_scratch[:], x[:]).then_inc(sem["x_parked"], 16)

        mask = C("s5b").rearrange("p (i g) -> p i g", i=4).unsqueeze(3).to_broadcast([P, 4, 8, S5_CH])
        pool.wait_ge(sem["s_pow"], 1)
        pool.wait_ge(sem["g_arg"], GLA_STEPS - 1)

        def table(t):
            cosT, sinT = rotation(t)
            G.memset(cosT[:, :, 0:1], 1.0)
            then(G.memset(sinT[:, :, 0:1], 0.0))
            for l in range(8):
                n = 1 << l
                c1, s1 = (s5pow[i][:, l, 4 * t:4 * t + 4].unsqueeze(2).to_broadcast([P, 4, n]) for i in range(2))
                c0, s0 = cosT[:, :, 0:n], sinT[:, :, 0:n]
                cn, sn = cosT[:, :, n:2 * n], sinT[:, :, n:2 * n]
                tmp = span(70, 0, 512).rearrange("p (i n) -> p i n", i=4)[:, :, 0:n]
                G.tensor_tensor(tmp, s0, s1, ALU.mult)
                then(G.tensor_tensor(cn, c0, c1, ALU.mult))
                then(G.tensor_tensor(cn, cn, tmp, ALU.subtract))
                G.tensor_tensor(tmp, c0, s1, ALU.mult)
                then(G.tensor_tensor(sn, s0, c1, ALU.mult))
                then(G.tensor_tensor(sn, sn, tmp, ALU.add))
            pool.sem_inc(sem["s_table"], 1)

        def spread_inputs(t):
            if t == 0:
                pool.wait_ge(sem["g_out"], 1)
            else:
                pool.wait_ge(sem["s_turned"], t)
            for part in range(2):
                m = G.tensor_tensor(span(52 + 2 * part, 0, 512).rearrange("p (i g c) -> p i g c", i=4, g=8),
                                    s5b[part][:, 4 * t:4 * t + 4].unsqueeze(2).to_broadcast([P, 4, 8, S5_CH]), mask, ALU.mult)
            m.then_inc(sem["s_pad"], 1)

        def spread_outputs(t):
            if t >= 1:
                pool.wait_ge(sem["s_cturned"], t)
            for part in range(2):
                m = G.tensor_tensor(span(66 + 2 * part, 0, 512).rearrange("p (h s) -> p h s", h=8),
                                    s5c[part][:, t:t + 1].to_broadcast([P, 8, S5_STATE]),
                                    C("s5c").unsqueeze(2).to_broadcast([P, 8, S5_STATE]), ALU.mult)
            m.then_inc(sem["s_cpad"], 1)

        for t in range(4):
            if t >= 2:
                pool.wait_ge(sem["s_x"], t - 1)
            table(t)
            spread_inputs(t)
            spread_outputs(t)
        pool.wait_ge(sem["s_x"], 3)
        pool.dma_start(flat(T(16, 8)).rearrange("p (k n) -> p k n", k=4),
                       a["s5_glu_w_2"][0].rearrange("(k p) n -> p k n", p=P)).then_inc(sem["glu_w_in"], 16)
        pool.wait_ge(sem["x_parked"], 16)
        pool.wait_ge(sem["merged_ready"], 4)
        pool.dma_start(x[:], x_scratch[:]).then_inc(sem["x_back"], 16)
        fold((6,))
        pool.wait_ge(sem["normed"], before(7, "normed"))
        G.memset(T(0, KT), 0.0).then_inc(sem["sum_clear"], 1)
        fold((8,))
    ctx.close()


INPUTS = """x norm_mix_g w_in pool_w pool_scale pool_out_norm_g attn_out_norm_g w_out norm_mlp_g w_up w_down norm_final_g
c_2 ada_w_2 ada_b_2 norm_g_2 w_in_2 rel_bias_2 diff_lambda_2 ml_conv_2 ml_gate_b_2 gla_wa2_2 gla_ba_2 s5_a_re_2 s5_a_im_2
s5_log_dt_2 s5_b_re_2 s5_b_im_2 s5_c_re_2 s5_c_im_2 s5_d_2 s5_glu_w_2 s5_glu_b_2 w_branch_2 w_gate_2 b_gate_2 w_out_2
ffn_w_in_2 ffn_w_out_2""".split()


def kernel(**inputs):
    import concourse.bacc as bacc
    from concourse.bass_utils import run_bass_kernel_spmd

    nc = bacc.Bacc("TRN2", target_bir_lowering=False, num_devices=1)
    arrays, aps = {}, {}
    for name in INPUTS:
        v = np.ascontiguousarray(inputs[name])
        arrays[f"in_{name}"] = v
        aps[name] = nc.dram_tensor(f"in_{name}", v.shape, mybir.dt.from_np(v.dtype), kind="ExternalInput").ap()
    arrays["in_constants"] = shape_constants()
    consts = nc.dram_tensor("in_constants", arrays["in_constants"].shape, F32, kind="ExternalInput").ap()
    out = nc.dram_tensor("out_0", (1, S, D), F32, kind="ExternalOutput").ap()
    two_blocks(nc, aps, consts, out)
    r = run_bass_kernel_spmd(nc, [arrays], core_ids=[0])
    return r.results[0]["out_0"]
```
